# Optimizing a Trainium2 kernel written in Bass

```python
import jax, jax.numpy as jnp
from jax import lax
import numpy as np

D_MODEL = 1024
BATCH = 1
SEQ = 1024
DEPTH = 1
DEC_BATCH = 1
DEC_SEQ = 32
PAST_LEN = 1024

CHUNK = 64
N_HEADS = 16
N_KV_HEADS = 4
HEAD_DIM = 64
GROUP = N_HEADS // N_KV_HEADS
WINDOW = 128
N_BACK_CHUNKS = WINDOW // CHUNK
D_ATTN = N_HEADS * HEAD_DIM
D_KV = N_KV_HEADS * HEAD_DIM
D_LRU = D_MODEL
N_LRU_BLOCKS = 16
LRU_BLOCK = D_LRU // N_LRU_BLOCKS
LRU_C = 8.0
LRU_CONV_W = 4
D_FF = 3 * D_MODEL
FFN_CONV_W = 3
N_BRANCH = 2
D_IN = 2 * D_LRU + D_ATTN + 2 * D_KV + N_BRANCH * D_MODEL
IN_SPLITS = [D_LRU, 2 * D_LRU, 2 * D_LRU + D_ATTN, 2 * D_LRU + D_ATTN + D_KV, 2 * D_LRU + D_ATTN + 2 * D_KV]
EPS = 1e-6
NEG = -1e30

kernel_name = "hawk_swa_sink_convffn_stream"

def rmsnorm(x, g):
    xf = x.astype(jnp.float32)
    y = xf * lax.rsqrt(jnp.mean(xf * xf, axis=-1, keepdims=True) + EPS)
    return (y * g.astype(jnp.float32)).astype(x.dtype)

def causal_dwconv(x, prev, w, b):
    width = w.shape[0]
    T = x.shape[1]
    xe = jnp.concatenate([prev.astype(x.dtype), x], axis=1)
    y = b
    for j in range(width):
        y = y + w[j] * xe[:, j:j + T]
    return y, xe[:, xe.shape[1] - (width - 1):]

def block_diag(x, w, b):
    B, T, _ = x.shape
    xr = x.reshape(B, T, N_LRU_BLOCKS, LRU_BLOCK)
    return jnp.einsum('btnc,ncd->btnd', xr, w).reshape(B, T, D_LRU) + b

def rg_lru(x, h_prev, w_a, b_a, w_i, b_i, lam):
    r = jax.nn.sigmoid(block_diag(x, w_a, b_a).astype(jnp.float32))
    i = jax.nn.sigmoid(block_diag(x, w_i, b_i).astype(jnp.float32))
    log_a = -LRU_C * r * jax.nn.softplus(-lam.astype(jnp.float32))
    a = jnp.exp(log_a)
    mult = jnp.sqrt(-jnp.expm1(2.0 * log_a))
    bterm = mult * i * x.astype(jnp.float32)

    def combine(lhs, rhs):
        a1, b1 = lhs
        a2, b2 = rhs
        return a1 * a2, a2 * b1 + b2

    A, Bc = lax.associative_scan(combine, (a, bterm), axis=1)
    h = A * h_prev.astype(jnp.float32)[:, None] + Bc
    return h.astype(x.dtype), h[:, -1].astype(h_prev.dtype)

def sink_softmax(s, sink):
    col = jnp.broadcast_to(sink, s.shape[:-1] + (1,))
    return jax.nn.softmax(jnp.concatenate([s, col], axis=-1), axis=-1)[..., :-1]

def attn_prompt(q, k, v, sink):
    B, S = q.shape[:2]
    nc = S // CHUNK
    nkb = N_BACK_CHUNKS + 1
    qc = q.reshape(B, nc, CHUNK, N_KV_HEADS, GROUP, HEAD_DIM)
    pad = ((0, 0), (N_BACK_CHUNKS * CHUNK, 0), (0, 0), (0, 0))
    kp = jnp.pad(k, pad).reshape(B, nc + N_BACK_CHUNKS, CHUNK, N_KV_HEADS, HEAD_DIM)
    vp = jnp.pad(v, pad).reshape(B, nc + N_BACK_CHUNKS, CHUNK, N_KV_HEADS, HEAD_DIM)
    kb = jnp.concatenate([kp[:, j:j + nc] for j in range(nkb)], axis=2)
    vb = jnp.concatenate([vp[:, j:j + nc] for j in range(nkb)], axis=2)
    key_chunk = jnp.arange(nc)[:, None] - N_BACK_CHUNKS + jnp.arange(nkb * CHUNK)[None, :] // CHUNK
    valid = key_chunk >= 0
    s = jnp.einsum('bnqkgd,bnskd->bnkgqs', qc.astype(jnp.float32), kb.astype(jnp.float32)) * (HEAD_DIM ** -0.5)
    s = jnp.where(valid[None, :, None, None, None, :], s, NEG)
    p = sink_softmax(s, sink.reshape(N_KV_HEADS, GROUP)[:, :, None, None].astype(jnp.float32))
    o = jnp.einsum('bnkgqs,bnskd->bnqkgd', p.astype(vb.dtype), vb)
    return o.reshape(B, S, D_ATTN)

def attn_sample(q, k, v, sink, k_cache, v_cache):
    B, T = q.shape[:2]
    kk = jnp.concatenate([k_cache.astype(k.dtype), k], axis=1)
    vv = jnp.concatenate([v_cache.astype(v.dtype), v], axis=1)
    qg = q.reshape(B, T, N_KV_HEADS, GROUP, HEAD_DIM)
    s = jnp.einsum('btkgd,bskd->bkgts', qg.astype(jnp.float32), kk.astype(jnp.float32)) * (HEAD_DIM ** -0.5)
    p = sink_softmax(s, sink.reshape(N_KV_HEADS, GROUP)[:, :, None, None].astype(jnp.float32))
    o = jnp.einsum('bkgts,bskd->btkgd', p.astype(vv.dtype), vv)
    return o.reshape(B, T, D_ATTN)

def layer(x, lp, lru_conv_prev, lru_h_prev, ffn_conv_prev, attn_fn):
    (g_mix, w_in, b_gate, w_lconv, b_lconv, w_a, b_a, w_i, b_i, lam, g_q, g_k, sink,
     w_br_lru, w_br_attn, w_out, g_ffn, w_up, w_fconv, b_fconv, w_down) = lp
    B, T, _ = x.shape
    xn = rmsnorm(x, g_mix)
    u_lru, y_lru, q, k, v, gates = jnp.split(xn @ w_in, IN_SPLITS, axis=-1)
    xc, lru_conv_new = causal_dwconv(u_lru, lru_conv_prev, w_lconv, b_lconv)
    h, lru_h_new = rg_lru(xc, lru_h_prev, w_a, b_a, w_i, b_i, lam)
    br_lru = (h * jax.nn.gelu(y_lru)) @ w_br_lru
    q = rmsnorm(q.reshape(B, T, N_HEADS, HEAD_DIM), g_q)
    k = rmsnorm(k.reshape(B, T, N_KV_HEADS, HEAD_DIM), g_k)
    v = v.reshape(B, T, N_KV_HEADS, HEAD_DIM)
    br_attn = attn_fn(q, k, v, sink) @ w_br_attn
    g = jax.nn.sigmoid((gates + b_gate).astype(jnp.float32)).astype(x.dtype).reshape(B, T, N_BRANCH, D_MODEL)
    x = x + (g[:, :, 0] * br_lru + g[:, :, 1] * br_attn) @ w_out
    gate_pre, up = jnp.split(rmsnorm(x, g_ffn) @ w_up, [D_FF], axis=-1)
    gc, ffn_conv_new = causal_dwconv(gate_pre, ffn_conv_prev, w_fconv, b_fconv)
    x = x + (jax.nn.gelu(gc) * up) @ w_down
    return x, k, v, lru_conv_new, lru_h_new, ffn_conv_new

def setup_inputs(seed: int = 0) -> dict:
    key = jax.random.key(seed)
    ks = jax.random.split(key, 32)
    nrm = lambda k, shape, scale: jax.random.normal(k, shape, jnp.float32) * scale
    a8 = jax.random.uniform(ks[13], (DEPTH, D_LRU), jnp.float32, 0.9, 0.999)
    base = a8 ** (1.0 / LRU_C)
    return {
        'x_prompt': nrm(ks[0], (BATCH, SEQ, D_MODEL), 1.0),
        'x_sample': nrm(ks[1], (DEC_BATCH, DEC_SEQ, D_MODEL), 1.0),
        'state_lru_conv': nrm(ks[2], (DEPTH, DEC_BATCH, LRU_CONV_W - 1, D_LRU), 1.0),
        'state_lru_h': nrm(ks[3], (DEPTH, DEC_BATCH, D_LRU), 0.5),
        'cache_k': nrm(ks[4], (DEPTH, DEC_BATCH, min(WINDOW, PAST_LEN), N_KV_HEADS, HEAD_DIM), 1.0),
        'cache_v': nrm(ks[5], (DEPTH, DEC_BATCH, min(WINDOW, PAST_LEN), N_KV_HEADS, HEAD_DIM), 1.0),
        'state_ffn_conv': nrm(ks[6], (DEPTH, DEC_BATCH, FFN_CONV_W - 1, D_FF), 1.0),
        'g_mix': 1.0 + nrm(ks[7], (DEPTH, D_MODEL), 0.02),
        'w_in': nrm(ks[8], (DEPTH, D_MODEL, D_IN), D_MODEL ** -0.5),
        'b_gate': nrm(ks[9], (DEPTH, N_BRANCH * D_MODEL), 0.02),
        'w_lru_conv': nrm(ks[10], (DEPTH, LRU_CONV_W, D_LRU), LRU_CONV_W ** -0.5),
        'b_lru_conv': nrm(ks[11], (DEPTH, D_LRU), 0.02),
        'w_lru_a': nrm(ks[12], (DEPTH, N_LRU_BLOCKS, LRU_BLOCK, LRU_BLOCK), LRU_BLOCK ** -0.5),
        'b_lru_a': nrm(ks[14], (DEPTH, D_LRU), 0.02),
        'w_lru_i': nrm(ks[15], (DEPTH, N_LRU_BLOCKS, LRU_BLOCK, LRU_BLOCK), LRU_BLOCK ** -0.5),
        'b_lru_i': nrm(ks[16], (DEPTH, D_LRU), 0.02),
        'lru_lambda': jnp.log(base) - jnp.log1p(-base),
        'g_q': 1.0 + nrm(ks[17], (DEPTH, HEAD_DIM), 0.02),
        'g_k': 1.0 + nrm(ks[18], (DEPTH, HEAD_DIM), 0.02),
        'attn_sink': nrm(ks[19], (DEPTH, N_HEADS), 0.5),
        'w_br_lru': nrm(ks[20], (DEPTH, D_LRU, D_MODEL), D_LRU ** -0.5),
        'w_br_attn': nrm(ks[21], (DEPTH, D_ATTN, D_MODEL), D_ATTN ** -0.5),
        'w_out': nrm(ks[22], (DEPTH, D_MODEL, D_MODEL), D_MODEL ** -0.5),
        'g_ffn': 1.0 + nrm(ks[23], (DEPTH, D_MODEL), 0.02),
        'w_up': nrm(ks[24], (DEPTH, D_MODEL, 2 * D_FF), D_MODEL ** -0.5),
        'w_ffn_conv': nrm(ks[25], (DEPTH, FFN_CONV_W, D_FF), FFN_CONV_W ** -0.5),
        'b_ffn_conv': nrm(ks[26], (DEPTH, D_FF), 0.02),
        'w_down': nrm(ks[27], (DEPTH, D_FF, D_MODEL), D_FF ** -0.5),
    }

def reference(x_prompt, x_sample, state_lru_conv, state_lru_h, cache_k, cache_v, state_ffn_conv,
              g_mix, w_in, b_gate, w_lru_conv, b_lru_conv, w_lru_a, b_lru_a, w_lru_i, b_lru_i,
              lru_lambda, g_q, g_k, attn_sink, w_br_lru, w_br_attn, w_out, g_ffn, w_up,
              w_ffn_conv, b_ffn_conv, w_down):
    params = (g_mix, w_in, b_gate, w_lru_conv, b_lru_conv, w_lru_a, b_lru_a, w_lru_i, b_lru_i,
              lru_lambda, g_q, g_k, attn_sink, w_br_lru, w_br_attn, w_out, g_ffn, w_up,
              w_ffn_conv, b_ffn_conv, w_down)
    xp, xs = x_prompt, x_sample
    B = xp.shape[0]
    p_lc, p_lh, p_k, p_v, p_fc = [], [], [], [], []
    s_lc, s_lh, s_k, s_v, s_fc = [], [], [], [], []
    for l in range(DEPTH):
        lp = tuple(p[l] for p in params)
        xp, kp, vp, lc, lh, fc = layer(
            xp, lp,
            jnp.zeros((B, LRU_CONV_W - 1, D_LRU), xp.dtype),
            jnp.zeros((B, D_LRU), xp.dtype),
            jnp.zeros((B, FFN_CONV_W - 1, D_FF), xp.dtype),
            attn_prompt)
        p_lc.append(lc); p_lh.append(lh); p_fc.append(fc)
        p_k.append(kp[:, kp.shape[1] - WINDOW:]); p_v.append(vp[:, vp.shape[1] - WINDOW:])
        ck, cv = cache_k[l], cache_v[l]
        xs, ks_, vs_, lc, lh, fc = layer(
            xs, lp, state_lru_conv[l], state_lru_h[l], state_ffn_conv[l],
            lambda q, k, v, s: attn_sample(q, k, v, s, ck, cv))
        s_lc.append(lc); s_lh.append(lh); s_fc.append(fc); s_k.append(ks_); s_v.append(vs_)
    return (xp, xs,
            jnp.stack(p_lc), jnp.stack(p_lh), jnp.stack(p_k), jnp.stack(p_v), jnp.stack(p_fc),
            jnp.stack(s_lc), jnp.stack(s_lh), jnp.stack(s_k), jnp.stack(s_v), jnp.stack(s_fc))


_drawn_inputs = setup_inputs


def setup_inputs(seed=0):
    import zlib

    import numpy as np

    out = dict(_drawn_inputs(seed))
    spreads = {}
    factors = {'g_mix': 2.758,
     'b_gate': 8.0,
     'b_lru_a': 8.0,
     'b_lru_i': 8.0,
     'g_q': 8.0,
     'g_k': 2.823,
     'attn_sink': 8.0,
     'g_ffn': 2.81,
     'b_ffn_conv': 5.536}
    for name, (base, spread) in spreads.items():
        noise = np.random.default_rng([zlib.crc32(name.encode()), seed]).standard_normal(out[name].shape)
        drawn = base * np.exp(spread * noise) if base else spread * noise
        out[name] = __import__('jax').numpy.asarray(drawn.astype(out[name].dtype))
    for name, factor in factors.items():
        out[name] = (out[name] * factor).astype(out[name].dtype)
    return out
```

```python
from contextlib import ExitStack

import concourse.bass as bass
import numpy as np
from concourse import mybir

F32 = mybir.dt.float32
F32R = mybir.dt.float32r
ACT = mybir.ActivationFunctionType
ALU = mybir.AluOpType
AXX = mybir.AxisListType.X

P = 128
DM, SEQ, DSEQ, PAD = 1024, 1024, 32, 4
NH, NKV, HD, CHUNK, WIN = 16, 4, 64, 64, 128
DFF = 3 * DM
KT = DM // P
FT = DFF // P
SMP = SEQ + PAD
T = SMP + DSEQ
CHUNKS = [(0, 354), (354, 354), (708, 352)]
NC = SEQ // CHUNK
EPS = 1e-6
LRU_HIST, FFN_HIST = 3, 2

ATT_PAIRS = 3
PAIR_G1 = 2 * ATT_PAIRS
PAIR_R = PAIR_G1 + KT
PAIR_G0 = PAIR_R + KT
PAIR_O = PAIR_G0 + KT
PAIR_F = PAIR_O + KT // 2
FFN_PARTS = FT // KT
PAIRS_PER_PART = KT + KT // 2
NPAIR = PAIR_F + FFN_PARTS * PAIRS_PER_PART
NSLOT = 2 * NPAIR

X_ACT = dict(G1=6 * ATT_PAIRS)
X_ACT["R"] = X_ACT["G1"] + 3 * KT
X_ACT["G0"] = X_ACT["R"] + 3 * KT
X_ACT["F"] = X_ACT["G0"] + 3 * KT
Y_ACT = dict(R=6 * ATT_PAIRS)
Y_ACT["O"] = Y_ACT["R"] + 3 * KT
X_DVE = dict(O=3, F=3 + 3 * KT // 2)
Y_DVE = dict(G1=3, G0=3 + 3 * KT, O=3 + 6 * KT, F=3 + 6 * KT + 3 * KT // 2)
UP, DOWN = 3 * KT, 3 * KT // 2
X_END = X_DVE["F"] + FFN_PARTS * DOWN
Y_END = Y_DVE["F"] + FFN_PARTS * (UP + DOWN)

VEC = {}
_at = 0
for _name, _n in (("bg_lru", KT), ("bg_att", KT), ("conv_w", 4 * KT), ("conv_b", KT), ("b_a", KT), ("b_i", KT), ("lam", KT),
                  ("g_mix", KT), ("g_ffn", KT), ("fconv_w", 3 * FT), ("fconv_b", FT), ("h0", KT), ("g_q", 1), ("g_k", 1),
                  ("sink_p", 8), ("sink_s", 4), ("conv0", LRU_HIST * KT), ("fconv0", FFN_HIST * FT)):
    VEC[_name] = (_at, _n)
    _at += _n
NVEC = _at


class Count:

    def __init__(self, sem):
        self.sem, self.n, self.turns = sem, 0, []

    def inc(self, ins):
        ins.then_inc(self.sem, 1)
        self.n += 1

    def value(self):
        v = self.n
        for i, k, _ in self.turns:
            v = i * k + v
        return v

    def enter(self, i, per_turn):
        self.turns.append((i, per_turn, self.n))

    def leave(self, trips):
        _, k, start = self.turns.pop()
        assert self.n - start == k, (self.n - start, k)
        self.n = start + k * trips


def build(nc, xT, W, wab, vecs, mats, kc, vc, yT, o_lconv, o_h, o_fconv, o_kp, o_ks, o_vp, o_vs):
    ctx = ExitStack()
    with ctx:
        def sem(name):
            return ctx.enter_context(nc.semaphore(name))

        base = [(nc.sbuf_base + 63) // 64 * 64]
        end = nc.sbuf_usable_end

        def place(name, shape, dt, at=None):
            size = 4 * int(np.prod(shape[1:]))
            if at is None:
                at = base[0]
                base[0] += (size + 31) // 32 * 32
                assert base[0] <= end, (name, base[0], end)
            return nc.alloc_sbuf_tensor_at(name, shape, dt, offset=at), at

        def sb(name, shape, dt=F32, at=None):
            return place(name, shape, dt, at)[0]

        FULL = [P, KT, T]
        x_hi, _ = place("x_hi", FULL, F32R)
        x_lo, _ = place("x_lo", FULL, F32R)
        c_hi, at_c = place("c_hi", FULL, F32R)
        d_lo, at_d = place("d_lo", FULL, F32R)
        act_lo, at_e = place("act_lo", FULL, F32R)
        resid = sb("resid", FULL, F32, at_c)
        sqsum = sb("sqsum", FULL, F32, at_d)
        merged = sb("merged", FULL, F32, at_e)
        act_hi = sb("act_hi", FULL, F32R, at_d)
        q2 = sb("q2", [P, NC + 1, 4 * CHUNK], F32, at_c + 4 * T * 4)
        qT = sb("qT", [P, 4, T], F32, at_e)
        kN = sb("kN", [P, T], F32, at_e + 4 * T * 4)
        row_bytes = (4 * T + 31) // 32 * 32
        kG = sb("kG", [P, T], F32, at_e + 4 * T * 4 + row_bytes)
        vT = sb("vT", [P, T], F32, at_e + 4 * T * 4 + 2 * row_bytes)
        kcs = sb("kcs", [P, 2, WIN], F32, at_e + 4 * T * 4 + 3 * row_bytes)
        vcs = sb("vcs", [P, 2, WIN], F32, at_e + 4 * T * 4 + 3 * row_bytes + 2 * WIN * 4)
        w_raw, w_hi, w_lo = [], [], []
        for s in range(2):
            r, at = place(f"w_raw{s}", [P, DM], F32)
            w_raw.append(r)
            w_lo.append(sb(f"w_lo{s}", [P, DM], F32R, at))
            w_hi.append(sb(f"w_hi{s}", [P, DM], F32R))
        vec = sb("vec", [P, NVEC])
        mat = sb("mat", [P, 3, P])
        ident, ones, bones = mat[:, 0, :], mat[:, 1, :], mat[:, 2, :]
        halfb = sb("halfb", [P, 4 * KT])
        lamc = sb("lamc", [P, 2, KT])
        lam_t = sb("lam_t", [P, 5, KT])
        st_lconv = sb("st_lconv", [P, KT, 2, LRU_HIST])
        st_h = sb("st_h", [P, KT, 2])
        st_fconv = sb("st_fconv", [P, FT, 2, FFN_HIST])
        negsink = sb("negsink", [P, 12])
        rq = sb("rq", [P, 4 * NC + 2])
        nrq = sb("nrq", [P, 4 * NC + 2])
        epsc = sb("epsc", [P, 2])
        tr = base[0]
        U = sb("U", [P, LRU_HIST + T], F32)
        FA = sb("FA", [P, T])
        FI = sb("FI", [P, T])
        FS = sb("FS", [P, T])
        XC = [sb(f"XC{i}", [P, 354]) for i in range(3)]
        wabs = sb("wabs", [P, 2, P])
        at = [tr]

        def ta(name, shape):
            size = 4 * int(np.prod(shape[1:]))
            t = sb(name, shape, F32, at[0])
            at[0] += (size + 31) // 32 * 32
            assert at[0] <= end
            return t
        qs = [ta(f"qs{i}", [P, 4, CHUNK]) for i in range(2)]
        ks = [ta(f"ks{i}", [P, 3 * CHUNK]) for i in range(2)]
        vs = [ta(f"vs{i}", [P, 3 * CHUNK]) for i in range(2)]
        pr = [ta(f"pr{i}", [P, 4, 3 * CHUNK]) for i in range(2)]
        pt = [ta(f"pt{i}", [P, 4 * P]) for i in range(2)]
        vt = [ta(f"vt{i}", [P, P]) for i in range(2)]
        small = [ta(f"small{i}", [P, 8, 4]) for i in range(2)]
        at = [tr]
        GB = ta("GB", [P, FFN_HIST + T])
        GC = [ta(f"GC{i}", [P, 354]) for i in range(3)]
        GV = [ta(f"GV{i}", [P, 354]) for i in range(3)]
        at = [tr]
        nacc = ta("nacc", [P, T])
        nrs = ta("nrs", [P, T])
        ntmp = [ta(f"ntmp{i}", [P, 354]) for i in range(4)]

        bankpair = [ctx.enter_context(nc.psum_tensor(f"banks{b}", [P, 2, 512], F32)) for b in range(4)]
        bank = [bankpair[b // 2][:, b % 2, :] for b in range(8)]
        XB, YB = bank[0:3], bank[3:6]

        def V(name, i=0, n=1):
            a, _ = VEC[name]
            return vec[:, a + i:a + i + n]

        def VD(name, i, n=1):
            a, _ = VEC[name]
            return vec[:, bass.ds(i + a, n)]

        def row(t, k, c0, cn):
            if isinstance(k, int):
                return t[:, k, c0:c0 + cn]
            return t[:, bass.ds(k, 1), c0:c0 + cn].rearrange("p a n -> p (a n)")

        def cols(c0, n):
            return slice(c0, c0 + n) if isinstance(c0, int) else bass.ds(c0, n)

        s_vec = sem("tables_loaded")
        s_x = [sem(f"x_loaded{k}") for k in range(KT)]
        s_cache = sem("cache_loaded")
        s_xres = [sem(f"residual_x_loaded{k}") for k in range(2)]
        s_wab = sem("lru_gate_weights_loaded")
        wx_loaded, wy_loaded = sem("wx_loaded"), sem("wy_loaded")
        wx_ready, wy_ready = sem("wx_ready"), sem("wy_ready")
        w_hi_done = sem("w_hi_done")
        x_done, y_done = sem("x_done"), sem("y_done")
        x_act, y_act = sem("x_freed_by_act"), sem("y_freed_by_act")
        x_dve, y_dve = sem("x_freed_by_dve"), sem("y_freed_by_dve")
        act_c, dve_c = sem("act_chain"), sem("dve_chain")
        s_eps, s_exp_lam, s_lamc = sem("eps_set"), sem("exp_lambda"), sem("lambda_ready")
        n_sq, n_acc, n_ps, n_rt, n_f32, n_hi, n_lo = (
            sem(f"norm_{x}") for x in ("squares", "summed", "psum", "root", "f32", "hi", "lo"))
        k_ps, k_rt, k_rdy = (sem(f"knorm_{x}") for x in ("psum", "root", "ready"))
        q_sq, q_ps, q_rt = sem("q_squares"), sem("q_sums"), sem("q_root")
        a_stg, a_S, a_stat, a_exp, a_nrm, a_T, a_ev, a_evv, a_O, a_hi, a_lo = (
            sem(f"att_{x}") for x in ("staged", "scores", "stats", "exp", "normalised", "transposed", "p_copied",
                                      "v_copied", "out", "hi", "lo"))
        r_u, r_fix, r_x0, r_xc, r_ps, r_tanh, r_sqa, r_om, r_root, r_h, r_gelu, r_z, r_hi, r_lo = (
            sem(f"lru_{x}") for x in ("u", "history", "x0", "xc", "psum", "tanh", "a_squared", "one_minus_a2", "root", "h",
                                      "gelu", "z", "hi", "lo"))
        m_mrg, m_hi, m_lo = sem("merged"), sem("merged_hi"), sem("merged_lo")
        f_fix, f_c0, f_conv, f_gelu, f_hi, f_lo = (
            sem(f"ffn_{x}") for x in ("history", "c0", "conv", "gelu", "hi", "lo"))
        s_out = sem("outputs_stored")
        s_own = [sem(f"own_{x}") for x in ("pool", "pe", "act")]

        block = ctx.enter_context(nc.Block())
        NB = NC + 1
        STG = 3 * NC + 5
        GEN = NC - 4

        @block.sync
        def _(sp):
            for k in range(KT):
                sp.dma_start(resid[:, k, :], xT[k]).then_inc(s_x[k], 16)
                if k == 0:
                    sp.dma_start(vec[:, :], vecs).then_inc(s_vec, 16)
                    sp.dma_start(mat[:, :, :], mats).then_inc(s_vec, 16)
            sp.dma_start(w_raw[0][:, :], W[0]).then_inc(wx_loaded, 16)
            sp.dma_start(w_raw[1][:, :], W[1]).then_inc(wy_loaded, 16)
            sp.wait_ge(n_acc, KT)
            sp.dma_start(kcs[:, :, :], kc).then_inc(s_cache, 16)
            sp.dma_start(vcs[:, :, :], vc).then_inc(s_cache, 16)
            with sp.Fori(0, NPAIR - 1) as i:
                for s, (done, loaded) in enumerate(((x_done, wx_loaded), (y_done, wy_loaded))):
                    sp.wait_ge(done, i * 3 + 3)
                    sp.dma_start(w_raw[s][:, :], W[bass.ds(i * 2 + (2 + s), 1)].rearrange("a p n -> (a p) n")).then_inc(loaded, 16)
            sp.wait_ge(r_lo, 3 * KT)
            sp.dma_start(o_lconv, st_lconv[:, :, :, :]).then_inc(s_out, 16)
            sp.dma_start(o_h, st_h[:, :, :]).then_inc(s_out, 16)
            sp.wait_ge(f_lo, 3 * FT)
            sp.dma_start(o_fconv, st_fconv[:, :, :, :]).then_inc(s_out, 16)
            for k in range(KT):
                sp.wait_ge(x_dve if k % 2 == 0 else y_dve, (X_END if k % 2 == 0 else Y_END) - 3 * (KT // 2 - 1 - k // 2))
                sp.dma_start(yT[k], resid[:, k, :]).then_inc(s_out, 16)
            sp.wait_ge(s_out, 16 * (8 + 3 + KT))

        @block.gpsimd
        def _(pool):
            def split(p):
                for s, (loaded, ready) in enumerate(((wx_loaded, wx_ready), (wy_loaded, wy_ready))):
                    pool.wait_ge(loaded, p * 16 + 16)
                    if not isinstance(p, int):
                        pool.sem_inc(s_own[0], 1)
                    nc.gpsimd.tensor_scalar(w_hi[s][:, :], w_raw[s][:, :], 1.0, 0.0, ALU.mult, ALU.add).then_inc(w_hi_done, 1)
                    pool.wait_ge(w_hi_done, p * 2 + (s + 1))
                    nc.gpsimd.tensor_tensor(w_lo[s][:, :], w_raw[s][:, :], w_hi[s][:, :].bitcast(F32), ALU.subtract).then_inc(ready, 1)

            def stage(s, q0, k0, keys):
                nc.gpsimd.tensor_copy(qs[s][:, :, :], qT[:, :, cols(q0, CHUNK)]).then_inc(a_stg, 1)
                nc.gpsimd.tensor_copy(ks[s][:, 0:keys], kG[:, cols(k0, keys)]).then_inc(a_stg, 1)
                nc.gpsimd.tensor_copy(vs[s][:, 0:keys], vT[:, cols(k0, keys)]).then_inc(a_stg, 1)

            for a in range(2):
                B0, p0 = NB * a, ATT_PAIRS * a
                for p in range(p0 + a, p0 + ATT_PAIRS + 1):
                    split(p)
                pool.wait_ge(k_rdy, a + 1)
                pool.wait_ge(x_act, 3 * (p0 + ATT_PAIRS))
                pool.wait_ge(y_act, 3 * (p0 + ATT_PAIRS))
                if a:
                    pool.wait_ge(a_O, B0)
                stage(0, 0, 0, CHUNK)
                stage(1, CHUNK, 0, 2 * CHUNK)
                with pool.Fori(0, (NC - 2) // 2) as i:
                    for s in range(2):
                        pool.wait_ge(a_O, i * 2 + (B0 + 1 + s))
                        stage(s, i * (2 * CHUNK) + (2 + s) * CHUNK, i * (2 * CHUNK) + s * CHUNK, 3 * CHUNK)
                pool.wait_ge(a_O, B0 + NC - 1)
                pool.wait_ge(s_cache, 32)
                nc.gpsimd.tensor_copy(qs[0][:, 0:2, :].rearrange("p a b -> p (a b)").rearrange("p (a b) -> p a b", b=DSEQ),
                                      qT[:, :, SMP:T]).then_inc(a_stg, 1)
                nc.gpsimd.tensor_scalar(ks[0][:, 0:WIN], kcs[:, a, :], V("g_q"), 0.0, ALU.mult, ALU.add).then_inc(a_stg, 1)
                nc.gpsimd.tensor_copy(ks[0][:, WIN:WIN + DSEQ], kG[:, SMP:T]).then_inc(a_stg, 1)
                nc.gpsimd.tensor_copy(vs[0][:, 0:WIN], vcs[:, a, :]).then_inc(a_stg, 1)
                nc.gpsimd.tensor_copy(vs[0][:, WIN:WIN + DSEQ], vT[:, SMP:T]).then_inc(a_stg, 1)
            with pool.Fori(0, NPAIR - 2 * ATT_PAIRS - 1) as i:
                split(i + (2 * ATT_PAIRS + 1))

        @block.tensor
        def _(pe):
            def tile(s, i, p0, hi, lo, free=None, freed=None):
                banks, ready, done = (XB, wx_ready, x_done) if s == 0 else (YB, wy_ready, y_done)
                pe.wait_ge(ready, i + (p0 + 1))
                for n, (c0, cn) in enumerate(CHUNKS):
                    if free is not None:
                        pe.wait_ge(free, freed + (n - 2))
                    for k in range(KT):
                        for j, (w, x) in enumerate(((w_hi, hi), (w_hi, lo), (w_lo, hi))):
                            last = nc.tensor.matmul(banks[n][:, 0:cn], w[s][:, k * P:(k + 1) * P], x[:, k, c0:c0 + cn],
                                                    start=(k == 0 and j == 0), stop=(k == KT - 1 and j == 2))
                    last.then_inc(done, 1)

            def loop_tiles(p0, trips, hix, lox, hiy, loy, fx, x0, fy, y0):
                with pe.Fori(0, trips) as i:
                    tile(0, i, p0, hix, lox, fx, i * 3 + x0)
                    tile(1, i, p0, hiy, loy, fy, i * 3 + y0)

            def norm_sums(which):
                pe.wait_ge(n_acc, KT * (which + 1))
                for n, (c0, cn) in enumerate(CHUNKS):
                    if n == 2:
                        pe.wait_ge(n_rt, 3 * which + 1)
                    nc.tensor.matmul(bank[6 + n % 2][:, 0:cn], ones, nacc[:, c0:c0 + cn], start=True, stop=True).then_inc(n_ps, 1)

            pe.wait_ge(s_vec, 32)
            norm_sums(0)
            pe.wait_ge(n_lo, 3 * KT)
            pe.wait_ge(n_rt, 3)

            for a in range(2):
                p0, B0, G0 = ATT_PAIRS * a, NB * a, STG * a
                if a:
                    pe.wait_ge(a_lo, B0)
                tile(0, 0, p0, x_hi, x_lo)
                tile(1, 0, p0, x_hi, x_lo)
                pe.wait_ge(x_act, 3 * (p0 + 1))
                for n, (c0, cn) in enumerate(CHUNKS):
                    if n == 2:
                        pe.wait_ge(k_rt, 3 * a + 1)
                    nc.tensor.matmul(bank[6 + n % 2][:, 0:cn], bones, kG[:, c0:c0 + cn], start=True, stop=True).then_inc(k_ps, 1)
                loop_tiles(p0 + 1, ATT_PAIRS - 1, x_hi, x_lo, x_hi, x_lo, x_act, 3 * p0 + 3, y_act, 3 * p0 + 3)
                pe.wait_ge(q_sq, 4 * (a + 1))
                pe.wait_ge(k_rt, 3 * (a + 1))
                for c in range(NC):
                    for u in range(2):
                        nc.tensor.matmul(bank[7][:, 4 * c + u:4 * c + u + 3:2], q2[:, c, 2 * u * CHUNK:2 * (u + 1) * CHUNK],
                                         bones[:, HD - 1:HD + 1], start=True, stop=True)
                nc.tensor.matmul(bank[7][:, 4 * NC:4 * NC + 2], q2[:, NC, 0:4 * DSEQ], bones[:, HD - 1:HD + 1],
                                 start=True, stop=True).then_inc(q_ps, 1)
                pe.wait_ge(q_rt, a + 1)

                def scores(b, s, keys, units, staged, first=False):
                    pe.wait_ge(a_stg, staged)
                    if not first:
                        pe.wait_ge(a_exp, b)
                    for e in range(2):
                        for u in range(units):
                            v = units * e + u
                            last = nc.tensor.matmul(bank[2 * s + v // 2][:, (v % 2) * 192:(v % 2) * 192 + keys],
                                                    qs[s][64 * e:64 * e + 64, 2 * u:2 * u + 2, :], ks[s][64 * e:64 * e + 64, 0:keys],
                                                    start=True, stop=True)
                    last.then_inc(a_S, 1)

                def rest(b, s, keys, units):
                    groups = [(0, min(keys, P))] + ([(P, keys - P)] if keys > P else [])
                    pe.wait_ge(a_evv, b)
                    pe.wait_ge(a_ev, b)
                    for g, (k0, kn) in enumerate(groups):
                        nc.tensor.transpose(bank[6][0:kn, g * P:g * P + P], vs[s][:, k0:k0 + kn], ident)
                    pe.wait_ge(a_nrm, b + 1)
                    for g, (k0, kn) in enumerate(groups):
                        for v in range(2 * units):
                            last = nc.tensor.transpose(bank[4 + g][0:kn, v * P:v * P + P], pr[s][:, v, k0:k0 + kn], ident)
                    last.then_inc(a_T, 1)
                    pe.wait_ge(a_ev, b + 1)
                    pe.wait_ge(a_evv, b + 1)
                    pe.wait_ge(a_lo, b)
                    for e in range(2):
                        for u in range(units):
                            v = units * e + u
                            for g, (k0, kn) in enumerate(groups):
                                last = nc.tensor.matmul(bank[7][64 * e:64 * e + 64, u * P:u * P + P], vt[g][0:kn, 64 * e:64 * e + 64],
                                                        pt[g][0:kn, v * P:v * P + P], start=(g == 0), stop=(g == len(groups) - 1))
                    last.then_inc(a_O, 1)

                scores(0, 0, CHUNK, 2, G0 + 3, True)
                scores(0, 1, 2 * CHUNK, 2, G0 + 6, True)
                rest(B0, 0, CHUNK, 2)
                scores(B0 + 1, 0, 3 * CHUNK, 2, G0 + 9)
                rest(B0 + 1, 1, 2 * CHUNK, 2)
                scores(B0 + 2, 1, 3 * CHUNK, 2, G0 + 12)
                with pe.Fori(0, GEN // 2) as i:
                    for s in range(2):
                        rest(i * 2 + (B0 + 2 + s), s, 3 * CHUNK, 2)
                        scores(i * 2 + (B0 + 3 + s), s, 3 * CHUNK, 2, i * 6 + (G0 + 15 + 3 * s))
                rest(B0 + NC - 2, 0, 3 * CHUNK, 2)
                pe.wait_ge(a_stg, G0 + STG)
                pe.wait_ge(a_exp, B0 + NC - 1)
                for e in range(2):
                    last = nc.tensor.matmul(bank[e][:, 0:WIN + DSEQ], qs[0][64 * e:64 * e + 64, 0:2, :],
                                            ks[0][64 * e:64 * e + 64, 0:WIN + DSEQ], start=True, stop=True)
                last.then_inc(a_S, 1)
                rest(B0 + NC - 1, 1, 3 * CHUNK, 2)
                rest(B0 + NC, 0, WIN + DSEQ, 1)

            pe.wait_ge(a_lo, 2 * NB)
            loop_tiles(PAIR_G1, KT, x_hi, x_lo, c_hi, d_lo, x_act, X_ACT["G1"], y_dve, Y_DVE["G1"])

            pe.wait_ge(y_dve, Y_DVE["G0"])
            with pe.Fori(0, KT) as j:
                tile(0, j, PAIR_R, x_hi, x_lo, x_act, j * 3 + X_ACT["R"])
                tile(1, j, PAIR_R, x_hi, x_lo, y_act, j * 3 + Y_ACT["R"])
                pe.wait_ge(s_wab, j * 16 + 16)
                for n, (c0, cn) in enumerate(CHUNKS):
                    pe.wait_ge(r_xc, j * 3 + (n + 1))
                    pe.wait_ge(r_tanh, j * 3 + n)
                    nc.tensor.matmul(bank[6][:, 0:cn], wabs[:, 0, :], XC[n][:, 0:cn], start=True, stop=True)
                    nc.tensor.matmul(bank[7][:, 0:cn], wabs[:, 1, :], XC[n][:, 0:cn], start=True, stop=True).then_inc(r_ps, 1)

            pe.wait_ge(r_lo, 3 * KT)
            loop_tiles(PAIR_G0, KT, x_hi, x_lo, c_hi, d_lo, x_act, X_ACT["G0"], y_dve, Y_DVE["G0"])

            pe.wait_ge(m_lo, 3 * KT)
            loop_tiles(PAIR_O, KT // 2, x_hi, x_lo, x_hi, x_lo, x_dve, X_DVE["O"], y_dve, Y_DVE["O"])
            norm_sums(1)
            pe.wait_ge(n_lo, 6 * KT)

            with pe.Fori(0, FFN_PARTS) as f:
                pe.wait_ge(x_dve, f * DOWN + X_DVE["F"])
                pe.sem_inc(s_own[1], 1)
                with pe.Fori(0, KT) as j:
                    pair = f * PAIRS_PER_PART + j
                    tile(0, pair, PAIR_F, x_hi, x_lo, x_act, f * UP + j * 3 + X_ACT["F"])
                    tile(1, pair, PAIR_F, x_hi, x_lo, y_dve, f * (UP + DOWN) + j * 3 + Y_DVE["F"])
                pe.wait_ge(f_lo, f * (3 * KT) + 3 * KT)
                pe.sem_inc(s_own[1], 1)
                with pe.Fori(0, KT // 2) as j:
                    pair = f * PAIRS_PER_PART + j
                    tile(0, pair, PAIR_F + KT, act_hi, act_lo, x_dve, f * DOWN + j * 3 + X_DVE["F"])
                    tile(1, pair, PAIR_F + KT, act_hi, act_lo, y_dve, f * (UP + DOWN) + j * 3 + (Y_DVE["F"] + UP))

        @block.scalar
        def _(act):
            A = nc.scalar.activation

            def wait(sem_, value):
                act.wait_ge(sem_, value)
                act.sem_inc(s_own[2], 1)

            def norm(which):
                for n, (c0, cn) in enumerate(CHUNKS):
                    act.wait_ge(n_ps, 3 * which + n + 1)
                    A(nrs[:, c0:c0 + cn], bank[6 + n % 2][:, 0:cn], ACT.Sqrt, bias=epsc[:, 0:1], scale=1.0 / DM).then_inc(n_rt, 1)
                for n, (c0, cn) in enumerate(CHUNKS):
                    with act.Fori(0, KT // 2) as i:
                        for h in range(2):
                            wait(n_f32, i * 2 + (KT * (3 * which + n) + h + 1))
                            A(row(x_hi, i * 2 + h, c0, cn), ntmp[h][:, 0:cn], ACT.Copy).then_inc(n_hi, 1)

            for k in range(KT):
                act.wait_ge(s_x[k], 16)
                A(merged[:, k, :], resid[:, k, :], ACT.Square).then_inc(n_sq, 1)
            act.wait_ge(s_vec, 32)
            A(halfb[:, 0:2 * KT], V("bg_lru", 0, 2 * KT), ACT.Copy, scale=0.5)
            A(halfb[:, 2 * KT:4 * KT], V("b_a", 0, 2 * KT), ACT.Copy, scale=0.5)
            A(lam_t[:, 0, :], V("lam", 0, KT), ACT.Abs).then_inc(act_c, 1)
            act.wait_ge(act_c, 1)
            A(lam_t[:, 1, :], lam_t[:, 0, :], ACT.Exp, scale=-1.0).then_inc(s_exp_lam, 1)
            act.wait_ge(s_eps, 1)
            norm(0)

            for a in range(2):
                p0, B0 = ATT_PAIRS * a, NB * a
                if a:
                    act.wait_ge(s_out, 16 * 4)
                for n, (c0, cn) in enumerate(CHUNKS):
                    act.wait_ge(x_done, 3 * p0 + n + 1)
                    A(kN[:, c0:c0 + cn], bank[n][:, 0:cn], ACT.Copy)
                    A(kG[:, c0:c0 + cn], bank[n][:, 0:cn], ACT.Square).then_inc(x_act, 1)
                for n, (c0, cn) in enumerate(CHUNKS):
                    act.wait_ge(y_done, 3 * p0 + n + 1)
                    A(vT[:, c0:c0 + cn], bank[3 + n][:, 0:cn], ACT.Copy).then_inc(y_act, 1)
                for n, (c0, cn) in enumerate(CHUNKS):
                    act.wait_ge(k_ps, 3 * a + n + 1)
                    A(nrs[:, c0:c0 + cn], bank[6 + n % 2][:, 0:cn], ACT.Sqrt, bias=epsc[:, 0:1], scale=1.0 / HD).then_inc(k_rt, 1)
                with act.Fori(0, ATT_PAIRS - 1) as i:
                    for s, (done, free) in enumerate(((x_done, x_act), (y_done, y_act))):
                        for n, (c0, cn) in enumerate(CHUNKS):
                            wait(done, i * 3 + (3 * p0 + 3 + n + 1))
                            A(row(qT, i * 2 + s, c0, cn), bank[3 * s + n][:, 0:cn], ACT.Copy).then_inc(free, 1)
                        wait(free, i * 3 + (3 * p0 + 6))
                        A(q2[:, 0:NC, bass.ds(i * (2 * CHUNK) + s * CHUNK, CHUNK)],
                          row(qT, i * 2 + s, 0, SEQ).rearrange("p (c n) -> p c n", n=CHUNK), ACT.Square)
                        A(q2[:, NC, bass.ds(i * (2 * DSEQ) + s * DSEQ, DSEQ)], row(qT, i * 2 + s, SMP, DSEQ), ACT.Square).then_inc(q_sq, 1)
                act.wait_ge(q_ps, a + 1)
                A(rq[:, :], bank[7][:, 0:4 * NC + 2], ACT.Sqrt, bias=epsc[:, 1:2]).then_inc(q_rt, 1)
                act.wait_ge(k_rdy, a + 1)
                act.wait_ge(y_act, 3 * (p0 + 1))
                act.dma_start(o_kp[a], kN[:, SEQ - WIN:SEQ]).then_inc(s_out, 16)
                act.dma_start(o_ks[a], kN[:, SMP:T]).then_inc(s_out, 16)
                act.dma_start(o_vp[a], vT[:, SEQ - WIN:SEQ]).then_inc(s_out, 16)
                act.dma_start(o_vs[a], vT[:, SMP:T]).then_inc(s_out, 16)

                def exps(b, s, keys, nu):
                    act.wait_ge(a_stat, b + 1)
                    sm = small[s]
                    A(sm[:, 4, 0:nu], sm[:, 3, 0:nu], ACT.Exp)
                    for v in range(nu):
                        b_, c_ = (2 * s + v // 2, v % 2 * 192) if nu == 4 else (v, 0)
                        last = A(pr[s][:, v, 0:keys], bank[b_][:, c_:c_ + keys], ACT.Exp,
                                 bias=sm[:, 2, v:v + 1], scale=sm[:, 1, v:v + 1], accum_out=sm[:, 5, v:v + 1])
                    last.then_inc(a_exp, 1)

                def evac(b, keys, nu):
                    act.wait_ge(a_T, b + 1)
                    act.wait_ge(a_O, b)
                    kn = min(keys, P)
                    A(pt[0][0:kn, 0:nu * P], bank[4][0:kn, 0:nu * P], ACT.Copy).then_inc(a_ev, 1)

                def hi(b, c0, cn):
                    wait(a_O, b + 1)
                    A(c_hi[:, 4 * a:4 * a + 4, cols(c0, cn)], bank[7][:, 0:4 * cn].rearrange("p (a b) -> p a b", b=cn),
                      ACT.Copy).then_inc(a_hi, 1)

                exps(B0, 0, CHUNK, 4)
                exps(B0 + 1, 1, 2 * CHUNK, 4)
                for l in range(2):
                    evac(B0 + l, (l + 1) * CHUNK, 4)
                    hi(B0 + l, l * CHUNK, CHUNK)
                    exps(B0 + 2 + l, l, 3 * CHUNK, 4)
                with act.Fori(0, GEN // 2) as i:
                    for s in range(2):
                        evac(i * 2 + (B0 + 2 + s), 3 * CHUNK, 4)
                        hi(i * 2 + (B0 + 2 + s), i * (2 * CHUNK) + (2 + s) * CHUNK, CHUNK)
                        exps(i * 2 + (B0 + 4 + s), s, 3 * CHUNK, 4)
                evac(B0 + NC - 2, 3 * CHUNK, 4)
                hi(B0 + NC - 2, SEQ - 2 * CHUNK, CHUNK)
                exps(B0 + NC, 0, WIN + DSEQ, 2)
                evac(B0 + NC - 1, 3 * CHUNK, 4)
                hi(B0 + NC - 1, SEQ - CHUNK, CHUNK)
                evac(B0 + NC, WIN + DSEQ, 2)
                hi(B0 + NC, SMP, DSEQ)

            def gates(p0, half0, used):
                with act.Fori(0, KT) as j:
                    for n, (c0, cn) in enumerate(CHUNKS):
                        wait(x_done, j * 3 + (3 * p0 + n + 1))
                        wait(y_dve, j * 3 + (used + n - 2))
                        A(GC[n][:, 0:cn], bank[n][:, 0:cn], ACT.Tanh, bias=halfb[:, bass.ds(j + half0, 1)], scale=0.5).then_inc(x_act, 1)

            gates(PAIR_G1, KT, Y_DVE["G1"])

            act.wait_ge(y_dve, Y_DVE["G0"])
            act.wait_ge(s_lamc, 1)
            with act.Fori(0, KT) as j:
                act.dma_start(wabs[:, :, :], wab[bass.ds(j, 1)].rearrange("a p m n -> (a p) m n")).then_inc(s_wab, 16)
                for n, (c0, cn) in enumerate(CHUNKS):
                    wait(x_done, j * 3 + (3 * PAIR_R + n + 1))
                    A(U[:, LRU_HIST + c0:LRU_HIST + c0 + cn], bank[n][:, 0:cn], ACT.Copy).then_inc(x_act, 1)
                wait(r_fix, j + 1)
                for n, (c0, cn) in enumerate(CHUNKS):
                    A(XC[n][:, 0:cn], U[:, LRU_HIST + c0:LRU_HIST + c0 + cn], ACT.Identity,
                      bias=VD("conv_b", j), scale=VD("conv_w", j * 4 + 3)).then_inc(r_x0, 1)
                act.wait_ge(r_lo, j * 3)
                for n, (c0, cn) in enumerate(CHUNKS):
                    ck = slice(c0, c0 + cn)
                    wait(r_ps, j * 3 + (n + 1))
                    A(FA[:, ck], bank[6][:, 0:cn], ACT.Tanh, bias=halfb[:, bass.ds(j + 2 * KT, 1)], scale=0.5)
                    A(FI[:, ck], bank[7][:, 0:cn], ACT.Tanh, bias=halfb[:, bass.ds(j + 3 * KT, 1)], scale=0.5).then_inc(r_tanh, 1)
                    wait(r_tanh, j * 3 + (n + 1))
                    A(row(resid, j, c0, cn), FA[:, ck], ACT.Tanh, bias=lamc[:, 0, bass.ds(j, 1)], scale=lamc[:, 0, bass.ds(j, 1)])
                    A(FA[:, ck], FA[:, ck], ACT.Exp, bias=lamc[:, 1, bass.ds(j, 1)], scale=lamc[:, 1, bass.ds(j, 1)]).then_inc(act_c, 1)
                    wait(act_c, j * 3 + (n + 2))
                    A(FS[:, ck], FA[:, ck], ACT.Square).then_inc(r_sqa, 1)
                act.wait_ge(r_om, j * 3 + 3)
                A(FS[:, :], FS[:, :], ACT.Sqrt, scale=0.25).then_inc(r_root, 1)
                act.wait_ge(r_h, j + 1)
                for n, (c0, cn) in enumerate(CHUNKS):
                    wait(y_done, j * 3 + (3 * PAIR_R + n + 1))
                    A(FS[:, c0:c0 + cn], bank[3 + n][:, 0:cn], ACT.Gelu_apprx_tanh).then_inc(y_act, 1)
                for n, (c0, cn) in enumerate(CHUNKS):
                    wait(r_z, j * 3 + (n + 1))
                    A(row(c_hi, j, c0, cn), FA[:, c0:c0 + cn], ACT.Copy).then_inc(r_hi, 1)

            gates(PAIR_G0, 0, Y_DVE["G0"])

            act.wait_ge(y_done, 3 * PAIR_O)
            for h in range(2):
                kk = slice(h * KT // 2, (h + 1) * KT // 2)
                act.dma_start(sqsum[:, kk, :], xT[kk].rearrange("k p n -> p k n")).then_inc(s_xres[h], 16)
            act.wait_ge(m_mrg, 3 * KT)
            for n, (c0, cn) in enumerate(CHUNKS):
                with act.Fori(0, KT) as k:
                    A(row(x_hi, k, c0, cn), row(merged, k, c0, cn), ACT.Copy, scale=0.5).then_inc(m_hi, 1)
            act.wait_ge(m_lo, 3 * KT)
            with act.Fori(0, KT // 2) as i:
                for s, (free, freed) in enumerate(((x_dve, X_DVE), (y_dve, Y_DVE))):
                    wait(free, i * 3 + (freed["O"] + 3))
                    A(row(merged, i * 2 + s, 0, T), row(resid, i * 2 + s, 0, T), ACT.Square).then_inc(n_sq, 1)
            norm(1)

            with act.Fori(0, FFN_PARTS) as f:
                with act.Fori(0, KT) as j:
                    p3 = f * (3 * PAIRS_PER_PART) + j * 3
                    used = f * (UP + DOWN) + j * 3 + Y_DVE["F"]
                    ft = f * KT + j
                    for n, (c0, cn) in enumerate(CHUNKS):
                        act.wait_ge(x_done, p3 + (3 * PAIR_F + n + 1))
                        A(GB[:, FFN_HIST + c0:FFN_HIST + c0 + cn], bank[n][:, 0:cn], ACT.Copy).then_inc(x_act, 1)
                    wait(f_fix, ft + 1)
                    for n, (c0, cn) in enumerate(CHUNKS):
                        wait(y_dve, used + (n - 2))
                        A(GC[n][:, 0:cn], GB[:, FFN_HIST + c0:FFN_HIST + c0 + cn], ACT.Identity,
                          bias=VD("fconv_b", ft), scale=VD("fconv_w", ft * 3 + 2)).then_inc(f_c0, 1)
                    for n, (c0, cn) in enumerate(CHUNKS):
                        wait(f_conv, ft * 3 + (n + 1))
                        A(GC[n][:, 0:cn], GC[n][:, 0:cn], ACT.Gelu_apprx_tanh).then_inc(f_gelu, 1)
                    for n, (c0, cn) in enumerate(CHUNKS):
                        wait(y_dve, used + (n + 1))
                        A(row(act_hi, j, c0, cn), GV[n][:, 0:cn], ACT.Copy).then_inc(f_hi, 1)

        @block.vector
        def _(dve):
            D = nc.vector
            ch = Count(dve_c)

            def link(ins):
                ch.inc(ins)
                dve.wait_ge(dve_c, ch.value())

            def norm(which):
                g = "g_ffn" if which else "g_mix"
                for n, (c0, cn) in enumerate(CHUNKS):
                    dve.wait_ge(n_rt, 3 * which + n + 1)
                    link(D.reciprocal(nrs[:, c0:c0 + cn], nrs[:, c0:c0 + cn]))
                    with dve.Fori(0, KT // 2) as i:
                        dve.wait_ge(n_lo, i * 2 + KT * (3 * which + n))
                        for h in range(2):
                            D.scalar_tensor_tensor(ntmp[h][:, 0:cn], row(resid, i * 2 + h, c0, cn), VD(g, i * 2 + h),
                                                   nrs[:, c0:c0 + cn], ALU.mult, ALU.mult).then_inc(n_f32, 1)
                        for h in range(2):
                            dve.wait_ge(n_hi, i * 2 + (KT * (3 * which + n) + h + 1))
                            D.tensor_tensor(row(x_lo, i * 2 + h, c0, cn), ntmp[h][:, 0:cn],
                                            row(x_hi, i * 2 + h, c0, cn).bitcast(F32), ALU.subtract).then_inc(n_lo, 1)

            dve.sem_inc(x_dve, 3)
            dve.sem_inc(y_dve, 3)
            D.memset(epsc[:, 0:1], EPS)
            D.memset(epsc[:, 1:2], HD * EPS).then_inc(s_eps, 1)
            link(D.memset(nacc[:, :], 0.0))
            for k in range(KT):
                dve.wait_ge(n_sq, k + 1)
                if k:
                    dve.wait_ge(n_acc, k)
                D.tensor_tensor(nacc[:, :], nacc[:, :], merged[:, k, :], ALU.add).then_inc(n_acc, 1)
            dve.wait_ge(s_exp_lam, 1)
            e, s_, s2, ac = (lam_t[:, i, :] for i in (1, 2, 3, 4))
            link(D.tensor_scalar(s2, e, 2.0, None, ALU.add))
            link(D.reciprocal(s2, s2))
            link(D.tensor_tensor(s_, e, s2, ALU.mult))
            link(D.tensor_tensor(s2, s_, s_, ALU.mult))
            link(D.memset(ac, 1.0 / 19))
            for m in range(17, 0, -2):
                link(D.tensor_tensor(ac, ac, s2, ALU.mult))
                link(D.tensor_scalar(ac, ac, 1.0 / m, None, ALU.add))
            link(D.tensor_tensor(ac, ac, s_, ALU.mult))
            link(D.tensor_scalar(s2, V("lam", 0, KT), -1.0, 0.0, ALU.mult, ALU.max))
            link(D.scalar_tensor_tensor(ac, ac, 2.0, s2, ALU.mult, ALU.add))
            D.tensor_scalar(lamc[:, 0, :], ac, 4.0, None, ALU.mult)
            D.tensor_scalar(lamc[:, 1, :], ac, -4.0, None, ALU.mult).then_inc(s_lamc, 1)
            link(D.tensor_scalar(negsink[:, :], V("sink_p", 0, 12), -1.0, None, ALU.mult))
            norm(0)

            for a in range(2):
                p0, B0 = ATT_PAIRS * a, NB * a
                for n, (c0, cn) in enumerate(CHUNKS):
                    ck = slice(c0, c0 + cn)
                    dve.wait_ge(k_rt, 3 * a + n + 1)
                    link(D.reciprocal(nrs[:, ck], nrs[:, ck]))
                    link(D.scalar_tensor_tensor(kN[:, ck], kN[:, ck], V("g_k"), nrs[:, ck], ALU.mult, ALU.mult))
                    last = D.tensor_scalar(kG[:, ck], kN[:, ck], V("g_q"), None, ALU.mult)
                last.then_inc(k_rdy, 1)
                dve.wait_ge(q_rt, a + 1)
                link(D.reciprocal(rq[:, :], rq[:, :]))
                link(D.tensor_scalar(nrq[:, :], rq[:, :], -1.0, None, ALU.mult))
                for t in (c_hi, d_lo):
                    D.memset(t[:, 4 * a:4 * a + 4, SEQ:SMP].bitcast(F32), 0.0)

                def stats(b, s, keys, nu, r0, sink0):
                    sm = small[s]
                    dve.wait_ge(a_S, b + 1)
                    if nu == 4:
                        src = bankpair[s][:, :, 0:384].rearrange("p b (v k) -> p b v k", v=2)[:, :, :, 0:keys]
                        dst = sm[:, 0, 0:4].rearrange("p (b v) -> p b v", v=2)
                    else:
                        src = bankpair[0][:, :, 0:keys]
                        dst = sm[:, 0, 0:2]
                    D.tensor_copy(sm[:, 1, 0:nu], rq[:, cols(r0, nu)])
                    link(D.tensor_reduce(dst, src, AXX, ALU.max))
                    link(D.tensor_tensor(sm[:, 6, 0:nu], sm[:, 0, 0:nu], nrq[:, cols(r0, nu)], ALU.mult))
                    link(D.tensor_tensor(sm[:, 2, 0:nu], sm[:, 6, 0:nu], negsink[:, sink0:sink0 + nu], ALU.min))
                    D.tensor_tensor(sm[:, 3, 0:nu], sm[:, 2, 0:nu], negsink[:, sink0:sink0 + nu], ALU.subtract).then_inc(a_stat, 1)

                def normalise(b, s, keys, nu):
                    sm = small[s]
                    dve.wait_ge(a_exp, b + 1)
                    link(D.tensor_tensor(sm[:, 7, 0:nu], sm[:, 5, 0:nu], sm[:, 4, 0:nu], ALU.add))
                    link(D.reciprocal(sm[:, 7, 0:nu], sm[:, 7, 0:nu]))
                    for v in range(nu):
                        last = D.tensor_scalar(pr[s][:, v, 0:keys], pr[s][:, v, 0:keys], sm[:, 7, v:v + 1], None, ALU.mult)
                    last.then_inc(a_nrm, 1)

                def evac(b, keys, nu):
                    dve.wait_ge(a_T, b + 1)
                    dve.wait_ge(a_O, b)
                    if keys > P:
                        D.tensor_copy(pt[1][0:keys - P, 0:nu * P], bank[5][0:keys - P, 0:nu * P])
                        D.tensor_copy(vt[1][0:keys - P, :], bank[6][0:keys - P, P:2 * P])
                    kn = min(keys, P)
                    D.tensor_copy(vt[0][0:kn, :], bank[6][0:kn, 0:P]).then_inc(a_evv, 1)

                def lo(b, c0, cn):
                    dve.wait_ge(a_hi, b + 1)
                    D.tensor_tensor(d_lo[:, 4 * a:4 * a + 4, cols(c0, cn)], bank[7][:, 0:4 * cn].rearrange("p (a b) -> p a b", b=cn),
                                    c_hi[:, 4 * a:4 * a + 4, cols(c0, cn)].bitcast(F32), ALU.subtract).then_inc(a_lo, 1)

                stats(B0, 0, CHUNK, 4, 0, 4 * a)
                stats(B0 + 1, 1, 2 * CHUNK, 4, 4, 4 * a)
                normalise(B0, 0, CHUNK, 4)
                for l in range(2):
                    evac(B0 + l, (l + 1) * CHUNK, 4)
                    normalise(B0 + l + 1, 1 - l, (l + 2) * CHUNK, 4)
                    lo(B0 + l, l * CHUNK, CHUNK)
                    stats(B0 + 2 + l, l, 3 * CHUNK, 4, 4 * (2 + l), 4 * a)
                with dve.Fori(0, GEN // 2) as i:
                    ch.enter(i, 2 * 5)
                    for s in range(2):
                        evac(i * 2 + (B0 + 2 + s), 3 * CHUNK, 4)
                        normalise(i * 2 + (B0 + 3 + s), 1 - s, 3 * CHUNK, 4)
                        lo(i * 2 + (B0 + 2 + s), i * (2 * CHUNK) + (2 + s) * CHUNK, CHUNK)
                        stats(i * 2 + (B0 + 4 + s), s, 3 * CHUNK, 4, i * 8 + 4 * (4 + s), 4 * a)
                    ch.leave(GEN // 2)
                evac(B0 + NC - 2, 3 * CHUNK, 4)
                normalise(B0 + NC - 1, 1, 3 * CHUNK, 4)
                lo(B0 + NC - 2, SEQ - 2 * CHUNK, CHUNK)
                stats(B0 + NC, 0, WIN + DSEQ, 2, 4 * NC, 8 + 2 * a)
                evac(B0 + NC - 1, 3 * CHUNK, 4)
                normalise(B0 + NC, 0, WIN + DSEQ, 2)
                lo(B0 + NC - 1, SEQ - CHUNK, CHUNK)
                evac(B0 + NC, WIN + DSEQ, 2)
                lo(B0 + NC, SMP, DSEQ)

            dve.wait_ge(s_out, 16 * 8)
            with dve.Fori(0, KT) as j:
                for n, (c0, cn) in enumerate(CHUNKS):
                    dve.wait_ge(x_act, j * 3 + (X_ACT["G1"] + n + 1))
                    dve.wait_ge(y_done, j * 3 + (3 * PAIR_G1 + n + 1))
                    D.scalar_tensor_tensor(row(merged, j, c0, cn), GC[n][:, 0:cn], 1.0, bank[3 + n][:, 0:cn],
                                           ALU.add, ALU.mult).then_inc(y_dve, 1)

            link(D.memset(U[:, 0:LRU_HIST], 0.0))
            with dve.Fori(0, KT) as j:
                ch.enter(j, 2 * 3 + 2)
                dve.wait_ge(x_act, j * 3 + (X_ACT["R"] + 3))
                hs = LRU_HIST + SMP - LRU_HIST
                for r, c0 in enumerate((SEQ, T)):
                    D.tensor_copy(st_lconv[:, bass.ds(j, 1), r, :].rearrange("p a n -> p (a n)"), U[:, c0:c0 + LRU_HIST])
                D.tensor_copy(U[:, hs:hs + LRU_HIST], VD("conv0", j * LRU_HIST, LRU_HIST)).then_inc(r_fix, 1)
                for n, (c0, cn) in enumerate(CHUNKS):
                    dve.wait_ge(r_x0, j * 3 + (n + 1))
                    for i, tap in enumerate((2, 1, 0)):
                        ins = D.scalar_tensor_tensor(XC[n][:, 0:cn], U[:, tap + c0:tap + c0 + cn], VD("conv_w", j * 4 + tap),
                                                     XC[n][:, 0:cn], ALU.mult, ALU.add)
                        if tap:
                            link(ins)
                    ins.then_inc(r_xc, 1)
                for n, (c0, cn) in enumerate(CHUNKS):
                    ck = slice(c0, c0 + cn)
                    dve.wait_ge(r_tanh, j * 3 + (n + 1))
                    D.scalar_tensor_tensor(FI[:, ck], FI[:, ck], 1.0, XC[n][:, 0:cn], ALU.add, ALU.mult)
                    dve.wait_ge(r_sqa, j * 3 + (n + 1))
                    D.scalar_tensor_tensor(FS[:, ck], FS[:, ck], 1.0, row(resid, j, c0, cn), ALU.add, ALU.mult).then_inc(r_om, 1)
                dve.wait_ge(r_root, j + 1)
                link(D.tensor_tensor(FI[:, :], FI[:, :], FS[:, :], ALU.mult))
                D.tensor_tensor_scan(FI[:, 0:SEQ], FA[:, 0:SEQ], FI[:, 0:SEQ], 0.0, ALU.mult, ALU.add)
                link(D.memset(FI[:, SEQ:SMP], 0.0))
                ch2 = D.tensor_tensor_scan(FI[:, SMP:T], FA[:, SMP:T], FI[:, SMP:T], VD("h0", j), ALU.mult, ALU.add)
                ch2.then_inc(r_h, 1)
                dve.wait_ge(r_h, j + 1)
                for r, c0 in enumerate((SEQ - 1, T - 1)):
                    D.tensor_copy(st_h[:, bass.ds(j, 1), r:r + 1].rearrange("p a n -> p (a n)"), FI[:, c0:c0 + 1])
                for n, (c0, cn) in enumerate(CHUNKS):
                    dve.wait_ge(y_act, j * 3 + (Y_ACT["R"] + n + 1))
                    D.tensor_tensor(FA[:, c0:c0 + cn], FI[:, c0:c0 + cn], FS[:, c0:c0 + cn], ALU.mult).then_inc(r_z, 1)
                for n, (c0, cn) in enumerate(CHUNKS):
                    dve.wait_ge(r_hi, j * 3 + (n + 1))
                    D.tensor_tensor(row(d_lo, j, c0, cn), FA[:, c0:c0 + cn], row(c_hi, j, c0, cn).bitcast(F32),
                                    ALU.subtract).then_inc(r_lo, 1)
                ch.leave(KT)

            with dve.Fori(0, KT) as j:
                for n, (c0, cn) in enumerate(CHUNKS):
                    dve.wait_ge(x_act, j * 3 + (X_ACT["G0"] + n + 1))
                    dve.wait_ge(y_done, j * 3 + (3 * PAIR_G0 + n + 1))
                    D.scalar_tensor_tensor(GV[n][:, 0:cn], GC[n][:, 0:cn], 1.0, bank[3 + n][:, 0:cn],
                                           ALU.add, ALU.mult).then_inc(y_dve, 1)
                    dve.wait_ge(y_dve, j * 3 + (Y_DVE["G0"] + n + 1))
                    D.tensor_tensor(row(merged, j, c0, cn), row(merged, j, c0, cn), GV[n][:, 0:cn], ALU.add).then_inc(m_mrg, 1)
            for n, (c0, cn) in enumerate(CHUNKS):
                with dve.Fori(0, KT) as k:
                    dve.wait_ge(m_hi, k + (KT * n + 1))
                    D.scalar_tensor_tensor(row(x_lo, k, c0, cn), row(merged, k, c0, cn), 0.5, row(x_hi, k, c0, cn).bitcast(F32),
                                           ALU.mult, ALU.subtract).then_inc(m_lo, 1)

            for h in range(2):
                dve.wait_ge(s_xres[h], 16)
            link(D.memset(nacc[:, :], 0.0))
            with dve.Fori(0, KT // 2) as i:
                for s, (done, free) in enumerate(((x_done, x_dve), (y_done, y_dve))):
                    for n, (c0, cn) in enumerate(CHUNKS):
                        dve.wait_ge(done, i * 3 + (3 * PAIR_O + n + 1))
                        D.tensor_tensor(row(resid, i * 2 + s, c0, cn), bank[3 * s + n][:, 0:cn], row(sqsum, i * 2 + s, c0, cn),
                                        ALU.add).then_inc(free, 1)
                    dve.wait_ge(n_sq, i * 2 + (KT + s + 1))
                    dve.wait_ge(n_acc, i * 2 + (KT + s))
                    D.tensor_tensor(nacc[:, :], nacc[:, :], row(merged, i * 2 + s, 0, T), ALU.add).then_inc(n_acc, 1)
            norm(1)

            link(D.memset(GB[:, 0:FFN_HIST], 0.0))
            with dve.Fori(0, FFN_PARTS) as f:
                ch.enter(f, 3 * KT)
                with dve.Fori(0, KT) as j:
                    ch.enter(j, 3)
                    p3 = f * (3 * PAIRS_PER_PART) + j * 3
                    ft = f * KT + j
                    dve.wait_ge(x_act, f * UP + j * 3 + (X_ACT["F"] + 3))
                    for r, c0 in enumerate((SEQ, T)):
                        D.tensor_copy(st_fconv[:, bass.ds(ft, 1), r, :].rearrange("p a n -> p (a n)"), GB[:, c0:c0 + FFN_HIST])
                    D.tensor_copy(GB[:, SMP:SMP + FFN_HIST], VD("fconv0", ft * FFN_HIST, FFN_HIST)).then_inc(f_fix, 1)
                    for n, (c0, cn) in enumerate(CHUNKS):
                        dve.wait_ge(f_c0, ft * 3 + (n + 1))
                        for tap in (1, 0):
                            ins = D.scalar_tensor_tensor(GC[n][:, 0:cn], GB[:, tap + c0:tap + c0 + cn], VD("fconv_w", ft * 3 + tap),
                                                         GC[n][:, 0:cn], ALU.mult, ALU.add)
                            if tap:
                                link(ins)
                        ins.then_inc(f_conv, 1)
                    for n, (c0, cn) in enumerate(CHUNKS):
                        dve.wait_ge(f_gelu, ft * 3 + (n + 1))
                        dve.wait_ge(y_done, p3 + (3 * PAIR_F + n + 1))
                        D.tensor_tensor(GV[n][:, 0:cn], GC[n][:, 0:cn], bank[3 + n][:, 0:cn], ALU.mult).then_inc(y_dve, 1)
                    for n, (c0, cn) in enumerate(CHUNKS):
                        dve.wait_ge(f_hi, ft * 3 + (n + 1))
                        D.tensor_tensor(row(act_lo, j, c0, cn), GV[n][:, 0:cn], row(act_hi, j, c0, cn).bitcast(F32),
                                        ALU.subtract).then_inc(f_lo, 1)
                    ch.leave(KT)
                ch.leave(FFN_PARTS)
                with dve.Fori(0, KT // 2) as i:
                    for s, (done, free) in enumerate(((x_done, x_dve), (y_done, y_dve))):
                        for n, (c0, cn) in enumerate(CHUNKS):
                            dve.wait_ge(done, f * (3 * PAIRS_PER_PART) + i * 3 + (3 * (PAIR_F + KT) + n + 1))
                            D.tensor_tensor(row(resid, i * 2 + s, c0, cn), row(resid, i * 2 + s, c0, cn), bank[3 * s + n][:, 0:cn],
                                            ALU.add).then_inc(free, 1)


def _tiles(w):
    k, n = w.shape
    return w.reshape(k // P, P, n // P, P).transpose(2, 1, 0, 3).reshape(n // P, P, k)


def _cols(v):
    return v.reshape(-1, P).T


def kernel(**inputs):
    import concourse.bacc as bacc
    from concourse.bass_utils import run_bass_kernel_spmd

    x = {k: np.asarray(v) for k, v in inputs.items()}
    f32 = np.float32
    cat, ct = np.concatenate, np.ascontiguousarray

    order = [4 * (2 * a + e) + s for a in range(2) for s in range(4) for e in range(2)]
    rows = cat([np.arange(HD) + HD * h for h in order])
    w_in = x["w_in"][0]
    u, y, q, k, v, g0, g1 = np.split(w_in, np.cumsum([DM, DM, DM, NKV * HD, NKV * HD, DM]), axis=1)
    q = _tiles(q[:, rows])
    k, v, u, y, g0, g1 = (_tiles(w) for w in (k, v, u, y, g0, g1))
    br_l, br_a = _tiles(x["w_br_lru"][0]), _tiles(x["w_br_attn"][0][rows])
    out = _tiles(x["w_out"][0])
    gate, up = (_tiles(w) for w in np.split(x["w_up"][0], 2, axis=1))
    down = [_tiles(w) for w in np.split(x["w_down"][0], FFN_PARTS, axis=0)]
    slots = []
    for a in range(2):
        slots += [k[a], v[a], *q[4 * a:4 * a + 4]]
    for one, two in ((g1, br_a), (u, y), (g0, br_l)):
        for j in range(KT):
            slots += [one[j], two[j]]
    slots += list(out)
    for f in range(FFN_PARTS):
        for j in range(KT):
            slots += [gate[KT * f + j], up[KT * f + j]]
        slots += list(down[f])
    W = np.stack(slots)
    assert W.shape[0] == NSLOT

    xT = np.zeros((DM, T), f32)
    xT[:, :SEQ], xT[:, SMP:] = x["x_prompt"][0].T, x["x_sample"][0].T
    wab = np.zeros((KT, P, 2, P), f32)
    for m, name in enumerate(("w_lru_a", "w_lru_i")):
        for j in range(KT):
            for e in range(2):
                wab[j, HD * e:HD * e + HD, m, HD * e:HD * e + HD] = x[name][0, 2 * j + e]
    sink = x["attn_sink"][0]
    sink_p = np.stack([np.repeat([sink[4 * (2 * a + e) + 2 * uu + s] for s in range(2)], CHUNK)
                       for a in range(2) for e in range(2) for uu in range(2)], axis=1)
    sink_s = np.stack([np.repeat([sink[4 * (2 * a + e) + s] for s in range(4)], DSEQ)
                       for a in range(2) for e in range(2)], axis=1)
    bg = x["b_gate"][0]
    parts = dict(bg_lru=_cols(bg[:DM]), bg_att=_cols(bg[DM:]),
                 conv_w=x["w_lru_conv"][0].reshape(4, KT, P).transpose(2, 1, 0).reshape(P, -1), conv_b=_cols(x["b_lru_conv"][0]),
                 b_a=_cols(x["b_lru_a"][0]), b_i=_cols(x["b_lru_i"][0]), lam=_cols(x["lru_lambda"][0]),
                 g_mix=_cols(x["g_mix"][0]), g_ffn=_cols(x["g_ffn"][0]),
                 fconv_w=x["w_ffn_conv"][0].reshape(3, FT, P).transpose(2, 1, 0).reshape(P, -1), fconv_b=_cols(x["b_ffn_conv"][0]),
                 h0=_cols(x["state_lru_h"][0, 0]), g_q=np.tile(x["g_q"][0], 2)[:, None], g_k=np.tile(x["g_k"][0], 2)[:, None],
                 sink_p=sink_p, sink_s=sink_s,
                 conv0=x["state_lru_conv"][0, 0].reshape(LRU_HIST, KT, P).transpose(2, 1, 0).reshape(P, -1),
                 fconv0=x["state_ffn_conv"][0, 0].reshape(FFN_HIST, FT, P).transpose(2, 1, 0).reshape(P, -1))
    vecs = cat([parts[name] for name in VEC], axis=1)
    assert vecs.shape[1] == NVEC and all(parts[n].shape[1] == VEC[n][1] for n in VEC)
    two = np.kron(np.eye(2, dtype=f32), np.ones((HD, HD), f32))
    mats = np.stack([np.eye(P, dtype=f32), np.ones((P, P), f32), two], axis=1)
    kc, vc = (x[name][0, 0].transpose(1, 2, 0).reshape(2, P, WIN).transpose(1, 0, 2) for name in ("cache_k", "cache_v"))

    nc = bacc.Bacc("TRN2", target_bir_lowering=False, num_devices=1)
    arrays, args = {}, []
    for name, a in (("xT", xT.reshape(KT, P, T)), ("W", W), ("wab", wab), ("vecs", vecs), ("mats", mats), ("kc", kc), ("vc", vc)):
        arrays[name] = ct(a)
        args.append(nc.dram_tensor(name, list(a.shape), F32, kind="ExternalInput").ap())
    outs = dict(yT=[KT, P, T], lconv=[P, KT, 2, LRU_HIST], h=[P, KT, 2], fconv=[P, FT, 2, FFN_HIST],
                kp=[2, P, WIN], ks=[2, P, DSEQ], vp=[2, P, WIN], vs=[2, P, DSEQ])
    for name, shape in outs.items():
        args.append(nc.dram_tensor("o_" + name, shape, F32, kind="ExternalOutput").ap())
    build(nc, *args)
    r = run_bass_kernel_spmd(nc, [arrays], core_ids=[0]).results[0]
    o = {name: np.asarray(r["o_" + name]) for name in outs}
    yT = o["yT"].reshape(DM, T)

    def state(t, r_):
        return ct(t[:, :, r_, :].transpose(2, 1, 0).reshape(1, 1, t.shape[3], -1))

    def heads(t):
        return ct(t.reshape(2, 2, HD, -1).transpose(3, 0, 1, 2).reshape(1, 1, t.shape[2], NKV, HD))

    def last(r_):
        return ct(o["h"][:, :, r_].T.reshape(1, 1, DM))

    return (ct(yT[:, :SEQ].T)[None], ct(yT[:, SMP:].T)[None],
            state(o["lconv"], 0), last(0), heads(o["kp"]), heads(o["vp"]), state(o["fconv"], 0),
            state(o["lconv"], 1), last(1), heads(o["ks"]), heads(o["vs"]), state(o["fconv"], 1))
```

```python
from contextlib import ExitStack

import concourse.bass as bass
import numpy as np
from concourse import mybir

F32 = mybir.dt.float32
F32R = mybir.dt.float32r
ACT = mybir.ActivationFunctionType
ALU = mybir.AluOpType
AXX = mybir.AxisListType.X

P = 128
DM, SEQ, DSEQ, PAD = 1024, 1024, 32, 4
NH, NKV, HD, CHUNK, WIN = 16, 4, 64, 64, 128
DFF = 3 * DM
KT = DM // P
FT = DFF // P
SMP = SEQ + PAD
T = SMP + DSEQ
CHUNKS = [(0, 354), (354, 354), (708, 352)]
NC = SEQ // CHUNK
EPS = 1e-6
LRU_HIST, FFN_HIST = 3, 2

ATT_PAIRS = 3
PAIR_G1 = 2 * ATT_PAIRS
PAIR_R = PAIR_G1 + KT
PAIR_G0 = PAIR_R + KT
PAIR_O = PAIR_G0 + KT
PAIR_F = PAIR_O + KT // 2
FFN_PARTS = FT // KT
PAIRS_PER_PART = KT + KT // 2
NPAIR = PAIR_F + FFN_PARTS * PAIRS_PER_PART
NSLOT = 2 * NPAIR

X_ACT = dict(G1=6 * ATT_PAIRS)
X_ACT["R"] = X_ACT["G1"] + 3
X_ACT["G0"] = X_ACT["R"] + 3 * KT
X_ACT["F"] = X_ACT["G0"] + 3
Y_ACT = dict(G1=6 * ATT_PAIRS)
Y_ACT["R"] = Y_ACT["G1"] + 3 * (KT - 1)
Y_ACT["G0"] = Y_ACT["R"] + 3 * KT
X_DVE = dict(G1=3, G0=3 * KT, O=6 * KT - 3, F=6 * KT - 3 + 3 * KT // 2)
Y_DVE = dict(G1=3, G0=6, O=9, F=9 + 3 * KT // 2)
START = 4
NORM_BLOCKS = [(n, min(P * b, cn - P)) for n, (_, cn) in enumerate(CHUNKS) for b in range(3)]
UP, DOWN = 3 * KT, 3 * KT // 2
X_END = X_DVE["F"] + FFN_PARTS * DOWN
Y_END = Y_DVE["F"] + FFN_PARTS * (UP + DOWN)

VEC = {}
_at = 0
for _name, _n in (("bg_lru", KT), ("bg_att", KT), ("conv_w", 4 * KT), ("conv_b", KT), ("b_a", KT), ("b_i", KT), ("lam", KT),
                  ("g_mix", KT), ("g_ffn", KT), ("fconv_w", 3 * FT), ("fconv_b", FT), ("h0", KT), ("g_q", 1), ("g_k", 1),
                  ("sink_p", 8), ("sink_s", 4), ("conv0", LRU_HIST * KT), ("fconv0", FFN_HIST * FT)):
    VEC[_name] = (_at, _n)
    _at += _n
NVEC = _at


class Count:

    def __init__(self, sem):
        self.sem, self.n, self.turns = sem, 0, []

    def inc(self, ins):
        ins.then_inc(self.sem, 1)
        self.n += 1

    def value(self):
        v = self.n
        for i, k, _ in self.turns:
            v = i * k + v
        return v

    def enter(self, i, per_turn):
        self.turns.append((i, per_turn, self.n))

    def leave(self, trips):
        _, k, start = self.turns.pop()
        assert self.n - start == k, (self.n - start, k)
        self.n = start + k * trips


def build(nc, xT, W, wab, vecs, mats, kc, vc, yT, o_lconv, o_h, o_fconv, o_kp, o_ks, o_vp, o_vs):
    ctx = ExitStack()
    with ctx:
        def sem(name):
            return ctx.enter_context(nc.semaphore(name))

        base = [(nc.sbuf_base + 63) // 64 * 64]
        end = nc.sbuf_usable_end

        def place(name, shape, dt, at=None):
            size = 4 * int(np.prod(shape[1:]))
            if at is None:
                at = base[0]
                base[0] += (size + 31) // 32 * 32
                assert base[0] <= end, (name, base[0], end)
            return nc.alloc_sbuf_tensor_at(name, shape, dt, offset=at), at

        def sb(name, shape, dt=F32, at=None):
            return place(name, shape, dt, at)[0]

        FULL = [P, KT, T]
        x_hi, _ = place("x_hi", FULL, F32R)
        x_lo, _ = place("x_lo", FULL, F32R)
        c_hi, at_c = place("c_hi", FULL, F32R)
        d_lo, at_d = place("d_lo", FULL, F32R)
        act_lo, at_e = place("act_lo", FULL, F32R)
        resid = sb("resid", FULL, F32, at_c)
        sqsum = sb("sqsum", FULL, F32, at_d)
        merged = sb("merged", FULL, F32, at_e)
        act_hi = sb("act_hi", FULL, F32R, at_d)
        q2 = sb("q2", [P, NC + 1, 4 * CHUNK], F32, at_c + 4 * T * 4)
        qT = sb("qT", [P, 4, T], F32, at_e)
        kN = sb("kN", [P, T], F32, at_e + 4 * T * 4)
        row_bytes = (4 * T + 31) // 32 * 32
        kG = sb("kG", [P, T], F32, at_e + 4 * T * 4 + row_bytes)
        vT = sb("vT", [P, T], F32, at_e + 4 * T * 4 + 2 * row_bytes)
        kcs = sb("kcs", [P, 2, WIN], F32, at_e + 4 * T * 4 + 3 * row_bytes)
        vcs = sb("vcs", [P, 2, WIN], F32, at_e + 4 * T * 4 + 3 * row_bytes + 2 * WIN * 4)
        w_raw, w_hi, w_lo = [], [], []
        for s in range(2):
            r, at = place(f"w_raw{s}", [P, DM], F32)
            w_raw.append(r)
            w_lo.append(sb(f"w_lo{s}", [P, DM], F32R, at))
            w_hi.append(sb(f"w_hi{s}", [P, DM], F32R))
        vec = sb("vec", [P, NVEC])
        mat = sb("mat", [P, 3, P])
        ident, ones, bones = mat[:, 0, :], mat[:, 1, :], mat[:, 2, :]
        halfb = sb("halfb", [P, 4 * KT])
        lamc = sb("lamc", [P, 2, KT])
        lam_t = sb("lam_t", [P, 5, KT])
        st_lconv = sb("st_lconv", [P, KT, 2, LRU_HIST])
        st_h = sb("st_h", [P, KT, 2])
        st_fconv = sb("st_fconv", [P, FT, 2, FFN_HIST])
        negsink = sb("negsink", [P, 12])
        rq = sb("rq", [P, 4 * NC + 2])
        nrq = sb("nrq", [P, 4 * NC + 2])
        epsc = sb("epsc", [P, 2])
        warm = sb("warm", [P, 1])
        tr = base[0]
        gates_bytes = 3 * 1440
        GG = [sb(f"GG{i}", [P, 354], F32, tr + 1440 * i) for i in range(3)]
        U = sb("U", [P, LRU_HIST + T], F32, tr)
        base[0] += gates_bytes
        FA = sb("FA", [P, T])
        FI = sb("FI", [P, T])
        FS = sb("FS", [P, T])
        XC = [sb(f"XC{i}", [P, 354]) for i in range(3)]
        wabs = sb("wabs", [P, 2, P])
        at = [tr]

        def ta(name, shape):
            size = 4 * int(np.prod(shape[1:]))
            t = sb(name, shape, F32, at[0])
            at[0] += (size + 31) // 32 * 32
            assert at[0] <= end
            return t
        qs = [ta(f"qs{i}", [P, 4, CHUNK]) for i in range(2)]
        ks = [ta(f"ks{i}", [P, 3 * CHUNK]) for i in range(2)]
        vs = [ta(f"vs{i}", [P, 3 * CHUNK]) for i in range(2)]
        pr = [ta(f"pr{i}", [P, 4, 3 * CHUNK]) for i in range(2)]
        pt = [ta(f"pt{i}", [P, 4 * P]) for i in range(2)]
        vt = [ta(f"vt{i}", [P, P]) for i in range(2)]
        small = [ta(f"small{i}", [P, 8, 4]) for i in range(2)]
        at = [tr]
        GB = ta("GB", [P, FFN_HIST + T])
        GC = [ta(f"GC{i}", [P, 354]) for i in range(3)]
        GV = [ta(f"GV{i}", [P, 354]) for i in range(3)]
        at = [tr]
        nacc = ta("nacc", [P, T])
        nrs = ta("nrs", [P, T])
        nst = ta("nst", [P, 4, 2 * len(NORM_BLOCKS)])
        dg = ta("dg", [P, len(NORM_BLOCKS), P])
        ntmp = [ta(f"ntmp{i}", [P, 354]) for i in range(4)]

        bankpair = [ctx.enter_context(nc.psum_tensor(f"banks{b}", [P, 2, 512], F32)) for b in range(4)]
        bank = [bankpair[b // 2][:, b % 2, :] for b in range(8)]
        XB, YB = bank[0:3], bank[3:6]

        def V(name, i=0, n=1):
            a, _ = VEC[name]
            return vec[:, a + i:a + i + n]

        def VD(name, i, n=1):
            a, _ = VEC[name]
            return vec[:, bass.ds(i + a, n)]

        def row(t, k, c0, cn):
            if isinstance(k, int):
                return t[:, k, c0:c0 + cn]
            return t[:, bass.ds(k, 1), c0:c0 + cn].rearrange("p a n -> p (a n)")

        def cols(c0, n):
            return slice(c0, c0 + n) if isinstance(c0, int) else bass.ds(c0, n)

        s_vec = sem("tables_loaded")
        s_x = [sem(f"x_loaded{k}") for k in range(KT)]
        s_cache = sem("cache_loaded")
        s_xres = [sem(f"residual_x_loaded{k}") for k in range(2)]
        s_wab = sem("lru_gate_weights_loaded")
        wx_loaded, wy_loaded = sem("wx_loaded"), sem("wy_loaded")
        wx_ready, wy_ready = sem("wx_ready"), sem("wy_ready")
        w_hi_done = sem("w_hi_done")
        x_done, y_done = sem("x_done"), sem("y_done")
        x_act, y_act = sem("x_freed_by_act"), sem("y_freed_by_act")
        x_dve, y_dve = sem("x_freed_by_dve"), sem("y_freed_by_dve")
        act_c, dve_c = sem("act_chain"), sem("dve_chain")
        s_eps, s_exp_lam, s_lamc = sem("eps_set"), sem("exp_lambda"), sem("lambda_ready")
        n_sq, n_acc, n_ps, n_rt, n_dg, n_bc, n_f32, n_hi, n_lo = (
            sem(f"norm_{x}") for x in ("squares", "summed", "psum", "root", "diagonals", "broadcast", "f32", "hi", "lo"))
        n_lop = sem("norm_lo_by_pool")
        k_ps, k_rt, k_rdy = (sem(f"knorm_{x}") for x in ("psum", "root", "ready"))
        q_sq, q_ps, q_rt = sem("q_squares"), sem("q_sums"), sem("q_root")
        a_stg, a_S, a_stat, a_exp, a_nrm, a_T, a_ev, a_evv, a_O, a_hi, a_lo = (
            sem(f"att_{x}") for x in ("staged", "scores", "stats", "exp", "normalised", "transposed", "p_copied",
                                      "v_copied", "out", "hi", "lo"))
        r_u, r_fix, r_x0, r_xc, r_ps, r_tanh, r_sqa, r_om, r_root, r_h, r_gelu, r_z, r_hi, r_lo = (
            sem(f"lru_{x}") for x in ("u", "history", "x0", "xc", "psum", "tanh", "a_squared", "one_minus_a2", "root", "h",
                                      "gelu", "z", "hi", "lo"))
        m_mrg, m_hi, m_lo = sem("merged"), sem("merged_hi"), sem("merged_lo")
        f_fix, f_c0, f_conv, f_gelu, f_hi, f_lo = (
            sem(f"ffn_{x}") for x in ("history", "c0", "conv", "gelu", "hi", "lo"))
        s_out = sem("outputs_stored")
        s_own = [sem(f"own_{x}") for x in ("pool", "pe", "act")]

        block = ctx.enter_context(nc.Block())
        NB = NC + 1
        STG = 3 * NC + 5
        GEN = NC - 4

        @block.sync
        def _(sp):
            for k in range(KT):
                sp.dma_start(resid[:, k, :], xT[k]).then_inc(s_x[k], 16)
                if k == 0:
                    sp.dma_start(vec[:, :], vecs).then_inc(s_vec, 16)
                    sp.dma_start(mat[:, :, :], mats).then_inc(s_vec, 16)
            sp.dma_start(w_raw[0][:, :], W[0]).then_inc(wx_loaded, 16)
            sp.dma_start(w_raw[1][:, :], W[1]).then_inc(wy_loaded, 16)
            sp.wait_ge(n_acc, KT)
            sp.dma_start(kcs[:, :, :], kc).then_inc(s_cache, 16)
            sp.dma_start(vcs[:, :, :], vc).then_inc(s_cache, 16)
            with sp.Fori(0, NPAIR - 1) as i:
                for s, (done, loaded) in enumerate(((x_done, wx_loaded), (y_done, wy_loaded))):
                    sp.wait_ge(done, i * 3 + 3)
                    sp.dma_start(w_raw[s][:, :], W[bass.ds(i * 2 + (2 + s), 1)].rearrange("a p n -> (a p) n")).then_inc(loaded, 16)
            sp.wait_ge(r_lo, START + 3 * KT)
            sp.dma_start(o_lconv, st_lconv[:, :, :, :]).then_inc(s_out, 16)
            sp.dma_start(o_h, st_h[:, :, :]).then_inc(s_out, 16)
            sp.wait_ge(f_lo, 3 * FT)
            sp.dma_start(o_fconv, st_fconv[:, :, :, :]).then_inc(s_out, 16)
            for k in range(KT):
                sp.wait_ge(x_dve if k % 2 == 0 else y_dve, (X_END if k % 2 == 0 else Y_END) - 3 * (KT // 2 - 1 - k // 2))
                sp.dma_start(yT[k], resid[:, k, :]).then_inc(s_out, 16)
            sp.wait_ge(s_out, 16 * (8 + 3 + KT))

        @block.gpsimd
        def _(pool):
            def split(p, slots=(0, 1)):
                for s in slots:
                    loaded, ready = ((wx_loaded, wx_ready), (wy_loaded, wy_ready))[s]
                    pool.wait_ge(loaded, p * 16 + 16)
                    if not isinstance(p, int):
                        pool.sem_inc(s_own[0], 1)
                    nc.gpsimd.tensor_scalar(w_hi[s][:, :], w_raw[s][:, :], 1.0, 0.0, ALU.mult, ALU.add).then_inc(w_hi_done, 1)
                    pool.wait_ge(w_hi_done, p * 2 + (s + 1))
                    nc.gpsimd.tensor_tensor(w_lo[s][:, :], w_raw[s][:, :], w_hi[s][:, :].bitcast(F32), ALU.subtract).then_inc(ready, 1)

            def norm(which):
                for n, (c0, cn) in enumerate(CHUNKS):
                    with pool.Fori(0, 2) as i:
                        for h in range(3):
                            pool.wait_ge(n_hi, i * 4 + (KT * (3 * which + n) + h + 1))
                            pool.sem_inc(s_own[0], 1)
                            nc.gpsimd.tensor_tensor(row(x_lo, i * 4 + h, c0, cn), ntmp[h][:, 0:cn],
                                                    row(x_hi, i * 4 + h, c0, cn).bitcast(F32), ALU.subtract).then_inc(n_lop, 1)

            def stage_qk(s, q0, k0, keys):
                nc.gpsimd.tensor_copy(qs[s][:, :, :], qT[:, :, cols(q0, CHUNK)]).then_inc(a_stg, 1)
                nc.gpsimd.tensor_copy(ks[s][:, 0:keys], kG[:, cols(k0, keys)]).then_inc(a_stg, 1)

            def stage_v(s, k0, keys):
                nc.gpsimd.tensor_copy(vs[s][:, 0:keys], vT[:, cols(k0, keys)]).then_inc(a_stg, 1)

            pool.sem_inc(n_lop, START)
            for a in range(2):
                B0, p0 = NB * a, ATT_PAIRS * a
                if a == 0:
                    split(0)
                    norm(0)
                for p in range(p0 + 1, p0 + ATT_PAIRS):
                    split(p)
                pool.wait_ge(k_rdy, a + 1)
                pool.wait_ge(x_act, 3 * (p0 + ATT_PAIRS))
                pool.wait_ge(y_act, 3 * (p0 + ATT_PAIRS - 1))
                for b in range(2):
                    stage_qk(b, b * CHUNK, 0, (b + 1) * CHUNK)
                split(p0 + ATT_PAIRS, (0,))
                pool.wait_ge(y_act, 3 * (p0 + ATT_PAIRS) - 2)
                for b in range(2):
                    stage_v(b, 0, (b + 1) * CHUNK)
                pool.wait_ge(y_act, 3 * (p0 + ATT_PAIRS))
                with pool.Fori(0, (NC - 2) // 2) as i:
                    for s in range(2):
                        k0 = i * (2 * CHUNK) + s * CHUNK
                        pool.wait_ge(a_S, i * 2 + (B0 + 1 + s))
                        stage_qk(s, k0 + 2 * CHUNK, k0, 3 * CHUNK)
                        pool.wait_ge(a_T, i * 2 + (B0 + 1 + s))
                        stage_v(s, k0, 3 * CHUNK)
                pool.wait_ge(a_T, B0 + NC - 1)
                pool.wait_ge(s_cache, 32)
                nc.gpsimd.tensor_copy(qs[0][:, 0:2, :].rearrange("p a b -> p (a b)").rearrange("p (a b) -> p a b", b=DSEQ),
                                      qT[:, :, SMP:T]).then_inc(a_stg, 1)
                nc.gpsimd.tensor_scalar(ks[0][:, 0:WIN], kcs[:, a, :], V("g_q"), 0.0, ALU.mult, ALU.add).then_inc(a_stg, 1)
                nc.gpsimd.tensor_copy(ks[0][:, WIN:WIN + DSEQ], kG[:, SMP:T]).then_inc(a_stg, 1)
                nc.gpsimd.tensor_copy(vs[0][:, 0:WIN], vcs[:, a, :]).then_inc(a_stg, 1)
                nc.gpsimd.tensor_copy(vs[0][:, WIN:WIN + DSEQ], vT[:, SMP:T]).then_inc(a_stg, 1)
                split(p0 + ATT_PAIRS, (1,))
            with pool.Fori(0, PAIR_F - 2 * ATT_PAIRS) as i:
                split(i + (2 * ATT_PAIRS + 1))
            norm(1)
            with pool.Fori(0, NPAIR - PAIR_F - 1) as i:
                split(i + (PAIR_F + 1))

        @block.tensor
        def _(pe):
            def chunk(s, n, hi, lo, before=None):
                cc, cn = CHUNKS[n]
                for k in range(KT):
                    if before is not None:
                        before(k)
                    for j, (w, x) in enumerate(((w_hi, hi), (w_hi, lo), (w_lo, hi))):
                        last = nc.tensor.matmul(bank[3 * s + n][:, 0:cn], w[s][:, k * P:(k + 1) * P], x[:, k, cc:cc + cn],
                                                start=(k == 0 and j == 0), stop=(k == KT - 1 and j == 2))
                last.then_inc(x_done if s == 0 else y_done, 1)

            def tile(s, i, p0, hi, lo, free=None, freed=None, before=None, after=None):
                pe.wait_ge(wx_ready if s == 0 else wy_ready, i + (p0 + 1))
                for n, (c0, cn) in enumerate(CHUNKS):
                    if free is not None:
                        pe.wait_ge(free, freed + (n - 2))
                    chunk(s, n, hi, lo, None if before is None else lambda k: before(n, k))
                    if after is not None:
                        after(n)

            def loop_tiles(p0, trips, hix, lox, hiy, loy, fx, x0, fy, y0):
                with pe.Fori(0, trips) as i:
                    tile(0, i, p0, hix, lox, fx, i * 3 + x0)
                    tile(1, i, p0, hiy, loy, fy, i * 3 + y0)

            def last_row(sem_, value):
                def before(n, k):
                    if k == KT - 1:
                        pe.wait_ge(sem_, value + (n + 1))
                return before

            def normed(which):
                def before(n, k):
                    if k % 4 == 0:
                        groups = 2 * (3 * which + n) + k // 4 + 1
                        pe.wait_ge(n_lo, START + groups)
                        pe.wait_ge(n_lop, START + 3 * groups)
                return before

            def norm_sums(which):
                pe.wait_ge(n_acc, KT * (3 * which + 1))
                for b, (n, off) in enumerate(NORM_BLOCKS):
                    c0 = CHUNKS[n][0] + off
                    last = nc.tensor.matmul(bank[7][:, 2 * b:2 * b + 2], nacc[:, c0:c0 + P], ones[:, 0:2], start=True, stop=True)
                last.then_inc(n_ps, 1)
                for b, (n, off) in enumerate(NORM_BLOCKS):
                    if b % 3 == 0:
                        pe.wait_ge(n_dg, 3 * which + n + 1)
                    last = nc.tensor.matmul(bank[5 + n][:, off:off + P], ones, dg[:, b, :], start=True, stop=True)
                    if b % 3 == 2:
                        last.then_inc(n_bc, 1)

            pe.wait_ge(s_vec, 32)
            norm_sums(0)

            for a in range(2):
                p0, B0, G0 = ATT_PAIRS * a, NB * a, STG * a
                def scores(b, s, keys, units, staged, first=False):
                    pe.wait_ge(a_stg, staged)
                    if not first:
                        pe.wait_ge(a_exp, b)
                    for e in range(2):
                        for u in range(units):
                            v = units * e + u
                            last = nc.tensor.matmul(bank[2 * s + v // 2][:, (v % 2) * 192:(v % 2) * 192 + keys],
                                                    qs[s][64 * e:64 * e + 64, 2 * u:2 * u + 2, :], ks[s][64 * e:64 * e + 64, 0:keys],
                                                    start=True, stop=True)
                    last.then_inc(a_S, 1)

                def groups_of(keys):
                    return [(0, min(keys, P))] + ([(P, keys - P)] if keys > P else [])

                def transposes(b, s, keys, units, staged):
                    groups = groups_of(keys)
                    pe.wait_ge(a_stg, staged)
                    pe.wait_ge(a_evv, b)
                    pe.wait_ge(a_ev, b)
                    for g, (k0, kn) in enumerate(groups):
                        nc.tensor.transpose(bank[6][0:kn, g * P:g * P + P], vs[s][:, k0:k0 + kn], ident)
                    pe.wait_ge(a_nrm, b + 1)
                    for g, (k0, kn) in enumerate(groups):
                        for v in range(2 * units):
                            last = nc.tensor.transpose(bank[4 + g][0:kn, v * P:v * P + P], pr[s][:, v, k0:k0 + kn], ident)
                    last.then_inc(a_T, 1)

                def product(b, keys, units):
                    groups = groups_of(keys)
                    pe.wait_ge(a_ev, b + 1)
                    pe.wait_ge(a_evv, b + 1)
                    pe.wait_ge(a_lo, b)
                    rows = units * P
                    for e in range(2):
                        for g, (k0, kn) in enumerate(groups):
                            last = nc.tensor.matmul(bank[7][64 * e:64 * e + 64, 0:rows], vt[g][0:kn, 64 * e:64 * e + 64],
                                                    pt[g][0:kn, e * rows:e * rows + rows], start=(g == 0), stop=(g == len(groups) - 1))
                    last.then_inc(a_O, 1)

                if a == 0:
                    tile(0, 0, p0, x_hi, x_lo, before=normed(0))
                else:
                    pe.wait_ge(a_lo, B0)
                def k_sums(n):
                    c0, cn = CHUNKS[n]
                    pe.wait_ge(x_act, 3 * p0 + n + 1)
                    if n == 2:
                        pe.wait_ge(k_rt, 3 * a + 1)
                    nc.tensor.matmul(bank[6 + n % 2][:, 0:cn], bones, kG[:, c0:c0 + cn], start=True, stop=True).then_inc(k_ps, 1)
                tile(1, 0, p0, x_hi, x_lo, after=k_sums)
                tile(0, 0, p0 + 1, x_hi, x_lo, x_act, 3 * p0 + 3)
                tile(1, 0, p0 + 1, x_hi, x_lo, y_act, 3 * p0 + 3)
                tile(0, 0, p0 + 2, x_hi, x_lo, x_act, 3 * p0 + 6)

                def beside_v(n):
                    if n == 0:
                        pe.wait_ge(q_sq, 4 * (a + 1))
                        pe.wait_ge(k_rt, 3 * (a + 1))
                        for c in range(NC):
                            for u in range(2):
                                nc.tensor.matmul(bank[7][:, 4 * c + u:4 * c + u + 3:2], q2[:, c, 2 * u * CHUNK:2 * (u + 1) * CHUNK],
                                                 bones[:, HD - 1:HD + 1], start=True, stop=True)
                        nc.tensor.matmul(bank[7][:, 4 * NC:4 * NC + 2], q2[:, NC, 0:4 * DSEQ], bones[:, HD - 1:HD + 1],
                                         start=True, stop=True).then_inc(q_ps, 1)
                    elif n == 1:
                        scores(0, 0, CHUNK, 2, G0 + 2, True)
                    else:
                        pe.wait_ge(y_act, 3 * p0 + 7)
                        scores(0, 1, 2 * CHUNK, 2, G0 + 4, True)

                tile(1, 0, p0 + 2, x_hi, x_lo, y_act, 3 * p0 + 6, after=beside_v)
                pe.wait_ge(y_act, 3 * p0 + 9)
                pe.wait_ge(q_rt, a + 1)

                for l in range(2):
                    transposes(B0 + l, l, (l + 1) * CHUNK, 2, G0 + 5 + l)
                    scores(B0 + l + 1, l, 3 * CHUNK, 2, G0 + 8 + 3 * l)
                    product(B0 + l, (l + 1) * CHUNK, 2)
                with pe.Fori(0, GEN // 2) as i:
                    for s in range(2):
                        transposes(i * 2 + (B0 + 2 + s), s, 3 * CHUNK, 2, i * 6 + (G0 + 9 + 3 * s))
                        scores(i * 2 + (B0 + 3 + s), s, 3 * CHUNK, 2, i * 6 + (G0 + 14 + 3 * s))
                        product(i * 2 + (B0 + 2 + s), 3 * CHUNK, 2)
                transposes(B0 + NC - 2, 0, 3 * CHUNK, 2, G0 + 3 * NC - 3)
                pe.wait_ge(a_stg, G0 + STG - 2)
                for e in range(2):
                    last = nc.tensor.matmul(bank[e][:, 0:WIN + DSEQ], qs[0][64 * e:64 * e + 64, 0:2, :],
                                            ks[0][64 * e:64 * e + 64, 0:WIN + DSEQ], start=True, stop=True)
                last.then_inc(a_S, 1)
                product(B0 + NC - 2, 3 * CHUNK, 2)
                transposes(B0 + NC - 1, 1, 3 * CHUNK, 2, G0 + 3 * NC)

                def last_blocks(n):
                    if n == 0:
                        product(B0 + NC - 1, 3 * CHUNK, 2)
                        transposes(B0 + NC, 0, WIN + DSEQ, 1, G0 + STG)
                    elif n == 1:
                        product(B0 + NC, WIN + DSEQ, 1)

                pe.wait_ge(a_exp, B0 + NB)
                tile(0, 0, p0 + ATT_PAIRS, x_hi, x_lo, after=last_blocks)

            pe.wait_ge(a_lo, 2 * NB)
            def gated(p0, stage, between=None, second=None, before=None):
                xa, ya, xd = X_ACT[stage], Y_ACT[stage], X_DVE[stage]
                if stage != "G1":
                    tile(0, 0, p0, x_hi, x_lo, x_act, xa)
                if between is not None:
                    between()
                tile(1, 0, p0, x_hi, x_lo, y_act, ya, before=second)
                pe.wait_ge(x_act, xa + 3)
                if before is not None:
                    pe.wait_ge(r_lo, START + 3 * (KT - 1))
                tile(0, 0, p0 + 1, c_hi, d_lo, before=before)
                tile(1, 0, p0 + 1, x_hi, x_lo, y_act, ya + 3)
                with pe.Fori(0, KT - 3) as i:
                    tile(0, i, p0 + 2, c_hi, d_lo, x_dve, i * 3 + (xd + 3))
                    tile(1, i, p0 + 2, x_hi, x_lo, y_act, i * 3 + (ya + 6))
                tile(0, 0, p0 + KT - 1, c_hi, d_lo, x_dve, xd + 3 * (KT - 2))
                tile(1, 0, p0 + KT - 1, c_hi, d_lo, y_act, ya + 3 * (KT - 1))

            gated(PAIR_G1, "G1")

            def lru_gates(j, n):
                cn = CHUNKS[n][1]
                pe.wait_ge(r_xc, j * 3 + (n + 1))
                pe.wait_ge(r_tanh, j * 3 + (START + n))
                nc.tensor.matmul(bank[6][:, 0:cn], wabs[:, 0, :], XC[n][:, 0:cn], start=True, stop=True)
                nc.tensor.matmul(bank[7][:, 0:cn], wabs[:, 1, :], XC[n][:, 0:cn], start=True, stop=True).then_inc(r_ps, 1)

            tile(0, 0, PAIR_R, x_hi, x_lo, x_dve, X_DVE["G0"])
            tile(1, 0, PAIR_R, x_hi, x_lo, y_dve, Y_DVE["G0"])
            with pe.Fori(0, KT - 1) as j:
                tile(0, j, PAIR_R + 1, x_hi, x_lo, x_act, j * 3 + (X_ACT["R"] + 3))
                pe.wait_ge(s_wab, j * 16 + 16)
                lru_gates(j, 0)
                tile(1, j, PAIR_R + 1, x_hi, x_lo, y_act, j * 3 + (Y_ACT["R"] + 3), after=lambda n: n < 2 and lru_gates(j, n + 1))

            def gates_first():
                pe.wait_ge(s_wab, 16 * KT)
                lru_gates(KT - 1, 0)

            def gates_later(n, k):
                if (n, k) in ((0, KT // 2), (1, 0)):
                    lru_gates(KT - 1, n + 1)

            gated(PAIR_G0, "G0", gates_first, gates_later, last_row(r_lo, START + 3 * (KT - 1)))

            pe.wait_ge(m_lo, KT - 1)
            tile(0, 0, PAIR_O, x_hi, x_lo, x_dve, X_DVE["O"], before=last_row(m_lo, KT - 1))
            tile(1, 0, PAIR_O, x_hi, x_lo, y_dve, Y_DVE["O"])
            loop_tiles(PAIR_O + 1, KT // 2 - 1, x_hi, x_lo, x_hi, x_lo, x_dve, X_DVE["O"] + 3, y_dve, Y_DVE["O"] + 3)
            norm_sums(1)

            with pe.Fori(0, FFN_PARTS) as f:
                pe.wait_ge(x_dve, f * DOWN + X_DVE["F"])
                pe.sem_inc(s_own[1], 1)
                with pe.Fori(0, KT) as j:
                    pair = f * PAIRS_PER_PART + j
                    tile(0, pair, PAIR_F, x_hi, x_lo, x_act, f * UP + j * 3 + X_ACT["F"], before=normed(1))
                    tile(1, pair, PAIR_F, x_hi, x_lo, y_dve, f * (UP + DOWN) + j * 3 + Y_DVE["F"])
                pe.wait_ge(f_lo, f * (3 * KT) + 3 * (KT - 1))
                pe.wait_ge(x_act, f * UP + (X_ACT["F"] + UP))
                pe.sem_inc(s_own[1], 1)
                with pe.Fori(0, KT // 2) as j:
                    pair = f * PAIRS_PER_PART + j
                    tile(0, pair, PAIR_F + KT, act_hi, act_lo, x_dve, f * DOWN + j * 3 + X_DVE["F"],
                         before=last_row(f_lo, f * (3 * KT) + 3 * (KT - 1)))
                    tile(1, pair, PAIR_F + KT, act_hi, act_lo, y_dve, f * (UP + DOWN) + j * 3 + (Y_DVE["F"] + UP))

        @block.scalar
        def _(act):
            A = nc.scalar.activation

            def wait(sem_, value):
                act.wait_ge(sem_, value)
                act.sem_inc(s_own[2], 1)

            def norm(which):
                A(warm[:, :], epsc[:, 0:1], ACT.Sqrt)
                act.wait_ge(n_ps, which + 1)
                A(nst[:, 0, :], bank[7][:, 0:2 * len(NORM_BLOCKS)], ACT.Sqrt, bias=epsc[:, 0:1], scale=1.0 / DM).then_inc(n_rt, 1)
                for n, (c0, cn) in enumerate(CHUNKS):
                    with act.Fori(0, 2) as i:
                        for h in range(4):
                            wait(n_f32, i * 4 + (KT * (3 * which + n) + h + 1))
                            A(row(x_hi, i * 4 + h, c0, cn), ntmp[h][:, 0:cn], ACT.Copy).then_inc(n_hi, 1)

            act.sem_inc(r_tanh, START)
            for k in range(KT):
                act.wait_ge(s_x[k], 16)
                A(merged[:, k, :], resid[:, k, :], ACT.Square).then_inc(n_sq, 1)
            act.wait_ge(s_eps, 1)
            norm(0)
            act.wait_ge(s_vec, 32)
            A(halfb[:, 0:2 * KT], V("bg_lru", 0, 2 * KT), ACT.Copy, scale=0.5)
            A(halfb[:, 2 * KT:4 * KT], V("b_a", 0, 2 * KT), ACT.Copy, scale=0.5)
            A(lam_t[:, 0, :], V("lam", 0, KT), ACT.Abs).then_inc(act_c, 1)
            act.wait_ge(act_c, 1)
            A(lam_t[:, 1, :], lam_t[:, 0, :], ACT.Exp, scale=-1.0).then_inc(s_exp_lam, 1)

            for a in range(2):
                p0, B0 = ATT_PAIRS * a, NB * a
                if a:
                    act.wait_ge(s_out, 16 * 4)
                for n, (c0, cn) in enumerate(CHUNKS):
                    act.wait_ge(x_done, 3 * p0 + n + 1)
                    A(kN[:, c0:c0 + cn], bank[n][:, 0:cn], ACT.Copy)
                    A(kG[:, c0:c0 + cn], bank[n][:, 0:cn], ACT.Square).then_inc(x_act, 1)

                def q_out(r_):
                    pair = p0 + (r_ + 1) // 2
                    s, done, free = (1, y_done, y_act) if r_ % 2 == 0 else (0, x_done, x_act)
                    for n, (c0, cn) in enumerate(CHUNKS):
                        act.wait_ge(done, 3 * pair + n + 1)
                        A(qT[:, r_, c0:c0 + cn], bank[3 * s + n][:, 0:cn], ACT.Copy).then_inc(free, 1)
                    act.wait_ge(free, 3 * pair + 3)
                    A(q2[:, 0:NC, r_ * CHUNK:(r_ + 1) * CHUNK], qT[:, r_, 0:SEQ].rearrange("p (c n) -> p c n", n=CHUNK), ACT.Square)
                    A(q2[:, NC, r_ * DSEQ:(r_ + 1) * DSEQ], qT[:, r_, SMP:T], ACT.Square).then_inc(q_sq, 1)

                def v_out(n):
                    c0, cn = CHUNKS[n]
                    act.wait_ge(y_done, 3 * (p0 + 2) + n + 1)
                    A(vT[:, c0:c0 + cn], bank[3 + n][:, 0:cn], ACT.Copy).then_inc(y_act, 1)

                q_out(0)
                for n, (c0, cn) in enumerate(CHUNKS):
                    act.wait_ge(k_ps, 3 * a + n + 1)
                    A(nrs[:, c0:c0 + cn], bank[6 + n % 2][:, 0:cn], ACT.Sqrt, bias=epsc[:, 0:1], scale=1.0 / HD).then_inc(k_rt, 1)
                for r_ in range(1, 4):
                    q_out(r_)
                v_out(0)
                act.wait_ge(q_ps, a + 1)
                A(rq[:, :], bank[7][:, 0:4 * NC + 2], ACT.Sqrt, bias=epsc[:, 1:2]).then_inc(q_rt, 1)

                def exps(b, s, keys, nu):
                    act.wait_ge(a_stat, b + 1)
                    sm = small[s]
                    A(sm[:, 4, 0:nu], sm[:, 3, 0:nu], ACT.Exp)
                    for v in range(nu):
                        b_, c_ = (2 * s + v // 2, v % 2 * 192) if nu == 4 else (v, 0)
                        last = A(pr[s][:, v, 0:keys], bank[b_][:, c_:c_ + keys], ACT.Exp,
                                 bias=sm[:, 2, v:v + 1], scale=sm[:, 1, v:v + 1], accum_out=sm[:, 5, v:v + 1])
                    last.then_inc(a_exp, 1)

                def evac(b, keys, nu):
                    act.wait_ge(a_T, b + 1)
                    act.wait_ge(a_O, b)
                    kn = min(keys, P)
                    A(pt[0][0:kn, 0:nu * P], bank[4][0:kn, 0:nu * P], ACT.Copy).then_inc(a_ev, 1)

                def hi(b, c0, cn):
                    wait(a_O, b + 1)
                    A(c_hi[:, 4 * a:4 * a + 4, cols(c0, cn)], bank[7][:, 0:4 * cn].rearrange("p (a b) -> p a b", b=cn),
                      ACT.Copy).then_inc(a_hi, 1)

                v_out(1)
                exps(B0, 0, CHUNK, 4)
                v_out(2)
                exps(B0 + 1, 1, 2 * CHUNK, 4)
                act.wait_ge(k_rdy, a + 1)
                act.wait_ge(y_act, 3 * (p0 + 3))
                act.dma_start(o_kp[a], kN[:, SEQ - WIN:SEQ]).then_inc(s_out, 16)
                act.dma_start(o_ks[a], kN[:, SMP:T]).then_inc(s_out, 16)
                act.dma_start(o_vp[a], vT[:, SEQ - WIN:SEQ]).then_inc(s_out, 16)
                act.dma_start(o_vs[a], vT[:, SMP:T]).then_inc(s_out, 16)
                for l in range(2):
                    evac(B0 + l, (l + 1) * CHUNK, 4)
                    hi(B0 + l, l * CHUNK, CHUNK)
                    exps(B0 + 2 + l, l, 3 * CHUNK, 4)
                with act.Fori(0, GEN // 2) as i:
                    for s in range(2):
                        evac(i * 2 + (B0 + 2 + s), 3 * CHUNK, 4)
                        hi(i * 2 + (B0 + 2 + s), i * (2 * CHUNK) + (2 + s) * CHUNK, CHUNK)
                        exps(i * 2 + (B0 + 4 + s), s, 3 * CHUNK, 4)
                evac(B0 + NC - 2, 3 * CHUNK, 4)
                hi(B0 + NC - 2, SEQ - 2 * CHUNK, CHUNK)
                exps(B0 + NC, 0, WIN + DSEQ, 2)
                evac(B0 + NC - 1, 3 * CHUNK, 4)
                hi(B0 + NC - 1, SEQ - CHUNK, CHUNK)
                evac(B0 + NC, WIN + DSEQ, 2)
                hi(B0 + NC, SMP, DSEQ)

            def first_gate(p0, half0):
                for n, (c0, cn) in enumerate(CHUNKS):
                    act.wait_ge(x_done, 3 * p0 + n + 1)
                    A(GG[n][:, 0:cn], bank[n][:, 0:cn], ACT.Tanh, bias=halfb[:, half0:half0 + 1], scale=0.5).then_inc(x_act, 1)

            def gates(p0, half0, stage):
                with act.Fori(0, KT - 1) as i:
                    for n, (c0, cn) in enumerate(CHUNKS):
                        wait(y_done, i * 3 + (3 * p0 + n + 1))
                        wait(x_dve, i * 3 + (X_DVE[stage] + n + 1))
                        A(GG[n][:, 0:cn], bank[3 + n][:, 0:cn], ACT.Tanh, bias=halfb[:, bass.ds(i + (half0 + 1), 1)],
                          scale=0.5).then_inc(y_act, 1)

            first_gate(PAIR_G1, KT)
            gates(PAIR_G1, KT, "G1")

            def load_wab(j):
                src = wab[j] if isinstance(j, int) else wab[bass.ds(j, 1)].rearrange("a p m n -> (a p) m n")
                act.dma_start(wabs[:, :, :], src).then_inc(s_wab, 16)

            def lru_u(j):
                for n, (c0, cn) in enumerate(CHUNKS):
                    wait(x_done, j * 3 + (3 * PAIR_R + n + 1))
                    A(U[:, LRU_HIST + c0:LRU_HIST + c0 + cn], bank[n][:, 0:cn], ACT.Copy).then_inc(x_act, 1)

            def lru_x0(j):
                wait(r_fix, j + 1)
                for n, (c0, cn) in enumerate(CHUNKS):
                    A(XC[n][:, 0:cn], U[:, LRU_HIST + c0:LRU_HIST + c0 + cn], ACT.Identity,
                      bias=VD("conv_b", j), scale=VD("conv_w", j * 4 + 3)).then_inc(r_x0, 1)

            def lru_decay(j):
                for n, (c0, cn) in enumerate(CHUNKS):
                    ck = slice(c0, c0 + cn)
                    wait(r_ps, j * 3 + (n + 1))
                    A(FA[:, ck], bank[6][:, 0:cn], ACT.Tanh, bias=halfb[:, cols(j + 2 * KT, 1)], scale=0.5)
                    A(FI[:, ck], bank[7][:, 0:cn], ACT.Tanh, bias=halfb[:, cols(j + 3 * KT, 1)], scale=0.5).then_inc(r_tanh, 1)
                    wait(r_tanh, j * 3 + (START + n + 1))
                    A(row(resid, j, c0, cn), FA[:, ck], ACT.Tanh, bias=lamc[:, 0, cols(j, 1)], scale=lamc[:, 0, cols(j, 1)])
                    A(FA[:, ck], FA[:, ck], ACT.Exp, bias=lamc[:, 1, cols(j, 1)], scale=lamc[:, 1, cols(j, 1)]).then_inc(act_c, 1)
                    wait(act_c, j * 3 + (n + 2))
                    A(FS[:, ck], FA[:, ck], ACT.Square).then_inc(r_sqa, 1)

            def lru_root(j):
                act.wait_ge(r_om, j * 3 + 3)
                A(FS[:, :], FS[:, :], ACT.Sqrt, scale=0.25).then_inc(r_root, 1)

            def lru_gelu(j):
                for n, (c0, cn) in enumerate(CHUNKS):
                    wait(y_done, j * 3 + (3 * PAIR_R + n + 1))
                    A(row(sqsum, j, c0, cn), bank[3 + n][:, 0:cn], ACT.Gelu_apprx_tanh).then_inc(y_act, 1)

            def lru_hi(j):
                for n, (c0, cn) in enumerate(CHUNKS):
                    wait(r_z, j * 3 + (n + 1))
                    A(row(c_hi, j, c0, cn), FA[:, c0:c0 + cn], ACT.Copy).then_inc(r_hi, 1)

            load_wab(0)
            act.wait_ge(y_dve, Y_DVE["G0"])
            act.wait_ge(s_lamc, 1)
            lru_u(0)
            lru_x0(0)
            lru_gelu(0)
            with act.Fori(0, KT - 1) as j:
                wait(r_xc, j * 3 + 3)
                lru_u(j + 1)
                wait(r_lo, j * 3 + START)
                lru_decay(j)
                load_wab(j + 1)
                lru_root(j)
                lru_x0(j + 1)
                lru_gelu(j + 1)
                lru_hi(j)
            act.wait_ge(r_xc, 3 * KT)
            first_gate(PAIR_G0, 0)
            act.wait_ge(r_lo, START + 3 * (KT - 1))
            lru_decay(KT - 1)
            lru_root(KT - 1)
            lru_hi(KT - 1)

            gates(PAIR_G0, 0, "G0")

            with act.Fori(0, KT - 1) as k:
                wait(m_mrg, k * 3 + 3)
                A(row(x_hi, k, 0, T), row(merged, k, 0, T), ACT.Copy, scale=0.5).then_inc(m_hi, 1)
            for n, (c0, cn) in enumerate(CHUNKS):
                act.wait_ge(m_mrg, 3 * (KT - 1) + n + 1)
                A(row(x_hi, KT - 1, c0, cn), row(merged, KT - 1, c0, cn), ACT.Copy, scale=0.5).then_inc(m_hi, 1)
            act.wait_ge(y_done, 3 * PAIR_O)
            for h in range(2):
                kk = slice(h * KT // 2, (h + 1) * KT // 2)
                act.dma_start(sqsum[:, kk, :], xT[kk].rearrange("k p n -> p k n")).then_inc(s_xres[h], 16)
            act.wait_ge(m_lo, KT + 2)
            with act.Fori(0, KT // 2) as i:
                for s, (free, freed) in enumerate(((x_dve, X_DVE), (y_dve, Y_DVE))):
                    for n, (c0, cn) in enumerate(CHUNKS):
                        wait(free, i * 3 + (freed["O"] + n + 1))
                        A(row(merged, i * 2 + s, c0, cn), row(resid, i * 2 + s, c0, cn), ACT.Square).then_inc(n_sq, 1)
            norm(1)

            with act.Fori(0, FFN_PARTS) as f:
                with act.Fori(0, KT) as j:
                    p3 = f * (3 * PAIRS_PER_PART) + j * 3
                    used = f * (UP + DOWN) + j * 3 + Y_DVE["F"]
                    ft = f * KT + j
                    for n, (c0, cn) in enumerate(CHUNKS):
                        act.wait_ge(x_done, p3 + (3 * PAIR_F + n + 1))
                        A(GB[:, FFN_HIST + c0:FFN_HIST + c0 + cn], bank[n][:, 0:cn], ACT.Copy).then_inc(x_act, 1)
                    wait(f_fix, ft + 1)
                    for n, (c0, cn) in enumerate(CHUNKS):
                        wait(y_dve, used + (n - 2))
                        A(GC[n][:, 0:cn], GB[:, FFN_HIST + c0:FFN_HIST + c0 + cn], ACT.Identity,
                          bias=VD("fconv_b", ft), scale=VD("fconv_w", ft * 3 + 2)).then_inc(f_c0, 1)
                    for n, (c0, cn) in enumerate(CHUNKS):
                        wait(f_conv, ft * 3 + (n + 1))
                        A(GC[n][:, 0:cn], GC[n][:, 0:cn], ACT.Gelu_apprx_tanh).then_inc(f_gelu, 1)
                    for n, (c0, cn) in enumerate(CHUNKS):
                        wait(y_dve, used + (n + 1))
                        A(row(act_hi, j, c0, cn), GV[n][:, 0:cn], ACT.Copy).then_inc(f_hi, 1)

        @block.vector
        def _(dve):
            D = nc.vector
            ch = Count(dve_c)

            def link(ins):
                ch.inc(ins)
                dve.wait_ge(dve_c, ch.value())

            def norm(which):
                g = "g_ffn" if which else "g_mix"
                root, y, m, t = (nst[:, i, :] for i in range(4))
                dve.wait_ge(n_rt, which + 1)
                link(D.reciprocal(y, root))
                D.tensor_scalar(m, bank[7][:, 0:2 * len(NORM_BLOCKS)], -0.5 / DM, -0.5 * EPS, ALU.mult, ALU.add)
                link(D.tensor_tensor(t, y, y, ALU.mult))
                link(D.tensor_tensor(t, t, m, ALU.mult))
                link(D.scalar_tensor_tensor(y, t, 1.5, y, ALU.add, ALU.mult))
                for b, (n, off) in enumerate(NORM_BLOCKS):
                    last = D.tensor_scalar(dg[:, b, :], ident, y[:, 2 * b:2 * b + 1], None, ALU.mult)
                    if b % 3 == 2:
                        last.then_inc(n_dg, 1)
                for n, (c0, cn) in enumerate(CHUNKS):
                    dve.wait_ge(n_bc, 3 * which + n + 1)
                    with dve.Fori(0, 2) as i:
                        groups = 2 * (3 * which + n)
                        for h in range(4):
                            if h < 3:
                                dve.wait_ge(n_lop, i * 3 + (START + 3 * groups + h - 2))
                            else:
                                dve.wait_ge(n_lo, i + (START + groups))
                            D.scalar_tensor_tensor(ntmp[h][:, 0:cn], row(resid, i * 4 + h, c0, cn), VD(g, i * 4 + h),
                                                   bank[5 + n][:, 0:cn], ALU.mult, ALU.mult).then_inc(n_f32, 1)
                        dve.wait_ge(n_hi, i * 4 + (4 * groups + 4))
                        D.tensor_tensor(row(x_lo, i * 4 + 3, c0, cn), ntmp[3][:, 0:cn],
                                        row(x_hi, i * 4 + 3, c0, cn).bitcast(F32), ALU.subtract).then_inc(n_lo, 1)

            dve.sem_inc(x_dve, 3)
            dve.sem_inc(y_dve, 3)
            dve.sem_inc(n_lo, START)
            dve.sem_inc(r_lo, START)
            D.memset(epsc[:, 0:1], EPS)
            D.memset(epsc[:, 1:2], HD * EPS).then_inc(s_eps, 1)
            link(D.memset(nacc[:, :], 0.0))
            for k in range(KT):
                dve.wait_ge(n_sq, k + 1)
                if k:
                    dve.wait_ge(n_acc, k)
                D.tensor_tensor(nacc[:, :], nacc[:, :], merged[:, k, :], ALU.add).then_inc(n_acc, 1)
            norm(0)
            dve.wait_ge(s_exp_lam, 1)
            e, s_, s2, ac = (lam_t[:, i, :] for i in (1, 2, 3, 4))
            link(D.tensor_scalar(s2, e, 2.0, None, ALU.add))
            link(D.reciprocal(s2, s2))
            link(D.tensor_tensor(s_, e, s2, ALU.mult))
            link(D.tensor_tensor(s2, s_, s_, ALU.mult))
            link(D.memset(ac, 1.0 / 19))
            for m in range(17, 0, -2):
                link(D.tensor_tensor(ac, ac, s2, ALU.mult))
                link(D.tensor_scalar(ac, ac, 1.0 / m, None, ALU.add))
            link(D.tensor_tensor(ac, ac, s_, ALU.mult))
            link(D.tensor_scalar(s2, V("lam", 0, KT), -1.0, 0.0, ALU.mult, ALU.max))
            link(D.scalar_tensor_tensor(ac, ac, 2.0, s2, ALU.mult, ALU.add))
            D.tensor_scalar(lamc[:, 0, :], ac, 4.0, None, ALU.mult)
            D.tensor_scalar(lamc[:, 1, :], ac, -4.0, None, ALU.mult).then_inc(s_lamc, 1)
            link(D.tensor_scalar(negsink[:, :], V("sink_p", 0, 12), -1.0, None, ALU.mult))

            for a in range(2):
                p0, B0 = ATT_PAIRS * a, NB * a
                for n, (c0, cn) in enumerate(CHUNKS):
                    ck = slice(c0, c0 + cn)
                    dve.wait_ge(k_rt, 3 * a + n + 1)
                    link(D.reciprocal(nrs[:, ck], nrs[:, ck]))
                    link(D.scalar_tensor_tensor(kN[:, ck], kN[:, ck], V("g_k"), nrs[:, ck], ALU.mult, ALU.mult))
                    last = D.tensor_scalar(kG[:, ck], kN[:, ck], V("g_q"), None, ALU.mult)
                last.then_inc(k_rdy, 1)
                dve.wait_ge(q_rt, a + 1)
                link(D.reciprocal(rq[:, :], rq[:, :]))
                link(D.tensor_scalar(nrq[:, :], rq[:, :], -1.0, None, ALU.mult))
                for t in (c_hi, d_lo):
                    D.memset(t[:, 4 * a:4 * a + 4, SEQ:SMP].bitcast(F32), 0.0)

                def stats(b, s, keys, nu, r0, sink0):
                    sm = small[s]
                    dve.wait_ge(a_S, b + 1)
                    if nu == 4:
                        src = bankpair[s][:, :, 0:384].rearrange("p b (v k) -> p b v k", v=2)[:, :, :, 0:keys]
                        dst = sm[:, 0, 0:4].rearrange("p (b v) -> p b v", v=2)
                    else:
                        src = bankpair[0][:, :, 0:keys]
                        dst = sm[:, 0, 0:2]
                    D.tensor_copy(sm[:, 1, 0:nu], rq[:, cols(r0, nu)])
                    link(D.tensor_reduce(dst, src, AXX, ALU.max))
                    link(D.tensor_tensor(sm[:, 6, 0:nu], sm[:, 0, 0:nu], nrq[:, cols(r0, nu)], ALU.mult))
                    link(D.tensor_tensor(sm[:, 2, 0:nu], sm[:, 6, 0:nu], negsink[:, sink0:sink0 + nu], ALU.min))
                    D.tensor_tensor(sm[:, 3, 0:nu], sm[:, 2, 0:nu], negsink[:, sink0:sink0 + nu], ALU.subtract).then_inc(a_stat, 1)

                def normalise(b, s, keys, nu):
                    sm = small[s]
                    dve.wait_ge(a_exp, b + 1)
                    link(D.tensor_tensor(sm[:, 7, 0:nu], sm[:, 5, 0:nu], sm[:, 4, 0:nu], ALU.add))
                    link(D.reciprocal(sm[:, 7, 0:nu], sm[:, 7, 0:nu]))
                    for v in range(nu):
                        last = D.tensor_scalar(pr[s][:, v, 0:keys], pr[s][:, v, 0:keys], sm[:, 7, v:v + 1], None, ALU.mult)
                    last.then_inc(a_nrm, 1)

                def evac(b, keys, nu):
                    dve.wait_ge(a_T, b + 1)
                    dve.wait_ge(a_O, b)
                    if keys > P:
                        D.tensor_copy(pt[1][0:keys - P, 0:nu * P], bank[5][0:keys - P, 0:nu * P])
                        D.tensor_copy(vt[1][0:keys - P, :], bank[6][0:keys - P, P:2 * P])
                    kn = min(keys, P)
                    D.tensor_copy(vt[0][0:kn, :], bank[6][0:kn, 0:P]).then_inc(a_evv, 1)

                def lo(b, c0, cn):
                    dve.wait_ge(a_hi, b + 1)
                    D.tensor_tensor(d_lo[:, 4 * a:4 * a + 4, cols(c0, cn)], bank[7][:, 0:4 * cn].rearrange("p (a b) -> p a b", b=cn),
                                    c_hi[:, 4 * a:4 * a + 4, cols(c0, cn)].bitcast(F32), ALU.subtract).then_inc(a_lo, 1)

                stats(B0, 0, CHUNK, 4, 0, 4 * a)
                normalise(B0, 0, CHUNK, 4)
                stats(B0 + 1, 1, 2 * CHUNK, 4, 4, 4 * a)
                for l in range(2):
                    evac(B0 + l, (l + 1) * CHUNK, 4)
                    normalise(B0 + l + 1, 1 - l, (l + 2) * CHUNK, 4)
                    stats(B0 + 2 + l, l, 3 * CHUNK, 4, 4 * (2 + l), 4 * a)
                    lo(B0 + l, l * CHUNK, CHUNK)
                with dve.Fori(0, GEN // 2) as i:
                    ch.enter(i, 2 * 5)
                    for s in range(2):
                        evac(i * 2 + (B0 + 2 + s), 3 * CHUNK, 4)
                        normalise(i * 2 + (B0 + 3 + s), 1 - s, 3 * CHUNK, 4)
                        stats(i * 2 + (B0 + 4 + s), s, 3 * CHUNK, 4, i * 8 + 4 * (4 + s), 4 * a)
                        lo(i * 2 + (B0 + 2 + s), i * (2 * CHUNK) + (2 + s) * CHUNK, CHUNK)
                    ch.leave(GEN // 2)
                evac(B0 + NC - 2, 3 * CHUNK, 4)
                normalise(B0 + NC - 1, 1, 3 * CHUNK, 4)
                stats(B0 + NC, 0, WIN + DSEQ, 2, 4 * NC, 8 + 2 * a)
                lo(B0 + NC - 2, SEQ - 2 * CHUNK, CHUNK)
                evac(B0 + NC - 1, 3 * CHUNK, 4)
                normalise(B0 + NC, 0, WIN + DSEQ, 2)
                lo(B0 + NC - 1, SEQ - CHUNK, CHUNK)
                evac(B0 + NC, WIN + DSEQ, 2)
                lo(B0 + NC, SMP, DSEQ)

            dve.wait_ge(s_out, 16 * 8)
            def joins(p0, stage, join):
                ya = Y_ACT[stage]
                dve.wait_ge(x_act, X_ACT[stage] + 3)
                with dve.Fori(0, KT - 1) as j:
                    for n in range(3):
                        dve.wait_ge(y_act, j * 3 + (ya + n - 2))
                        dve.wait_ge(x_done, j * 3 + (3 * p0 + 3 + n + 1))
                        join(j, n, XB, x_dve)

            def last_join(p0, stage, join):
                for n in range(3):
                    dve.wait_ge(y_act, Y_ACT[stage] + 3 * (KT - 2) + n + 1)
                    dve.wait_ge(y_done, 3 * (p0 + KT - 1) + n + 1)
                    join(KT - 1, n, YB, y_dve)

            def join_attention(j, n, banks, freed):
                c0, cn = CHUNKS[n]
                D.scalar_tensor_tensor(row(merged, j, c0, cn), GG[n][:, 0:cn], 1.0, banks[n][:, 0:cn],
                                       ALU.add, ALU.mult).then_inc(freed, 1)

            joins(PAIR_G1, "G1", join_attention)
            last_join(PAIR_G1, "G1", join_attention)

            dve.wait_ge(y_dve, Y_DVE["G0"])
            link(D.memset(U[:, 0:LRU_HIST], 0.0))

            def lru_history(j):
                dve.wait_ge(x_act, j * 3 + (X_ACT["R"] + 3))
                for r, c0 in enumerate((SEQ, T)):
                    D.tensor_copy(st_lconv[:, cols(j, 1), r, :].rearrange("p a n -> p (a n)"), U[:, c0:c0 + LRU_HIST])
                D.tensor_copy(U[:, SMP:SMP + LRU_HIST], VD("conv0", j * LRU_HIST, LRU_HIST)).then_inc(r_fix, 1)

            def lru_conv(j, n):
                c0, cn = CHUNKS[n]
                dve.wait_ge(r_x0, j * 3 + (n + 1))
                for tap in (2, 1, 0):
                    ins = D.scalar_tensor_tensor(XC[n][:, 0:cn], U[:, tap + c0:tap + c0 + cn], VD("conv_w", j * 4 + tap),
                                                 XC[n][:, 0:cn], ALU.mult, ALU.add)
                    if tap:
                        link(ins)
                ins.then_inc(r_xc, 1)

            def lru_inputs(j):
                for n, (c0, cn) in enumerate(CHUNKS):
                    ck = slice(c0, c0 + cn)
                    dve.wait_ge(r_tanh, j * 3 + (START + n + 1))
                    D.scalar_tensor_tensor(FI[:, ck], FI[:, ck], 1.0, XC[n][:, 0:cn], ALU.add, ALU.mult)
                    dve.wait_ge(r_sqa, j * 3 + (n + 1))
                    D.scalar_tensor_tensor(FS[:, ck], FS[:, ck], 1.0, row(resid, j, c0, cn), ALU.add, ALU.mult).then_inc(r_om, 1)

            def lru_scan(j):
                dve.wait_ge(r_root, j + 1)
                link(D.tensor_tensor(FI[:, :], FI[:, :], FS[:, :], ALU.mult))
                D.tensor_tensor_scan(FI[:, 0:SEQ], FA[:, 0:SEQ], FI[:, 0:SEQ], 0.0, ALU.mult, ALU.add)
                D.memset(FI[:, SEQ:SMP], 0.0)
                D.tensor_tensor_scan(FI[:, SMP:T], FA[:, SMP:T], FI[:, SMP:T], VD("h0", j), ALU.mult, ALU.add).then_inc(r_h, 1)
                dve.wait_ge(r_h, j + 1)
                for r, c0 in enumerate((SEQ - 1, T - 1)):
                    D.tensor_copy(st_h[:, cols(j, 1), r:r + 1].rearrange("p a n -> p (a n)"), FI[:, c0:c0 + 1])
                for n, (c0, cn) in enumerate(CHUNKS):
                    dve.wait_ge(y_act, j * 3 + (Y_ACT["R"] + n + 1))
                    D.tensor_tensor(FA[:, c0:c0 + cn], FI[:, c0:c0 + cn], row(sqsum, j, c0, cn), ALU.mult).then_inc(r_z, 1)

            def lru_lo(j):
                for n, (c0, cn) in enumerate(CHUNKS):
                    dve.wait_ge(r_hi, j * 3 + (n + 1))
                    D.tensor_tensor(row(d_lo, j, c0, cn), FA[:, c0:c0 + cn], row(c_hi, j, c0, cn).bitcast(F32),
                                    ALU.subtract).then_inc(r_lo, 1)

            lru_history(0)
            for n in range(3):
                lru_conv(0, n)
            with dve.Fori(0, KT - 1) as j:
                ch.enter(j, 2 * 3 + 1)
                lru_history(j + 1)
                lru_inputs(j)
                lru_scan(j)
                lru_conv(j + 1, 0)
                lru_lo(j)
                lru_conv(j + 1, 1)
                lru_conv(j + 1, 2)
                ch.leave(KT - 1)
            lru_inputs(KT - 1)
            lru_scan(KT - 1)
            lru_lo(KT - 1)

            def join_lru(j, n, banks, freed):
                c0, cn = CHUNKS[n]
                D.scalar_tensor_tensor(GV[n][:, 0:cn], GG[n][:, 0:cn], 1.0, banks[n][:, 0:cn], ALU.add, ALU.mult).then_inc(freed, 1)
                dve.wait_ge(freed, Y_DVE["G0"] + n + 1 if freed is y_dve else j * 3 + (X_DVE["G0"] + n + 1))
                D.tensor_tensor(row(merged, j, c0, cn), row(merged, j, c0, cn), GV[n][:, 0:cn], ALU.add).then_inc(m_mrg, 1)

            joins(PAIR_G0, "G0", join_lru)
            with dve.Fori(0, KT - 1) as k:
                dve.wait_ge(m_hi, k + 1)
                D.scalar_tensor_tensor(row(x_lo, k, 0, T), row(merged, k, 0, T), 0.5, row(x_hi, k, 0, T).bitcast(F32),
                                       ALU.mult, ALU.subtract).then_inc(m_lo, 1)
            last_join(PAIR_G0, "G0", join_lru)
            for n, (c0, cn) in enumerate(CHUNKS):
                dve.wait_ge(m_hi, KT + n)
                D.scalar_tensor_tensor(row(x_lo, KT - 1, c0, cn), row(merged, KT - 1, c0, cn), 0.5,
                                       row(x_hi, KT - 1, c0, cn).bitcast(F32), ALU.mult, ALU.subtract).then_inc(m_lo, 1)

            for h in range(2):
                dve.wait_ge(s_xres[h], 16)
            link(D.memset(nacc[:, :], 0.0))
            with dve.Fori(0, KT // 2) as i:
                for s, (done, free) in enumerate(((x_done, x_dve), (y_done, y_dve))):
                    for n, (c0, cn) in enumerate(CHUNKS):
                        dve.wait_ge(done, i * 3 + (3 * PAIR_O + n + 1))
                        D.tensor_tensor(row(resid, i * 2 + s, c0, cn), bank[3 * s + n][:, 0:cn], row(sqsum, i * 2 + s, c0, cn),
                                        ALU.add).then_inc(free, 1)
                        dve.wait_ge(n_sq, i * 6 + (KT + 3 * s + n + 1))
                        dve.wait_ge(n_acc, i * 6 + (KT + 3 * s + n - 2))
                        D.tensor_tensor(nacc[:, c0:c0 + cn], nacc[:, c0:c0 + cn], row(merged, i * 2 + s, c0, cn), ALU.add).then_inc(n_acc, 1)
            norm(1)

            link(D.memset(GB[:, 0:FFN_HIST], 0.0))
            with dve.Fori(0, FFN_PARTS) as f:
                ch.enter(f, 3 * KT)
                with dve.Fori(0, KT) as j:
                    ch.enter(j, 3)
                    p3 = f * (3 * PAIRS_PER_PART) + j * 3
                    ft = f * KT + j
                    dve.wait_ge(x_act, f * UP + j * 3 + (X_ACT["F"] + 3))
                    for r, c0 in enumerate((SEQ, T)):
                        D.tensor_copy(st_fconv[:, bass.ds(ft, 1), r, :].rearrange("p a n -> p (a n)"), GB[:, c0:c0 + FFN_HIST])
                    D.tensor_copy(GB[:, SMP:SMP + FFN_HIST], VD("fconv0", ft * FFN_HIST, FFN_HIST)).then_inc(f_fix, 1)
                    for n, (c0, cn) in enumerate(CHUNKS):
                        dve.wait_ge(f_c0, ft * 3 + (n + 1))
                        for tap in (1, 0):
                            ins = D.scalar_tensor_tensor(GC[n][:, 0:cn], GB[:, tap + c0:tap + c0 + cn], VD("fconv_w", ft * 3 + tap),
                                                         GC[n][:, 0:cn], ALU.mult, ALU.add)
                            if tap:
                                link(ins)
                        ins.then_inc(f_conv, 1)
                    for n, (c0, cn) in enumerate(CHUNKS):
                        dve.wait_ge(f_gelu, ft * 3 + (n + 1))
                        dve.wait_ge(y_done, p3 + (3 * PAIR_F + n + 1))
                        D.tensor_tensor(GV[n][:, 0:cn], GC[n][:, 0:cn], bank[3 + n][:, 0:cn], ALU.mult).then_inc(y_dve, 1)
                    for n, (c0, cn) in enumerate(CHUNKS):
                        dve.wait_ge(f_hi, ft * 3 + (n + 1))
                        D.tensor_tensor(row(act_lo, j, c0, cn), GV[n][:, 0:cn], row(act_hi, j, c0, cn).bitcast(F32),
                                        ALU.subtract).then_inc(f_lo, 1)
                    ch.leave(KT)
                ch.leave(FFN_PARTS)
                with dve.Fori(0, KT // 2) as i:
                    for s, (done, free) in enumerate(((x_done, x_dve), (y_done, y_dve))):
                        for n, (c0, cn) in enumerate(CHUNKS):
                            dve.wait_ge(done, f * (3 * PAIRS_PER_PART) + i * 3 + (3 * (PAIR_F + KT) + n + 1))
                            D.tensor_tensor(row(resid, i * 2 + s, c0, cn), row(resid, i * 2 + s, c0, cn), bank[3 * s + n][:, 0:cn],
                                            ALU.add).then_inc(free, 1)


def _tiles(w):
    k, n = w.shape
    return w.reshape(k // P, P, n // P, P).transpose(2, 1, 0, 3).reshape(n // P, P, k)


def _cols(v):
    return v.reshape(-1, P).T


def kernel(**inputs):
    import concourse.bacc as bacc
    from concourse.bass_utils import run_bass_kernel_spmd

    x = {k: np.asarray(v) for k, v in inputs.items()}
    f32 = np.float32
    cat, ct = np.concatenate, np.ascontiguousarray

    order = [4 * (2 * a + e) + s for a in range(2) for s in range(4) for e in range(2)]
    rows = cat([np.arange(HD) + HD * h for h in order])
    w_in = x["w_in"][0]
    u, y, q, k, v, g0, g1 = np.split(w_in, np.cumsum([DM, DM, DM, NKV * HD, NKV * HD, DM]), axis=1)
    q = _tiles(q[:, rows])
    k, v, u, y, g0, g1 = (_tiles(w) for w in (k, v, u, y, g0, g1))
    br_l, br_a = _tiles(x["w_br_lru"][0]), _tiles(x["w_br_attn"][0][rows])
    out = _tiles(x["w_out"][0])
    gate, up = (_tiles(w) for w in np.split(x["w_up"][0], 2, axis=1))
    down = [_tiles(w) for w in np.split(x["w_down"][0], FFN_PARTS, axis=0)]
    slots = []
    for a in range(2):
        slots += [k[a], *q[4 * a:4 * a + 4], v[a]]
    def gated(g, b):
        return [g[0], g[1]] + [w for j in range(KT - 2) for w in (b[j], g[j + 2])] + [b[KT - 2], b[KT - 1]]

    slots += gated(g1, br_a)
    for j in range(KT):
        slots += [u[j], y[j]]
    slots += gated(g0, br_l)
    slots += list(out)
    for f in range(FFN_PARTS):
        for j in range(KT):
            slots += [gate[KT * f + j], up[KT * f + j]]
        slots += list(down[f])
    W = np.stack(slots)
    assert W.shape[0] == NSLOT

    xT = np.zeros((DM, T), f32)
    xT[:, :SEQ], xT[:, SMP:] = x["x_prompt"][0].T, x["x_sample"][0].T
    wab = np.zeros((KT, P, 2, P), f32)
    for m, name in enumerate(("w_lru_a", "w_lru_i")):
        for j in range(KT):
            for e in range(2):
                wab[j, HD * e:HD * e + HD, m, HD * e:HD * e + HD] = x[name][0, 2 * j + e]
    sink = x["attn_sink"][0]
    sink_p = np.stack([np.repeat([sink[4 * (2 * a + e) + 2 * uu + s] for s in range(2)], CHUNK)
                       for a in range(2) for e in range(2) for uu in range(2)], axis=1)
    sink_s = np.stack([np.repeat([sink[4 * (2 * a + e) + s] for s in range(4)], DSEQ)
                       for a in range(2) for e in range(2)], axis=1)
    bg = x["b_gate"][0]
    parts = dict(bg_lru=_cols(bg[:DM]), bg_att=_cols(bg[DM:]),
                 conv_w=x["w_lru_conv"][0].reshape(4, KT, P).transpose(2, 1, 0).reshape(P, -1), conv_b=_cols(x["b_lru_conv"][0]),
                 b_a=_cols(x["b_lru_a"][0]), b_i=_cols(x["b_lru_i"][0]), lam=_cols(x["lru_lambda"][0]),
                 g_mix=_cols(x["g_mix"][0]), g_ffn=_cols(x["g_ffn"][0]),
                 fconv_w=x["w_ffn_conv"][0].reshape(3, FT, P).transpose(2, 1, 0).reshape(P, -1), fconv_b=_cols(x["b_ffn_conv"][0]),
                 h0=_cols(x["state_lru_h"][0, 0]), g_q=np.tile(x["g_q"][0], 2)[:, None], g_k=np.tile(x["g_k"][0], 2)[:, None],
                 sink_p=sink_p, sink_s=sink_s,
                 conv0=x["state_lru_conv"][0, 0].reshape(LRU_HIST, KT, P).transpose(2, 1, 0).reshape(P, -1),
                 fconv0=x["state_ffn_conv"][0, 0].reshape(FFN_HIST, FT, P).transpose(2, 1, 0).reshape(P, -1))
    vecs = cat([parts[name] for name in VEC], axis=1)
    assert vecs.shape[1] == NVEC and all(parts[n].shape[1] == VEC[n][1] for n in VEC)
    two = np.kron(np.eye(2, dtype=f32), np.ones((HD, HD), f32))
    mats = np.stack([np.eye(P, dtype=f32), np.ones((P, P), f32), two], axis=1)
    kc, vc = (x[name][0, 0].transpose(1, 2, 0).reshape(2, P, WIN).transpose(1, 0, 2) for name in ("cache_k", "cache_v"))

    nc = bacc.Bacc("TRN2", target_bir_lowering=False, num_devices=1)
    arrays, args = {}, []
    for name, a in (("xT", xT.reshape(KT, P, T)), ("W", W), ("wab", wab), ("vecs", vecs), ("mats", mats), ("kc", kc), ("vc", vc)):
        arrays[name] = ct(a)
        args.append(nc.dram_tensor(name, list(a.shape), F32, kind="ExternalInput").ap())
    outs = dict(yT=[KT, P, T], lconv=[P, KT, 2, LRU_HIST], h=[P, KT, 2], fconv=[P, FT, 2, FFN_HIST],
                kp=[2, P, WIN], ks=[2, P, DSEQ], vp=[2, P, WIN], vs=[2, P, DSEQ])
    for name, shape in outs.items():
        args.append(nc.dram_tensor("o_" + name, shape, F32, kind="ExternalOutput").ap())
    build(nc, *args)
    r = run_bass_kernel_spmd(nc, [arrays], core_ids=[0]).results[0]
    o = {name: np.asarray(r["o_" + name]) for name in outs}
    yT = o["yT"].reshape(DM, T)

    def state(t, r_):
        return ct(t[:, :, r_, :].transpose(2, 1, 0).reshape(1, 1, t.shape[3], -1))

    def heads(t):
        return ct(t.reshape(2, 2, HD, -1).transpose(3, 0, 1, 2).reshape(1, 1, t.shape[2], NKV, HD))

    def last(r_):
        return ct(o["h"][:, :, r_].T.reshape(1, 1, DM))

    return (ct(yT[:, :SEQ].T)[None], ct(yT[:, SMP:].T)[None],
            state(o["lconv"], 0), last(0), heads(o["kp"]), heads(o["vp"]), state(o["fconv"], 0),
            state(o["lconv"], 1), last(1), heads(o["ks"]), heads(o["vs"]), state(o["fconv"], 1))
```

```python
from contextlib import ExitStack

import concourse.bass as bass
import numpy as np
from concourse import mybir

F32 = mybir.dt.float32
F32R = mybir.dt.float32r
ACT = mybir.ActivationFunctionType
ALU = mybir.AluOpType
AXX = mybir.AxisListType.X

P = 128
DM, SEQ, DSEQ, PAD = 1024, 1024, 32, 4
NKV, HD, CHUNK, WIN = 4, 64, 64, 128
DFF = 3 * DM
KT = DM // P
FT = DFF // P
SMP = SEQ + PAD
T = SMP + DSEQ
CHUNKS = [(0, 354), (354, 354), (708, 352)]
NC = SEQ // CHUNK
EPS = 1e-6
LRU_HIST, FFN_HIST = 3, 2

ATT_PAIRS = 3
PAIR_G1 = 2 * ATT_PAIRS
PAIR_R = PAIR_G1 + KT
PAIR_G0 = PAIR_R + KT
PAIR_O = PAIR_G0 + KT
PAIR_F = PAIR_O + KT // 2
FFN_PARTS = FT // KT
PAIRS_PER_PART = KT + KT // 2
NPAIR = PAIR_F + FFN_PARTS * PAIRS_PER_PART
NSLOT = 2 * NPAIR

X_ACT = dict(G1=6 * ATT_PAIRS)
X_ACT["R"] = X_ACT["G1"] + 3
X_ACT["G0"] = X_ACT["R"] + 3 * KT
X_ACT["F"] = X_ACT["G0"] + 3
Y_ACT = dict(G1=6 * ATT_PAIRS)
Y_ACT["R"] = Y_ACT["G1"] + 3 * (KT - 1)
Y_ACT["G0"] = Y_ACT["R"] + 3 * KT
X_DVE = dict(G1=3, G0=3 * KT, O=6 * KT - 3, F=6 * KT - 3 + 3 * KT // 2)
Y_DVE = dict(G1=3, G0=6, O=9, F=9 + 3 * KT // 2)
START = 4
NORM_BLOCKS = [(n, min(P * b, cn - P)) for n, (_, cn) in enumerate(CHUNKS) for b in range(3)]
UP, DOWN = 3 * KT, 3 * KT // 2
X_END = X_DVE["F"] + FFN_PARTS * DOWN
Y_END = Y_DVE["F"] + FFN_PARTS * (UP + DOWN)

VEC = {}
_at = 0
for _name, _n in (("bg_lru", KT), ("bg_att", KT), ("conv_w", 4 * KT), ("conv_b", KT), ("b_a", KT), ("b_i", KT), ("lam", KT),
                  ("g_mix", KT), ("g_ffn", KT), ("fconv_w", 3 * FT), ("fconv_b", FT), ("h0", KT), ("g_q", 1), ("g_k", 1),
                  ("sink_p", 8), ("sink_s", 4), ("conv0", LRU_HIST * KT), ("fconv0", FFN_HIST * FT)):
    VEC[_name] = (_at, _n)
    _at += _n
NVEC = _at


class Count:

    def __init__(self, sem):
        self.sem, self.n, self.turns = sem, 0, []

    def inc(self, ins):
        ins.then_inc(self.sem, 1)
        self.n += 1

    def value(self):
        v = self.n
        for i, k, _ in self.turns:
            v = i * k + v
        return v

    def enter(self, i, per_turn):
        self.turns.append((i, per_turn, self.n))

    def leave(self, trips):
        _, k, start = self.turns.pop()
        assert self.n - start == k, (self.n - start, k)
        self.n = start + k * trips


def build(nc, xT, W, wab, vecs, mats, kc, vc, yT, o_lconv, o_h, o_fconv, o_kp, o_ks, o_vp, o_vs):
    ctx = ExitStack()
    with ctx:
        def sem(name):
            return ctx.enter_context(nc.semaphore(name))

        base = [(nc.sbuf_base + 63) // 64 * 64]
        end = nc.sbuf_usable_end

        def place(name, shape, dt, at=None):
            size = 4 * int(np.prod(shape[1:]))
            if at is None:
                at = base[0]
                base[0] += (size + 31) // 32 * 32
                assert base[0] <= end, (name, base[0], end)
            return nc.alloc_sbuf_tensor_at(name, shape, dt, offset=at), at

        def sb(name, shape, dt=F32, at=None):
            return place(name, shape, dt, at)[0]

        FULL = [P, KT, T]
        x_hi, _ = place("x_hi", FULL, F32R)
        x_lo, _ = place("x_lo", FULL, F32R)
        c_hi, at_c = place("c_hi", FULL, F32R)
        d_lo, at_d = place("d_lo", FULL, F32R)
        act_lo, at_e = place("act_lo", FULL, F32R)
        resid = sb("resid", FULL, F32, at_c)
        sqsum = sb("sqsum", FULL, F32, at_d)
        merged = sb("merged", FULL, F32, at_e)
        act_hi = sb("act_hi", FULL, F32R, at_d)
        irms = sb("irms", [P, T], F32, at_c + 6 * T * 4)
        sq = sb("sq", [P, 2, T], F32, at_c + 4 * T * 4)
        qT = sb("qT", [P, 4, T], F32, at_e)
        kN = sb("kN", [P, T], F32, at_e + 4 * T * 4)
        row_bytes = (4 * T + 31) // 32 * 32
        kG = sb("kG", [P, T], F32, at_e + 4 * T * 4 + row_bytes)
        vT = sb("vT", [P, T], F32, at_e + 4 * T * 4 + 2 * row_bytes)
        kcs = sb("kcs", [P, 2, WIN], F32, at_e + 4 * T * 4 + 3 * row_bytes)
        vcs = sb("vcs", [P, 2, WIN], F32, at_e + 4 * T * 4 + 3 * row_bytes + 2 * WIN * 4)
        w_raw, w_hi, w_lo = [], [], []
        for s in range(2):
            r, at = place(f"w_raw{s}", [P, DM], F32)
            w_raw.append(r)
            w_lo.append(sb(f"w_lo{s}", [P, DM], F32R, at))
            w_hi.append(sb(f"w_hi{s}", [P, DM], F32R))
        vec = sb("vec", [P, NVEC])
        mat = sb("mat", [P, 3, P])
        ident, ones, bones = mat[:, 0, :], mat[:, 1, :], mat[:, 2, :]
        halfb = sb("halfb", [P, 4 * KT])
        lamc = sb("lamc", [P, 2, KT])
        lam_t = sb("lam_t", [P, 5, KT])
        st_lconv = sb("st_lconv", [P, KT, 2, LRU_HIST])
        st_h = sb("st_h", [P, KT, 2])
        st_fconv = sb("st_fconv", [P, FT, 2, FFN_HIST])
        negsink = sb("negsink", [P, 12])
        epsc = sb("epsc", [P, 2])
        warm = sb("warm", [P, 1])
        tr = base[0]
        gates_bytes = 3 * 1440
        GG = [sb(f"GG{i}", [P, 354], F32, tr + 1440 * i) for i in range(3)]
        U = sb("U", [P, LRU_HIST + T], F32, tr)
        base[0] += gates_bytes
        FA = sb("FA", [P, T])
        FI = sb("FI", [P, T])
        FS = sb("FS", [P, T])
        XC = [sb(f"XC{i}", [P, 354]) for i in range(3)]
        wabs = sb("wabs", [P, 2, P])
        at = [tr]

        def ta(name, shape):
            size = 4 * int(np.prod(shape[1:]))
            t = sb(name, shape, F32, at[0])
            at[0] += (size + 31) // 32 * 32
            assert at[0] <= end
            return t
        qs = [ta(f"qs{i}", [P, 4, CHUNK]) for i in range(2)]
        ks = [ta(f"ks{i}", [P, 3 * CHUNK]) for i in range(2)]
        vs = [ta(f"vs{i}", [P, 3 * CHUNK]) for i in range(2)]
        pr = [ta(f"pr{i}", [P, 4, 3 * CHUNK]) for i in range(2)]
        pt = [ta(f"pt{i}", [P, 4 * P]) for i in range(2)]
        vt = [ta(f"vt{i}", [P, P]) for i in range(2)]
        of = ta("of", [P, 4 * CHUNK])
        small = [ta(f"small{i}", [P, 6, 4]) for i in range(2)]
        at = [tr]
        GB = ta("GB", [P, FFN_HIST + T])
        GC = [ta(f"GC{i}", [P, 354]) for i in range(3)]
        GV = [ta(f"GV{i}", [P, 354]) for i in range(3)]
        at = [tr]
        nacc = ta("nacc", [P, T])
        nst = ta("nst", [P, 4, 2 * len(NORM_BLOCKS)])
        dg = ta("dg", [P, len(NORM_BLOCKS), P])
        ntmp = [ta(f"ntmp{i}", [P, 354]) for i in range(4)]

        bankpair = [ctx.enter_context(nc.psum_tensor(f"banks{b}", [P, 2, 512], F32)) for b in range(4)]
        bank = [bankpair[b // 2][:, b % 2, :] for b in range(8)]
        XB, YB = bank[0:3], bank[3:6]

        def V(name, i=0, n=1):
            a, _ = VEC[name]
            return vec[:, a + i:a + i + n]

        def VD(name, i, n=1):
            a, _ = VEC[name]
            return vec[:, bass.ds(i + a, n)]

        def row(t, k, c0, cn):
            if isinstance(k, int):
                return t[:, k, c0:c0 + cn]
            return t[:, bass.ds(k, 1), c0:c0 + cn].rearrange("p a n -> p (a n)")

        def cols(c0, n):
            return slice(c0, c0 + n) if isinstance(c0, int) else bass.ds(c0, n)

        s_vec = sem("tables_loaded")
        s_x = [sem(f"x_loaded{i}") for i in range(2 * len(CHUNKS))]
        s_cache = sem("cache_loaded")
        s_xres = [sem(f"residual_x_loaded{k}") for k in range(2)]
        s_wab = sem("lru_gate_weights_loaded")
        wx_loaded, wy_loaded = sem("wx_loaded"), sem("wy_loaded")
        wx_ready, wy_ready = sem("wx_ready"), sem("wy_ready")
        w_hi_done = sem("w_hi_done")
        x_done, y_done = sem("x_done"), sem("y_done")
        x_act, y_act = sem("x_freed_by_act"), sem("y_freed_by_act")
        x_dve, y_dve = sem("x_freed_by_dve"), sem("y_freed_by_dve")
        act_c, dve_c = sem("act_chain"), sem("dve_chain")
        s_eps, s_exp_lam, s_lamc = sem("eps_set"), sem("exp_lambda"), sem("lambda_ready")
        n_sq, n_acc, n_ps, n_rt, n_dg, n_bc, n_f32, n_hi, n_lo = (
            sem(f"norm_{x}") for x in ("squares", "summed", "psum", "root", "diagonals", "broadcast", "f32", "hi", "lo"))
        n_lop = sem("norm_lo_by_pool")
        h_ps, h_rt, h_rdy = (sem(f"heads_norm_{x}") for x in ("psum", "root", "ready"))
        a_stv = sem("att_v_staged")
        a_stg, a_S, a_stat, a_exp, a_nrm, a_T, a_ev, a_evv, a_O, a_hi, a_lo = (
            sem(f"att_{x}") for x in ("q_k_staged", "scores", "stats", "exp", "normalised", "transposed", "p_v_copied",
                                      "late_p_copied", "out", "hi", "lo"))
        r_fix, r_x0, r_xc, r_ps, r_tanh, r_sqa, r_om, r_root, r_h, r_z, r_hi, r_lo = (
            sem(f"lru_{x}") for x in ("history", "x0", "xc", "psum", "tanh", "a_squared", "one_minus_a2", "root", "h",
                                      "z", "hi", "lo"))
        m_mrg, m_hi, m_lo = sem("merged"), sem("merged_hi"), sem("merged_lo")
        f_fix, f_c0, f_conv, f_gelu, f_hi, f_lo = (
            sem(f"ffn_{x}") for x in ("history", "c0", "conv", "gelu", "hi", "lo"))
        s_out = sem("outputs_stored")
        s_own = [sem(f"own_{x}") for x in ("pool", "pe", "act")]

        block = ctx.enter_context(nc.Block())
        NB = NC + 1
        STG = 2 * NC + 3
        GEN = NC - 4

        @block.sync
        def _(sp):
            for n, (c0, cn) in enumerate(CHUNKS):
                for h in range(2):
                    kk = slice(h * KT // 2, (h + 1) * KT // 2)
                    sp.dma_start(resid[:, kk, c0:c0 + cn], xT[kk, :, c0:c0 + cn].rearrange("k p n -> p k n")).then_inc(s_x[2 * n + h], 16)
                if n == 0:
                    sp.dma_start(mat[:, :, :], mats).then_inc(s_vec, 16)
                    sp.dma_start(vec[:, :], vecs).then_inc(s_vec, 16)
                    sp.dma_start(w_raw[0][:, :], W[0]).then_inc(wx_loaded, 16)
            sp.dma_start(w_raw[1][:, :], W[1]).then_inc(wy_loaded, 16)
            sp.wait_ge(n_ps, 3)
            sp.dma_start(kcs[:, :, :], kc).then_inc(s_cache, 16)
            sp.dma_start(vcs[:, :, :], vc).then_inc(s_cache, 16)
            with sp.Fori(0, NPAIR - 1) as i:
                for s, (done, loaded) in enumerate(((x_done, wx_loaded), (y_done, wy_loaded))):
                    sp.wait_ge(done, i * 3 + 3)
                    sp.dma_start(w_raw[s][:, :], W[bass.ds(i * 2 + (2 + s), 1)].rearrange("a p n -> (a p) n")).then_inc(loaded, 16)
            sp.wait_ge(r_lo, START + 3 * KT)
            sp.dma_start(o_lconv, st_lconv[:, :, :, :]).then_inc(s_out, 16)
            sp.dma_start(o_h, st_h[:, :, :]).then_inc(s_out, 16)
            sp.wait_ge(f_lo, 3 * FT)
            sp.dma_start(o_fconv, st_fconv[:, :, :, :]).then_inc(s_out, 16)
            for k in range(KT):
                sp.wait_ge(x_dve if k % 2 == 0 else y_dve, (X_END if k % 2 == 0 else Y_END) - 3 * (KT // 2 - 1 - k // 2))
                sp.dma_start(yT[k], resid[:, k, :]).then_inc(s_out, 16)
            sp.wait_ge(s_out, 16 * (8 + 3 + KT))

        @block.gpsimd
        def _(pool):
            def split(p, slots=(0, 1)):
                for s in slots:
                    loaded, ready = ((wx_loaded, wx_ready), (wy_loaded, wy_ready))[s]
                    pool.wait_ge(loaded, p * 16 + 16)
                    if not isinstance(p, int):
                        pool.sem_inc(s_own[0], 1)
                    nc.gpsimd.tensor_scalar(w_hi[s][:, :], w_raw[s][:, :], 1.0, 0.0, ALU.mult, ALU.add).then_inc(w_hi_done, 1)
                    pool.wait_ge(w_hi_done, p * 2 + (s + 1))
                    nc.gpsimd.tensor_tensor(w_lo[s][:, :], w_raw[s][:, :], w_hi[s][:, :].bitcast(F32), ALU.subtract).then_inc(ready, 1)

            def norm(which):
                for n, (c0, cn) in enumerate(CHUNKS):
                    with pool.Fori(0, 2) as i:
                        for h in range(1, 4):
                            pool.wait_ge(n_hi, i * 4 + (KT * (3 * which + n) + h + 1))
                            pool.sem_inc(s_own[0], 1)
                            nc.gpsimd.tensor_tensor(row(x_lo, i * 4 + h, c0, cn), ntmp[h][:, 0:cn],
                                                    row(x_hi, i * 4 + h, c0, cn).bitcast(F32), ALU.subtract).then_inc(n_lop, 1)

            def stage_qk(s, q0, k0, keys):
                nc.gpsimd.tensor_copy(qs[s][:, :, :], qT[:, :, cols(q0, CHUNK)]).then_inc(a_stg, 1)
                nc.gpsimd.tensor_copy(ks[s][:, 0:keys], kG[:, cols(k0, keys)]).then_inc(a_stg, 1)

            def stage_v(s, k0, keys):
                nc.gpsimd.tensor_copy(vs[s][:, 0:keys], vT[:, cols(k0, keys)]).then_inc(a_stv, 1)

            def att_lo(a, b, c0, cn):
                pool.wait_ge(a_hi, b + 1)
                pool.sem_inc(s_own[0], 1)
                nc.gpsimd.tensor_tensor(d_lo[:, 4 * a:4 * a + 4, cols(c0, cn)], of[:, 0:4 * cn].rearrange("p (a b) -> p a b", b=cn),
                                        c_hi[:, 4 * a:4 * a + 4, cols(c0, cn)].bitcast(F32), ALU.subtract).then_inc(a_lo, 1)

            pool.sem_inc(n_lop, START)
            for a in range(2):
                B0, p0 = NB * a, ATT_PAIRS * a
                if a == 0:
                    split(0, (0,))
                    norm(0)
                    split(0, (1,))
                for p in range(p0 + 1, p0 + ATT_PAIRS):
                    split(p)
                pool.wait_ge(h_rdy, 15 * a + 13)
                for b in range(2):
                    stage_qk(b, b * CHUNK, 0, (b + 1) * CHUNK)
                split(p0 + ATT_PAIRS, (0,))
                pool.wait_ge(y_act, 3 * (p0 + ATT_PAIRS) - 2)
                for b in range(2):
                    stage_v(b, 0, (b + 1) * CHUNK)
                pool.wait_ge(h_rdy, 15 * a + 15)

                def next_qk(l, s):
                    pool.wait_ge(a_S, l + (B0 - 1))
                    if not isinstance(l, int):
                        pool.sem_inc(s_own[0], 1)
                    stage_qk(s, l * CHUNK, l * CHUNK - 2 * CHUNK, 3 * CHUNK)

                def next_v(l, s):
                    pool.wait_ge(a_T, l + (B0 - 1))
                    if not isinstance(l, int):
                        pool.sem_inc(s_own[0], 1)
                    stage_v(s, l * CHUNK - 2 * CHUNK, 3 * CHUNK)

                next_qk(2, 0)
                next_qk(3, 1)
                next_qk(4, 0)
                pool.wait_ge(y_act, 3 * (p0 + ATT_PAIRS))
                next_v(2, 0)
                with pool.Fori(0, GEN // 2 - 1) as i:
                    for l in range(2):
                        next_qk(i * 2 + (5 + l), 1 - l)
                        next_v(i * 2 + (3 + l), 1 - l)
                        att_lo(a, i * 2 + (B0 + l), i * (2 * CHUNK) + l * CHUNK, CHUNK)
                next_qk(NC - 1, 1)
                next_v(NC - 3, 1)
                att_lo(a, B0 + NC - 6, SEQ - 6 * CHUNK, CHUNK)
                pool.wait_ge(a_S, B0 + NC - 1)
                pool.wait_ge(s_cache, 32)
                nc.gpsimd.tensor_copy(qs[0][:, 0:2, :].rearrange("p a b -> p (a b)").rearrange("p (a b) -> p a b", b=DSEQ),
                                      qT[:, :, SMP:T]).then_inc(a_stg, 1)
                nc.gpsimd.tensor_scalar(ks[0][:, 0:WIN], kcs[:, a, :], V("g_q"), 0.0, ALU.mult, ALU.add).then_inc(a_stg, 1)
                nc.gpsimd.tensor_copy(ks[0][:, WIN:WIN + DSEQ], kG[:, SMP:T]).then_inc(a_stg, 1)
                next_v(NC - 2, 0)
                att_lo(a, B0 + NC - 5, SEQ - 5 * CHUNK, CHUNK)
                next_v(NC - 1, 1)
                att_lo(a, B0 + NC - 4, SEQ - 4 * CHUNK, CHUNK)
                pool.wait_ge(a_T, B0 + NC - 1)
                nc.gpsimd.tensor_copy(vs[0][:, 0:WIN], vcs[:, a, :]).then_inc(a_stv, 1)
                nc.gpsimd.tensor_copy(vs[0][:, WIN:WIN + DSEQ], vT[:, SMP:T]).then_inc(a_stv, 1)
                att_lo(a, B0 + NC - 3, SEQ - 3 * CHUNK, CHUNK)
                att_lo(a, B0 + NC - 2, SEQ - 2 * CHUNK, CHUNK)
                att_lo(a, B0 + NC - 1, SEQ - CHUNK, CHUNK)
                att_lo(a, B0 + NC, SMP, DSEQ)
                split(p0 + ATT_PAIRS, (1,))
            with pool.Fori(0, PAIR_F - 2 * ATT_PAIRS - 1) as i:
                split(i + (2 * ATT_PAIRS + 1))
            split(PAIR_F, (0,))
            norm(1)
            split(PAIR_F, (1,))
            with pool.Fori(0, NPAIR - PAIR_F - 1) as i:
                split(i + (PAIR_F + 1))

        @block.tensor
        def _(pe):
            def chunk(s, n, hi, lo, before=None):
                cc, cn = CHUNKS[n]
                for k in range(KT):
                    if before is not None:
                        before(k)
                    for j, (w, x) in enumerate(((w_hi, hi), (w_hi, lo), (w_lo, hi))):
                        last = nc.tensor.matmul(bank[3 * s + n][:, 0:cn], w[s][:, k * P:(k + 1) * P], x[:, k, cc:cc + cn],
                                                start=(k == 0 and j == 0), stop=(k == KT - 1 and j == 2))
                last.then_inc(x_done if s == 0 else y_done, 1)

            def tile(s, i, p0, hi, lo, free=None, freed=None, before=None, after=None):
                pe.wait_ge(wx_ready if s == 0 else wy_ready, i + (p0 + 1))
                for n, (c0, cn) in enumerate(CHUNKS):
                    if free is not None:
                        pe.wait_ge(free, freed + (n - 2))
                    chunk(s, n, hi, lo, None if before is None else lambda k: before(n, k))
                    if after is not None:
                        after(n)

            def loop_tiles(p0, trips, hix, lox, hiy, loy, fx, x0, fy, y0):
                with pe.Fori(0, trips) as i:
                    tile(0, i, p0, hix, lox, fx, i * 3 + x0)
                    tile(1, i, p0, hiy, loy, fy, i * 3 + y0)

            def last_row(sem_, value):
                def before(n, k):
                    if k == KT - 1:
                        pe.wait_ge(sem_, value + (n + 1))
                return before

            def norm_sums(which, n):
                pe.wait_ge(n_acc, START + 3 * KT * which + n + 1)
                for b, (_, off) in enumerate(NORM_BLOCKS[3 * n:3 * n + 3]):
                    c0 = CHUNKS[n][0] + off
                    last = nc.tensor.matmul(bank[n][:, 2 * b:2 * b + 2], nacc[:, c0:c0 + P], ones[:, 0:2], start=True, stop=True)
                last.then_inc(n_ps, 1)

            def norm_spread(which, n):
                pe.wait_ge(n_dg, 3 * which + n + 1)
                for b, (_, off) in enumerate(NORM_BLOCKS[3 * n:3 * n + 3]):
                    last = nc.tensor.matmul(bank[6 + n % 2][:, off:off + P], ones, dg[:, 3 * n + b, :], start=True, stop=True)
                last.then_inc(n_bc, 1)

            def normed(which):
                def before(n, k):
                    if (n, k) == ((0, 0) if which else (0, KT // 2)):
                        norm_spread(which, 1)
                    if (n, k) == ((0, KT // 2) if which else (1, 0)):
                        norm_sums(which, 2)
                    if (n, k) == (1, KT // 2):
                        norm_spread(which, 2)
                    if k % 4 == 0:
                        groups = 2 * (3 * which + n) + k // 4 + 1
                        pe.wait_ge(n_lo, START + groups)
                        pe.wait_ge(n_lop, START + 3 * groups)
                return before

            pe.wait_ge(s_vec, 32)
            norm_sums(0, 0)
            norm_spread(0, 0)
            norm_sums(0, 1)

            for a in range(2):
                p0, B0, G0 = ATT_PAIRS * a, NB * a, STG * a
                def scores(b, s, keys, units, staged, first=False):
                    pe.wait_ge(a_stg, staged)
                    if not first:
                        pe.wait_ge(a_exp, b)
                    for e in range(2):
                        for u in range(units):
                            v = units * e + u
                            last = nc.tensor.matmul(bank[2 * s + v // 2][:, (v % 2) * 192:(v % 2) * 192 + keys],
                                                    qs[s][64 * e:64 * e + 64, 2 * u:2 * u + 2, :], ks[s][64 * e:64 * e + 64, 0:keys],
                                                    start=True, stop=True)
                    last.then_inc(a_S, 1)

                def groups_of(keys):
                    return [(0, min(keys, P))] + ([(P, keys - P)] if keys > P else [])

                def transposes(b, s, keys, units, staged):
                    groups = groups_of(keys)
                    pe.wait_ge(a_stv, staged)
                    if keys > 2 * CHUNK:
                        pe.wait_ge(a_evv, b + (START - 2 * a - 2))
                    pe.wait_ge(a_ev, b)
                    for g, (k0, kn) in enumerate(groups):
                        nc.tensor.transpose(bank[6][0:kn, g * P:g * P + P], vs[s][:, k0:k0 + kn], ident)
                    pe.wait_ge(a_nrm, b + 1)
                    for g, (k0, kn) in enumerate(groups):
                        for v in range(2 * units):
                            last = nc.tensor.transpose(bank[4 + g][0:kn, v * P:v * P + P], pr[s][:, v, k0:k0 + kn], ident)
                    last.then_inc(a_T, 1)

                def product(b, keys, units):
                    groups = groups_of(keys)
                    pe.wait_ge(a_ev, b + 1)
                    if keys > P:
                        pe.wait_ge(a_evv, b + (START - 2 * a - 1))
                    pe.wait_ge(a_hi, b)
                    rows = units * P
                    for e in range(2):
                        for g, (k0, kn) in enumerate(groups):
                            last = nc.tensor.matmul(bank[7][64 * e:64 * e + 64, 0:rows], vt[g][0:kn, 64 * e:64 * e + 64],
                                                    pt[g][0:kn, e * rows:e * rows + rows], start=(g == 0), stop=(g == len(groups) - 1))
                    last.then_inc(a_O, 1)

                if a == 0:
                    tile(0, 0, p0, x_hi, x_lo, before=normed(0))
                else:
                    pe.wait_ge(a_lo, B0)

                def sums(r_):
                    pair, free = p0 + r_ // 2, x_act if r_ % 2 == 0 else y_act

                    def before(n, k):
                        for c in ((0, 1) if (n, k) == (0, 0) else (2,) if (n, k) == (0, KT // 2) else ()):
                            c0, cn = CHUNKS[c]
                            m = 3 * (5 * a + r_) + c
                            pe.wait_ge(free, 3 * pair + c + 1)
                            if m > 1:
                                pe.wait_ge(h_rt, m - 1)
                            nc.tensor.matmul(bank[6 + m % 2][:, 0:cn], bones, sq[:, r_ % 2, c0:c0 + cn],
                                             start=True, stop=True).then_inc(h_ps, 1)
                    return before

                tile(1, 0, p0, x_hi, x_lo, before=sums(0))
                tile(0, 0, p0 + 1, x_hi, x_lo, x_act, 3 * p0 + 3, before=sums(1))
                tile(1, 0, p0 + 1, x_hi, x_lo, y_act, 3 * p0 + 3, before=sums(2))
                tile(0, 0, p0 + 2, x_hi, x_lo, x_act, 3 * p0 + 6, before=sums(3))

                def beside_v(n):
                    if n == 1:
                        scores(0, 0, CHUNK, 2, G0 + 2, True)
                        pe.wait_ge(y_act, 3 * p0 + 7)
                        scores(0, 1, 2 * CHUNK, 2, G0 + 4, True)

                tile(1, 0, p0 + 2, x_hi, x_lo, y_act, 3 * p0 + 6, before=sums(4), after=beside_v)
                pe.wait_ge(y_act, 3 * p0 + 8)
                pe.wait_ge(h_rt, 15 * (a + 1))

                V0 = (NB + 1) * a
                scores(B0 + 1, 0, 3 * CHUNK, 2, G0 + 6)
                transposes(B0, 0, CHUNK, 2, V0 + 1)
                scores(B0 + 2, 1, 3 * CHUNK, 2, G0 + 8)
                transposes(B0 + 1, 1, 2 * CHUNK, 2, V0 + 2)
                product(B0, CHUNK, 2)
                pe.wait_ge(y_act, 3 * p0 + 9)
                for s in range(2):
                    scores(B0 + 3 + s, s, 3 * CHUNK, 2, G0 + 10 + 2 * s)
                    transposes(B0 + 2 + s, s, 3 * CHUNK, 2, V0 + 3 + s)
                    product(B0 + 1 + s, (2 + s) * CHUNK, 2)
                with pe.Fori(0, GEN // 2 - 1) as i:
                    for s in range(2):
                        scores(i * 2 + (B0 + 5 + s), s, 3 * CHUNK, 2, i * 4 + (G0 + 14 + 2 * s))
                        transposes(i * 2 + (B0 + 4 + s), s, 3 * CHUNK, 2, i * 2 + (V0 + 5 + s))
                        product(i * 2 + (B0 + 3 + s), 3 * CHUNK, 2)
                pe.wait_ge(a_stg, G0 + STG)
                pe.wait_ge(a_exp, B0 + NC - 1)
                for e in range(2):
                    last = nc.tensor.matmul(bank[e][:, 0:WIN + DSEQ], qs[0][64 * e:64 * e + 64, 0:2, :],
                                            ks[0][64 * e:64 * e + 64, 0:WIN + DSEQ], start=True, stop=True)
                last.then_inc(a_S, 1)
                transposes(B0 + NC - 2, 0, 3 * CHUNK, 2, V0 + NC - 1)
                product(B0 + NC - 3, 3 * CHUNK, 2)
                transposes(B0 + NC - 1, 1, 3 * CHUNK, 2, V0 + NC)
                product(B0 + NC - 2, 3 * CHUNK, 2)

                def last_blocks(n):
                    if n == 0:
                        transposes(B0 + NC, 0, WIN + DSEQ, 1, V0 + NB + 1)
                        product(B0 + NC - 1, 3 * CHUNK, 2)
                    elif n == 1:
                        product(B0 + NC, WIN + DSEQ, 1)

                pe.wait_ge(a_exp, B0 + NB)
                tile(0, 0, p0 + ATT_PAIRS, x_hi, x_lo, after=last_blocks)

            pe.wait_ge(a_lo, 2 * NB)
            def gated(p0, stage, between=None, second=None, before=None):
                xa, ya, xd = X_ACT[stage], Y_ACT[stage], X_DVE[stage]
                if stage != "G1":
                    tile(0, 0, p0, x_hi, x_lo, x_act, xa)
                if between is not None:
                    between()
                tile(1, 0, p0, x_hi, x_lo, y_act, ya, before=second)
                pe.wait_ge(x_act, xa + 3)
                if before is not None:
                    pe.wait_ge(r_lo, START + 3 * (KT - 1))
                tile(0, 0, p0 + 1, c_hi, d_lo, before=before)
                tile(1, 0, p0 + 1, x_hi, x_lo, y_act, ya + 3)
                with pe.Fori(0, KT - 3) as i:
                    tile(0, i, p0 + 2, c_hi, d_lo, x_dve, i * 3 + (xd + 3))
                    tile(1, i, p0 + 2, x_hi, x_lo, y_act, i * 3 + (ya + 6))
                tile(0, 0, p0 + KT - 1, c_hi, d_lo, x_dve, xd + 3 * (KT - 2))
                tile(1, 0, p0 + KT - 1, c_hi, d_lo, y_act, ya + 3 * (KT - 1))

            gated(PAIR_G1, "G1")

            def lru_gates(j, n):
                cn = CHUNKS[n][1]
                pe.wait_ge(r_xc, j * 3 + (n + 1))
                pe.wait_ge(r_tanh, j * 3 + (START + n))
                nc.tensor.matmul(bank[6][:, 0:cn], wabs[:, 0, :], XC[n][:, 0:cn], start=True, stop=True)
                nc.tensor.matmul(bank[7][:, 0:cn], wabs[:, 1, :], XC[n][:, 0:cn], start=True, stop=True).then_inc(r_ps, 1)

            tile(0, 0, PAIR_R, x_hi, x_lo, x_dve, X_DVE["G0"])
            tile(1, 0, PAIR_R, x_hi, x_lo, y_dve, Y_DVE["G0"])
            with pe.Fori(0, KT - 1) as j:
                tile(0, j, PAIR_R + 1, x_hi, x_lo, x_act, j * 3 + (X_ACT["R"] + 3))
                pe.wait_ge(s_wab, j * 16 + 16)
                lru_gates(j, 0)
                tile(1, j, PAIR_R + 1, x_hi, x_lo, y_act, j * 3 + (Y_ACT["R"] + 3), after=lambda n: n < 2 and lru_gates(j, n + 1))

            def gates_first():
                pe.wait_ge(s_wab, 16 * KT)
                lru_gates(KT - 1, 0)

            def gates_later(n, k):
                if (n, k) in ((0, KT // 2), (1, 0)):
                    lru_gates(KT - 1, n + 1)

            gated(PAIR_G0, "G0", gates_first, gates_later, last_row(r_lo, START + 3 * (KT - 1)))

            pe.wait_ge(m_lo, KT - 1)
            tile(0, 0, PAIR_O, x_hi, x_lo, x_dve, X_DVE["O"], before=last_row(m_lo, KT - 1))
            tile(1, 0, PAIR_O, x_hi, x_lo, y_dve, Y_DVE["O"])
            loop_tiles(PAIR_O + 1, KT // 2 - 2, x_hi, x_lo, x_hi, x_lo, x_dve, X_DVE["O"] + 3, y_dve, Y_DVE["O"] + 3)
            last_o = 3 * (KT // 2 - 1)
            tile(0, 0, PAIR_F - 1, x_hi, x_lo, x_dve, X_DVE["O"] + last_o)

            def norm_begins(n, k):
                if (n, k) == (1, KT - 3):
                    norm_sums(1, 0)
                elif (n, k) == (2, 3):
                    norm_spread(1, 0)
                elif (n, k) == (2, KT - 1):
                    norm_sums(1, 1)

            tile(1, 0, PAIR_F - 1, x_hi, x_lo, y_dve, Y_DVE["O"] + last_o, before=norm_begins)

            def up(f, j, before=None):
                pair = f * PAIRS_PER_PART + j
                tile(0, pair, PAIR_F, x_hi, x_lo, x_act, f * UP + j * 3 + X_ACT["F"], before=before)
                tile(1, pair, PAIR_F, x_hi, x_lo, y_dve, f * (UP + DOWN) + j * 3 + Y_DVE["F"])

            def down(f):
                pe.wait_ge(f_lo, f * (3 * KT) + 3 * (KT - 1))
                pe.wait_ge(x_act, f * UP + (X_ACT["F"] + UP))
                pe.sem_inc(s_own[1], 1)
                with pe.Fori(0, KT // 2) as j:
                    pair = f * PAIRS_PER_PART + j
                    tile(0, pair, PAIR_F + KT, act_hi, act_lo, x_dve, f * DOWN + j * 3 + X_DVE["F"],
                         before=last_row(f_lo, f * (3 * KT) + 3 * (KT - 1)))
                    tile(1, pair, PAIR_F + KT, act_hi, act_lo, y_dve, f * (UP + DOWN) + j * 3 + (Y_DVE["F"] + UP))

            pe.wait_ge(x_dve, X_DVE["F"])
            up(0, 0, normed(1))
            with pe.Fori(0, KT - 1) as j:
                up(0, j + 1)
            down(0)
            with pe.Fori(0, FFN_PARTS - 1) as i:
                f = i + 1
                pe.wait_ge(x_dve, f * DOWN + X_DVE["F"])
                pe.sem_inc(s_own[1], 1)
                with pe.Fori(0, KT) as j:
                    up(f, j)
                down(f)

        @block.scalar
        def _(act):
            A = nc.scalar.activation

            def wait(sem_, value):
                act.wait_ge(sem_, value)
                act.sem_inc(s_own[2], 1)

            def norm_root(which, n):
                act.wait_ge(n_ps, 3 * which + n + 1)
                A(nst[:, 0, 6 * n:6 * n + 6], bank[n][:, 0:6], ACT.Sqrt, bias=epsc[:, 0:1], scale=1.0 / DM).then_inc(n_rt, 1)

            def norm_hi(which, n, i):
                c0, cn = CHUNKS[n]
                for h in range(4):
                    wait(n_f32, i * 4 + (KT * (3 * which + n) + h + 1))
                    A(row(x_hi, i * 4 + h, c0, cn), ntmp[h][:, 0:cn], ACT.Copy).then_inc(n_hi, 1)

            def squares(n):
                c0, cn = CHUNKS[n]
                for h in range(2):
                    kk = slice(h * KT // 2, (h + 1) * KT // 2)
                    act.wait_ge(s_x[2 * n + h], 16)
                    A(merged[:, kk, c0:c0 + cn], resid[:, kk, c0:c0 + cn], ACT.Square).then_inc(n_sq, 1)

            act.sem_inc(r_tanh, START)
            act.wait_ge(s_eps, 1)
            A(warm[:, :], epsc[:, 0:1], ACT.Sqrt)
            squares(0)
            norm_root(0, 0)
            squares(1)
            for n in range(3):
                for i in range(2):
                    norm_hi(0, n, i)
                    if n < 2 and i == 0:
                        norm_root(0, n + 1)
                    if n == 0 and i == 0:
                        squares(2)
            act.wait_ge(s_vec, 32)
            A(halfb[:, 0:2 * KT], V("bg_lru", 0, 2 * KT), ACT.Copy, scale=0.5)
            A(halfb[:, 2 * KT:4 * KT], V("b_a", 0, 2 * KT), ACT.Copy, scale=0.5)
            A(lam_t[:, 0, :], V("lam", 0, KT), ACT.Abs).then_inc(act_c, 1)
            act.wait_ge(act_c, 1)
            A(lam_t[:, 1, :], lam_t[:, 0, :], ACT.Exp, scale=-1.0).then_inc(s_exp_lam, 1)

            for a in range(2):
                p0, B0 = ATT_PAIRS * a, NB * a
                if a:
                    act.wait_ge(s_out, 16 * 4)

                def out(r_, n):
                    c0, cn = CHUNKS[n]
                    s, done, free = (0, x_done, x_act) if r_ % 2 == 0 else (1, y_done, y_act)
                    act.wait_ge(done, 3 * (p0 + r_ // 2) + n + 1)
                    A(qT[:, r_ - 1, c0:c0 + cn] if r_ else kN[:, c0:c0 + cn], bank[3 * s + n][:, 0:cn], ACT.Copy)
                    A(sq[:, r_ % 2, c0:c0 + cn], bank[3 * s + n][:, 0:cn], ACT.Square).then_inc(free, 1)

                def v_out(n):
                    c0, cn = CHUNKS[n]
                    act.wait_ge(y_done, 3 * (p0 + 2) + n + 1)
                    A(vT[:, c0:c0 + cn], bank[3 + n][:, 0:cn], ACT.Copy).then_inc(y_act, 1)

                for r_ in range(5):
                    for n in range(3):
                        out(r_, n)
                    for n, (c0, cn) in enumerate(CHUNKS):
                        m = 3 * (5 * a + r_) + n
                        act.wait_ge(h_ps, m + 1)
                        if m > 2:
                            act.wait_ge(h_rdy, m - 2)
                        A(irms[:, c0:c0 + cn], bank[6 + m % 2][:, 0:cn], ACT.Sqrt, bias=epsc[:, (r_ > 0):(r_ > 0) + 1],
                          scale=1.0 if r_ else 1.0 / HD).then_inc(h_rt, 1)
                v_out(0)

                def exps(b, s, keys, nu):
                    act.wait_ge(a_stat, b + 1)
                    sm = small[s]
                    A(sm[:, 3, 0:nu], sm[:, 2, 0:nu], ACT.Exp)
                    for v in range(nu):
                        b_, c_ = (2 * s + v // 2, v % 2 * 192) if nu == 4 else (v, 0)
                        last = A(pr[s][:, v, 0:keys], bank[b_][:, c_:c_ + keys], ACT.Exp,
                                 bias=sm[:, 1, v:v + 1], accum_out=sm[:, 4, v:v + 1])
                    last.then_inc(a_exp, 1)

                def evac(b, keys, nu):
                    act.wait_ge(a_T, b + 1)
                    act.wait_ge(a_O, b)
                    kn = min(keys, P)
                    if keys > P:
                        A(vt[1][0:keys - P, :], bank[6][0:keys - P, P:2 * P], ACT.Copy)
                    A(vt[0][0:kn, :], bank[6][0:kn, 0:P], ACT.Copy)
                    A(pt[0][0:kn, 0:nu * P], bank[4][0:kn, 0:nu * P], ACT.Copy).then_inc(a_ev, 1)

                def hi(b, c0, cn):
                    wait(a_O, b + 1)
                    wait(a_lo, b)
                    A(of[:, 0:4 * cn], bank[7][:, 0:4 * cn], ACT.Copy)
                    A(c_hi[:, 4 * a:4 * a + 4, cols(c0, cn)], bank[7][:, 0:4 * cn].rearrange("p (a b) -> p a b", b=cn),
                      ACT.Copy).then_inc(a_hi, 1)

                v_out(1)
                exps(B0, 0, CHUNK, 4)
                exps(B0 + 1, 1, 2 * CHUNK, 4)
                v_out(2)
                act.wait_ge(h_rdy, 15 * a + 3)
                act.wait_ge(y_act, 3 * (p0 + 3))
                act.dma_start(o_kp[a], kN[:, SEQ - WIN:SEQ]).then_inc(s_out, 16)
                act.dma_start(o_ks[a], kN[:, SMP:T]).then_inc(s_out, 16)
                act.dma_start(o_vp[a], vT[:, SEQ - WIN:SEQ]).then_inc(s_out, 16)
                act.dma_start(o_vs[a], vT[:, SMP:T]).then_inc(s_out, 16)
                evac(B0, CHUNK, 4)
                exps(B0 + 2, 0, 3 * CHUNK, 4)
                evac(B0 + 1, 2 * CHUNK, 4)
                hi(B0, 0, CHUNK)
                exps(B0 + 3, 1, 3 * CHUNK, 4)
                with act.Fori(0, GEN // 2) as i:
                    for s in range(2):
                        evac(i * 2 + (B0 + 2 + s), 3 * CHUNK, 4)
                        hi(i * 2 + (B0 + 1 + s), i * (2 * CHUNK) + (1 + s) * CHUNK, CHUNK)
                        exps(i * 2 + (B0 + 4 + s), s, 3 * CHUNK, 4)
                evac(B0 + NC - 2, 3 * CHUNK, 4)
                hi(B0 + NC - 3, SEQ - 3 * CHUNK, CHUNK)
                exps(B0 + NC, 0, WIN + DSEQ, 2)
                evac(B0 + NC - 1, 3 * CHUNK, 4)
                hi(B0 + NC - 2, SEQ - 2 * CHUNK, CHUNK)
                evac(B0 + NC, WIN + DSEQ, 2)
                hi(B0 + NC - 1, SEQ - CHUNK, CHUNK)
                hi(B0 + NC, SMP, DSEQ)

            def first_gate(p0, half0):
                for n, (c0, cn) in enumerate(CHUNKS):
                    act.wait_ge(x_done, 3 * p0 + n + 1)
                    A(GG[n][:, 0:cn], bank[n][:, 0:cn], ACT.Tanh, bias=halfb[:, half0:half0 + 1], scale=0.5).then_inc(x_act, 1)

            def gates(p0, half0, stage):
                with act.Fori(0, KT - 1) as i:
                    for n, (c0, cn) in enumerate(CHUNKS):
                        wait(y_done, i * 3 + (3 * p0 + n + 1))
                        wait(x_dve, i * 3 + (X_DVE[stage] + n + 1))
                        A(GG[n][:, 0:cn], bank[3 + n][:, 0:cn], ACT.Tanh, bias=halfb[:, bass.ds(i + (half0 + 1), 1)],
                          scale=0.5).then_inc(y_act, 1)

            first_gate(PAIR_G1, KT)
            gates(PAIR_G1, KT, "G1")

            def load_wab(j):
                src = wab[j] if isinstance(j, int) else wab[bass.ds(j, 1)].rearrange("a p m n -> (a p) m n")
                act.dma_start(wabs[:, :, :], src).then_inc(s_wab, 16)

            def lru_u(j):
                for n, (c0, cn) in enumerate(CHUNKS):
                    wait(x_done, j * 3 + (3 * PAIR_R + n + 1))
                    A(U[:, LRU_HIST + c0:LRU_HIST + c0 + cn], bank[n][:, 0:cn], ACT.Copy).then_inc(x_act, 1)

            def lru_x0(j):
                wait(r_fix, j + 1)
                for n, (c0, cn) in enumerate(CHUNKS):
                    A(XC[n][:, 0:cn], U[:, LRU_HIST + c0:LRU_HIST + c0 + cn], ACT.Identity,
                      bias=VD("conv_b", j), scale=VD("conv_w", j * 4 + 3)).then_inc(r_x0, 1)

            def lru_decay(j):
                for n, (c0, cn) in enumerate(CHUNKS):
                    ck = slice(c0, c0 + cn)
                    wait(r_ps, j * 3 + (n + 1))
                    A(FA[:, ck], bank[6][:, 0:cn], ACT.Tanh, bias=halfb[:, cols(j + 2 * KT, 1)], scale=0.5)
                    A(FI[:, ck], bank[7][:, 0:cn], ACT.Tanh, bias=halfb[:, cols(j + 3 * KT, 1)], scale=0.5).then_inc(r_tanh, 1)
                    wait(r_tanh, j * 3 + (START + n + 1))
                    A(row(resid, j, c0, cn), FA[:, ck], ACT.Tanh, bias=lamc[:, 0, cols(j, 1)], scale=lamc[:, 0, cols(j, 1)])
                    A(FA[:, ck], FA[:, ck], ACT.Exp, bias=lamc[:, 1, cols(j, 1)], scale=lamc[:, 1, cols(j, 1)]).then_inc(act_c, 1)
                    wait(act_c, j * 3 + (n + 2))
                    A(FS[:, ck], FA[:, ck], ACT.Square).then_inc(r_sqa, 1)

            def lru_root(j):
                act.wait_ge(r_om, j * 3 + 3)
                A(FS[:, :], FS[:, :], ACT.Sqrt, scale=0.25).then_inc(r_root, 1)

            def lru_gelu(j):
                for n, (c0, cn) in enumerate(CHUNKS):
                    wait(y_done, j * 3 + (3 * PAIR_R + n + 1))
                    A(row(sqsum, j, c0, cn), bank[3 + n][:, 0:cn], ACT.Gelu_apprx_tanh).then_inc(y_act, 1)

            def lru_hi(j):
                for n, (c0, cn) in enumerate(CHUNKS):
                    wait(r_z, j * 3 + (n + 1))
                    A(row(c_hi, j, c0, cn), FA[:, c0:c0 + cn], ACT.Copy).then_inc(r_hi, 1)

            load_wab(0)
            act.wait_ge(y_dve, Y_DVE["G0"])
            act.wait_ge(s_lamc, 1)
            lru_u(0)
            lru_x0(0)
            lru_gelu(0)
            with act.Fori(0, KT - 1) as j:
                wait(r_xc, j * 3 + 3)
                lru_u(j + 1)
                wait(r_lo, j * 3 + START)
                lru_decay(j)
                load_wab(j + 1)
                lru_root(j)
                lru_x0(j + 1)
                lru_gelu(j + 1)
                lru_hi(j)
            act.wait_ge(r_xc, 3 * KT)
            first_gate(PAIR_G0, 0)
            act.wait_ge(r_lo, START + 3 * (KT - 1))
            lru_decay(KT - 1)
            lru_root(KT - 1)
            lru_hi(KT - 1)

            gates(PAIR_G0, 0, "G0")

            with act.Fori(0, KT - 1) as k:
                wait(m_mrg, k * 3 + 3)
                A(row(x_hi, k, 0, T), row(merged, k, 0, T), ACT.Copy, scale=0.5).then_inc(m_hi, 1)
            for n, (c0, cn) in enumerate(CHUNKS):
                act.wait_ge(m_mrg, 3 * (KT - 1) + n + 1)
                A(row(x_hi, KT - 1, c0, cn), row(merged, KT - 1, c0, cn), ACT.Copy, scale=0.5).then_inc(m_hi, 1)
            act.wait_ge(y_done, 3 * PAIR_O)
            for h in range(2):
                kk = slice(h * KT // 2, (h + 1) * KT // 2)
                act.dma_start(sqsum[:, kk, :], xT[kk].rearrange("k p n -> p k n")).then_inc(s_xres[h], 16)
            act.wait_ge(m_lo, KT + 2)

            def h_squares(i, s, n):
                (c0, cn), free, freed = CHUNKS[n], (x_dve, y_dve)[s], (X_DVE, Y_DVE)[s]["O"]
                wait(free, i * 3 + (freed + n + 1))
                A(row(merged, i * 2 + s, c0, cn), row(resid, i * 2 + s, c0, cn), ACT.Square).then_inc(n_sq, 1)

            with act.Fori(0, KT // 2 - 1) as i:
                for s in range(2):
                    for n in range(3):
                        h_squares(i, s, n)
            last = KT // 2 - 1
            for n in range(3):
                h_squares(last, 0, n)
            h_squares(last, 1, 0)
            norm_root(1, 0)
            h_squares(last, 1, 1)
            norm_hi(1, 0, 0)
            norm_root(1, 1)
            h_squares(last, 1, 2)
            norm_hi(1, 0, 1)
            norm_hi(1, 1, 0)
            norm_root(1, 2)
            norm_hi(1, 1, 1)
            for i in range(2):
                norm_hi(1, 2, i)

            with act.Fori(0, FFN_PARTS) as f:
                with act.Fori(0, KT) as j:
                    p3 = f * (3 * PAIRS_PER_PART) + j * 3
                    used = f * (UP + DOWN) + j * 3 + Y_DVE["F"]
                    ft = f * KT + j
                    for n, (c0, cn) in enumerate(CHUNKS):
                        act.wait_ge(x_done, p3 + (3 * PAIR_F + n + 1))
                        A(GB[:, FFN_HIST + c0:FFN_HIST + c0 + cn], bank[n][:, 0:cn], ACT.Copy).then_inc(x_act, 1)
                    wait(f_fix, ft + 1)
                    for n, (c0, cn) in enumerate(CHUNKS):
                        wait(y_dve, used + (n - 2))
                        A(GC[n][:, 0:cn], GB[:, FFN_HIST + c0:FFN_HIST + c0 + cn], ACT.Identity,
                          bias=VD("fconv_b", ft), scale=VD("fconv_w", ft * 3 + 2)).then_inc(f_c0, 1)
                    for n, (c0, cn) in enumerate(CHUNKS):
                        wait(f_conv, ft * 3 + (n + 1))
                        A(GC[n][:, 0:cn], GC[n][:, 0:cn], ACT.Gelu_apprx_tanh).then_inc(f_gelu, 1)
                    for n, (c0, cn) in enumerate(CHUNKS):
                        wait(y_dve, used + (n + 1))
                        A(row(act_hi, j, c0, cn), GV[n][:, 0:cn], ACT.Copy).then_inc(f_hi, 1)

        @block.vector
        def _(dve):
            D = nc.vector
            ch = Count(dve_c)

            def link(ins):
                ch.inc(ins)
                dve.wait_ge(dve_c, ch.value())

            def norm_scale(which, n):
                root, y, m, t = (nst[:, i, 6 * n:6 * n + 6] for i in range(4))
                dve.wait_ge(n_rt, 3 * which + n + 1)
                link(D.reciprocal(y, root))
                D.tensor_scalar(m, bank[n][:, 0:6], -0.5 / DM, -0.5 * EPS, ALU.mult, ALU.add)
                link(D.tensor_tensor(t, y, y, ALU.mult))
                link(D.tensor_tensor(t, t, m, ALU.mult))
                link(D.scalar_tensor_tensor(y, t, 1.5, y, ALU.add, ALU.mult))
                for b in range(3):
                    last = D.tensor_scalar(dg[:, 3 * n + b, :], ident, y[:, 2 * b:2 * b + 1], None, ALU.mult)
                last.then_inc(n_dg, 1)

            def norm_rows(which, n, i):
                (c0, cn), g = CHUNKS[n], "g_ffn" if which else "g_mix"
                groups = 2 * (3 * which + n)
                dve.wait_ge(n_bc, 3 * which + n + 1)
                for h in range(4):
                    if h > 0:
                        dve.wait_ge(n_lop, i * 3 + (START + 3 * groups + h - 3))
                    else:
                        dve.wait_ge(n_lo, i + (START + groups))
                    D.scalar_tensor_tensor(ntmp[h][:, 0:cn], row(resid, i * 4 + h, c0, cn), VD(g, i * 4 + h),
                                           bank[6 + n % 2][:, 0:cn], ALU.mult, ALU.mult).then_inc(n_f32, 1)
                dve.wait_ge(n_hi, i * 4 + (4 * groups + 1))
                D.tensor_tensor(row(x_lo, i * 4, c0, cn), ntmp[0][:, 0:cn],
                                row(x_hi, i * 4, c0, cn).bitcast(F32), ALU.subtract).then_inc(n_lo, 1)

            dve.sem_inc(x_dve, 3)
            dve.sem_inc(y_dve, 3)
            dve.sem_inc(n_lo, START)
            dve.sem_inc(n_acc, START)
            dve.sem_inc(a_evv, START)
            dve.sem_inc(r_lo, START)
            D.memset(epsc[:, 0:1], EPS)
            D.memset(epsc[:, 1:2], HD * EPS).then_inc(s_eps, 1)
            dve.wait_ge(s_vec, 32)

            def x_sums(n):
                c0, cn = CHUNKS[n]
                dve.wait_ge(n_sq, 2 * n + 2)
                for rows in (4, 2):
                    link(D.tensor_tensor(merged[:, 0:rows, c0:c0 + cn], merged[:, 0:rows, c0:c0 + cn],
                                         merged[:, rows:2 * rows, c0:c0 + cn], ALU.add))
                D.tensor_tensor(nacc[:, c0:c0 + cn], merged[:, 0, c0:c0 + cn], merged[:, 1, c0:c0 + cn], ALU.add).then_inc(n_acc, 1)

            x_sums(0)
            norm_scale(0, 0)
            for n in range(3):
                if n < 2:
                    x_sums(n + 1)
                norm_rows(0, n, 0)
                if n < 2:
                    norm_scale(0, n + 1)
                norm_rows(0, n, 1)
            dve.wait_ge(s_exp_lam, 1)
            e, s_, s2, ac = (lam_t[:, i, :] for i in (1, 2, 3, 4))
            link(D.tensor_scalar(s2, e, 2.0, None, ALU.add))
            link(D.reciprocal(s2, s2))
            link(D.tensor_tensor(s_, e, s2, ALU.mult))
            link(D.tensor_tensor(s2, s_, s_, ALU.mult))
            link(D.memset(ac, 1.0 / 19))
            for m in range(17, 0, -2):
                link(D.tensor_tensor(ac, ac, s2, ALU.mult))
                link(D.tensor_scalar(ac, ac, 1.0 / m, None, ALU.add))
            link(D.tensor_tensor(ac, ac, s_, ALU.mult))
            link(D.tensor_scalar(s2, V("lam", 0, KT), -1.0, 0.0, ALU.mult, ALU.max))
            link(D.scalar_tensor_tensor(ac, ac, 2.0, s2, ALU.mult, ALU.add))
            D.tensor_scalar(lamc[:, 0, :], ac, 4.0, None, ALU.mult)
            D.tensor_scalar(lamc[:, 1, :], ac, -4.0, None, ALU.mult).then_inc(s_lamc, 1)
            link(D.tensor_scalar(negsink[:, :], V("sink_p", 0, 12), -1.0, None, ALU.mult))

            for a in range(2):
                p0, B0 = ATT_PAIRS * a, NB * a
                for r_ in range(5):
                    for n, (c0, cn) in enumerate(CHUNKS):
                        ck = slice(c0, c0 + cn)
                        dve.wait_ge(h_rt, 3 * (5 * a + r_) + n + 1)
                        link(D.reciprocal(irms[:, ck], irms[:, ck]))
                        if r_ == 0:
                            link(D.scalar_tensor_tensor(kN[:, ck], kN[:, ck], V("g_k"), irms[:, ck], ALU.mult, ALU.mult))
                            last = D.tensor_scalar(kG[:, ck], kN[:, ck], V("g_q"), None, ALU.mult)
                        else:
                            last = D.tensor_tensor(qT[:, r_ - 1, ck], qT[:, r_ - 1, ck], irms[:, ck], ALU.mult)
                        last.then_inc(h_rdy, 1)
                dve.wait_ge(h_rdy, 15 * (a + 1))
                for t in (c_hi, d_lo):
                    D.memset(t[:, 4 * a:4 * a + 4, SEQ:SMP].bitcast(F32), 0.0)

                def stats(b, s, keys, nu, sink0):
                    sm = small[s]
                    dve.wait_ge(a_S, b + 1)
                    if nu == 4:
                        src = bankpair[s][:, :, 0:384].rearrange("p b (v k) -> p b v k", v=2)[:, :, :, 0:keys]
                        dst = sm[:, 0, 0:4].rearrange("p (b v) -> p b v", v=2)
                    else:
                        src = bankpair[0][:, :, 0:keys]
                        dst = sm[:, 0, 0:2]
                    link(D.tensor_reduce(dst, src, AXX, ALU.max))
                    link(D.scalar_tensor_tensor(sm[:, 1, 0:nu], sm[:, 0, 0:nu], -1.0, negsink[:, sink0:sink0 + nu], ALU.mult, ALU.min))
                    D.tensor_tensor(sm[:, 2, 0:nu], sm[:, 1, 0:nu], negsink[:, sink0:sink0 + nu], ALU.subtract).then_inc(a_stat, 1)

                def normalise(b, s, keys, nu):
                    sm = small[s]
                    dve.wait_ge(a_exp, b + 1)
                    link(D.tensor_tensor(sm[:, 5, 0:nu], sm[:, 4, 0:nu], sm[:, 3, 0:nu], ALU.add))
                    link(D.reciprocal(sm[:, 5, 0:nu], sm[:, 5, 0:nu]))
                    for v in range(nu):
                        last = D.tensor_scalar(pr[s][:, v, 0:keys], pr[s][:, v, 0:keys], sm[:, 5, v:v + 1], None, ALU.mult)
                    last.then_inc(a_nrm, 1)

                def evac(b, keys, nu):
                    dve.wait_ge(a_T, b + 1)
                    dve.wait_ge(a_O, b)
                    D.tensor_copy(pt[1][0:keys - P, 0:nu * P], bank[5][0:keys - P, 0:nu * P]).then_inc(a_evv, 1)

                stats(B0, 0, CHUNK, 4, 4 * a)
                normalise(B0, 0, CHUNK, 4)
                stats(B0 + 1, 1, 2 * CHUNK, 4, 4 * a)
                for l in range(2):
                    stats(B0 + 2 + l, l, 3 * CHUNK, 4, 4 * a)
                    normalise(B0 + l + 1, 1 - l, (l + 2) * CHUNK, 4)
                with dve.Fori(0, GEN // 2) as i:
                    ch.enter(i, 2 * 4)
                    for s in range(2):
                        stats(i * 2 + (B0 + 4 + s), s, 3 * CHUNK, 4, 4 * a)
                        normalise(i * 2 + (B0 + 3 + s), 1 - s, 3 * CHUNK, 4)
                        evac(i * 2 + (B0 + 2 + s), 3 * CHUNK, 4)
                    ch.leave(GEN // 2)
                stats(B0 + NC, 0, WIN + DSEQ, 2, 8 + 2 * a)
                normalise(B0 + NC - 1, 1, 3 * CHUNK, 4)
                evac(B0 + NC - 2, 3 * CHUNK, 4)
                evac(B0 + NC - 1, 3 * CHUNK, 4)
                normalise(B0 + NC, 0, WIN + DSEQ, 2)
                evac(B0 + NC, WIN + DSEQ, 2)

            dve.wait_ge(s_out, 16 * 8)
            def joins(p0, stage, join):
                ya = Y_ACT[stage]
                dve.wait_ge(x_act, X_ACT[stage] + 3)
                with dve.Fori(0, KT - 1) as j:
                    for n in range(3):
                        dve.wait_ge(y_act, j * 3 + (ya + n - 2))
                        dve.wait_ge(x_done, j * 3 + (3 * p0 + 3 + n + 1))
                        join(j, n, XB, x_dve)

            def last_join(p0, stage, join):
                for n in range(3):
                    dve.wait_ge(y_act, Y_ACT[stage] + 3 * (KT - 2) + n + 1)
                    dve.wait_ge(y_done, 3 * (p0 + KT - 1) + n + 1)
                    join(KT - 1, n, YB, y_dve)

            def join_attention(j, n, banks, freed):
                c0, cn = CHUNKS[n]
                D.scalar_tensor_tensor(row(merged, j, c0, cn), GG[n][:, 0:cn], 1.0, banks[n][:, 0:cn],
                                       ALU.add, ALU.mult).then_inc(freed, 1)

            joins(PAIR_G1, "G1", join_attention)
            last_join(PAIR_G1, "G1", join_attention)

            dve.wait_ge(y_dve, Y_DVE["G0"])
            link(D.memset(U[:, 0:LRU_HIST], 0.0))

            def lru_history(j):
                dve.wait_ge(x_act, j * 3 + (X_ACT["R"] + 3))
                for r, c0 in enumerate((SEQ, T)):
                    D.tensor_copy(st_lconv[:, cols(j, 1), r, :].rearrange("p a n -> p (a n)"), U[:, c0:c0 + LRU_HIST])
                D.tensor_copy(U[:, SMP:SMP + LRU_HIST], VD("conv0", j * LRU_HIST, LRU_HIST)).then_inc(r_fix, 1)

            def lru_conv(j, n):
                c0, cn = CHUNKS[n]
                dve.wait_ge(r_x0, j * 3 + (n + 1))
                for tap in (2, 1, 0):
                    ins = D.scalar_tensor_tensor(XC[n][:, 0:cn], U[:, tap + c0:tap + c0 + cn], VD("conv_w", j * 4 + tap),
                                                 XC[n][:, 0:cn], ALU.mult, ALU.add)
                    if tap:
                        link(ins)
                ins.then_inc(r_xc, 1)

            def lru_inputs(j):
                for n, (c0, cn) in enumerate(CHUNKS):
                    ck = slice(c0, c0 + cn)
                    dve.wait_ge(r_tanh, j * 3 + (START + n + 1))
                    D.scalar_tensor_tensor(FI[:, ck], FI[:, ck], 1.0, XC[n][:, 0:cn], ALU.add, ALU.mult)
                    dve.wait_ge(r_sqa, j * 3 + (n + 1))
                    D.scalar_tensor_tensor(FS[:, ck], FS[:, ck], 1.0, row(resid, j, c0, cn), ALU.add, ALU.mult).then_inc(r_om, 1)

            def lru_scan(j):
                dve.wait_ge(r_root, j + 1)
                link(D.tensor_tensor(FI[:, :], FI[:, :], FS[:, :], ALU.mult))
                D.tensor_tensor_scan(FI[:, 0:SEQ], FA[:, 0:SEQ], FI[:, 0:SEQ], 0.0, ALU.mult, ALU.add)
                D.memset(FI[:, SEQ:SMP], 0.0)
                D.tensor_tensor_scan(FI[:, SMP:T], FA[:, SMP:T], FI[:, SMP:T], VD("h0", j), ALU.mult, ALU.add).then_inc(r_h, 1)
                dve.wait_ge(r_h, j + 1)
                for r, c0 in enumerate((SEQ - 1, T - 1)):
                    D.tensor_copy(st_h[:, cols(j, 1), r:r + 1].rearrange("p a n -> p (a n)"), FI[:, c0:c0 + 1])
                for n, (c0, cn) in enumerate(CHUNKS):
                    dve.wait_ge(y_act, j * 3 + (Y_ACT["R"] + n + 1))
                    D.tensor_tensor(FA[:, c0:c0 + cn], FI[:, c0:c0 + cn], row(sqsum, j, c0, cn), ALU.mult).then_inc(r_z, 1)

            def lru_lo(j):
                for n, (c0, cn) in enumerate(CHUNKS):
                    dve.wait_ge(r_hi, j * 3 + (n + 1))
                    D.tensor_tensor(row(d_lo, j, c0, cn), FA[:, c0:c0 + cn], row(c_hi, j, c0, cn).bitcast(F32),
                                    ALU.subtract).then_inc(r_lo, 1)

            lru_history(0)
            for n in range(3):
                lru_conv(0, n)
            with dve.Fori(0, KT - 1) as j:
                ch.enter(j, 2 * 3 + 1)
                lru_history(j + 1)
                lru_inputs(j)
                lru_scan(j)
                lru_conv(j + 1, 0)
                lru_lo(j)
                lru_conv(j + 1, 1)
                lru_conv(j + 1, 2)
                ch.leave(KT - 1)
            lru_inputs(KT - 1)
            lru_scan(KT - 1)
            lru_lo(KT - 1)

            def join_lru(j, n, banks, freed):
                c0, cn = CHUNKS[n]
                D.scalar_tensor_tensor(GV[n][:, 0:cn], GG[n][:, 0:cn], 1.0, banks[n][:, 0:cn], ALU.add, ALU.mult).then_inc(freed, 1)
                dve.wait_ge(freed, Y_DVE["G0"] + n + 1 if freed is y_dve else j * 3 + (X_DVE["G0"] + n + 1))
                D.tensor_tensor(row(merged, j, c0, cn), row(merged, j, c0, cn), GV[n][:, 0:cn], ALU.add).then_inc(m_mrg, 1)

            joins(PAIR_G0, "G0", join_lru)
            with dve.Fori(0, KT - 1) as k:
                dve.wait_ge(m_hi, k + 1)
                D.scalar_tensor_tensor(row(x_lo, k, 0, T), row(merged, k, 0, T), 0.5, row(x_hi, k, 0, T).bitcast(F32),
                                       ALU.mult, ALU.subtract).then_inc(m_lo, 1)
            last_join(PAIR_G0, "G0", join_lru)
            for n, (c0, cn) in enumerate(CHUNKS):
                dve.wait_ge(m_hi, KT + n)
                D.scalar_tensor_tensor(row(x_lo, KT - 1, c0, cn), row(merged, KT - 1, c0, cn), 0.5,
                                       row(x_hi, KT - 1, c0, cn).bitcast(F32), ALU.mult, ALU.subtract).then_inc(m_lo, 1)

            for h in range(2):
                dve.wait_ge(s_xres[h], 16)
            link(D.memset(nacc[:, :], 0.0))

            def h_out(i, s, n):
                (c0, cn), done, free = CHUNKS[n], (x_done, y_done)[s], (x_dve, y_dve)[s]
                dve.wait_ge(done, i * 3 + (3 * PAIR_O + n + 1))
                D.tensor_tensor(row(resid, i * 2 + s, c0, cn), bank[3 * s + n][:, 0:cn], row(sqsum, i * 2 + s, c0, cn),
                                ALU.add).then_inc(free, 1)
                dve.wait_ge(n_sq, i * 6 + (6 + 3 * s + n + 1))
                dve.wait_ge(n_acc, i * 6 + (START + 3 + 3 * s + n - 2))
                D.tensor_tensor(nacc[:, c0:c0 + cn], nacc[:, c0:c0 + cn], row(merged, i * 2 + s, c0, cn), ALU.add).then_inc(n_acc, 1)

            with dve.Fori(0, KT // 2 - 1) as i:
                for s in range(2):
                    for n in range(3):
                        h_out(i, s, n)
            last_i = KT // 2 - 1
            for n in range(3):
                h_out(last_i, 0, n)
            h_out(last_i, 1, 0)
            norm_scale(1, 0)
            h_out(last_i, 1, 1)
            norm_rows(1, 0, 0)
            norm_scale(1, 1)
            h_out(last_i, 1, 2)
            norm_rows(1, 0, 1)
            norm_rows(1, 1, 0)
            norm_scale(1, 2)
            norm_rows(1, 1, 1)
            for i in range(2):
                norm_rows(1, 2, i)

            link(D.memset(GB[:, 0:FFN_HIST], 0.0))
            with dve.Fori(0, FFN_PARTS) as f:
                ch.enter(f, 3 * KT)
                with dve.Fori(0, KT) as j:
                    ch.enter(j, 3)
                    p3 = f * (3 * PAIRS_PER_PART) + j * 3
                    ft = f * KT + j
                    dve.wait_ge(x_act, f * UP + j * 3 + (X_ACT["F"] + 3))
                    for r, c0 in enumerate((SEQ, T)):
                        D.tensor_copy(st_fconv[:, bass.ds(ft, 1), r, :].rearrange("p a n -> p (a n)"), GB[:, c0:c0 + FFN_HIST])
                    D.tensor_copy(GB[:, SMP:SMP + FFN_HIST], VD("fconv0", ft * FFN_HIST, FFN_HIST)).then_inc(f_fix, 1)
                    for n, (c0, cn) in enumerate(CHUNKS):
                        dve.wait_ge(f_c0, ft * 3 + (n + 1))
                        for tap in (1, 0):
                            ins = D.scalar_tensor_tensor(GC[n][:, 0:cn], GB[:, tap + c0:tap + c0 + cn], VD("fconv_w", ft * 3 + tap),
                                                         GC[n][:, 0:cn], ALU.mult, ALU.add)
                            if tap:
                                link(ins)
                        ins.then_inc(f_conv, 1)
                    for n, (c0, cn) in enumerate(CHUNKS):
                        dve.wait_ge(f_gelu, ft * 3 + (n + 1))
                        dve.wait_ge(y_done, p3 + (3 * PAIR_F + n + 1))
                        D.tensor_tensor(GV[n][:, 0:cn], GC[n][:, 0:cn], bank[3 + n][:, 0:cn], ALU.mult).then_inc(y_dve, 1)
                    for n, (c0, cn) in enumerate(CHUNKS):
                        dve.wait_ge(f_hi, ft * 3 + (n + 1))
                        D.tensor_tensor(row(act_lo, j, c0, cn), GV[n][:, 0:cn], row(act_hi, j, c0, cn).bitcast(F32),
                                        ALU.subtract).then_inc(f_lo, 1)
                    ch.leave(KT)
                ch.leave(FFN_PARTS)
                with dve.Fori(0, KT // 2) as i:
                    for s, (done, free) in enumerate(((x_done, x_dve), (y_done, y_dve))):
                        for n, (c0, cn) in enumerate(CHUNKS):
                            dve.wait_ge(done, f * (3 * PAIRS_PER_PART) + i * 3 + (3 * (PAIR_F + KT) + n + 1))
                            D.tensor_tensor(row(resid, i * 2 + s, c0, cn), row(resid, i * 2 + s, c0, cn), bank[3 * s + n][:, 0:cn],
                                            ALU.add).then_inc(free, 1)


def _tiles(w):
    k, n = w.shape
    return w.reshape(k // P, P, n // P, P).transpose(2, 1, 0, 3).reshape(n // P, P, k)


def _cols(v):
    return v.reshape(-1, P).T


def kernel(**inputs):
    import concourse.bacc as bacc
    from concourse.bass_utils import run_bass_kernel_spmd

    x = {k: np.asarray(v) for k, v in inputs.items()}
    f32 = np.float32
    cat, ct = np.concatenate, np.ascontiguousarray

    order = [4 * (2 * a + e) + s for a in range(2) for s in range(4) for e in range(2)]
    rows = cat([np.arange(HD) + HD * h for h in order])
    w_in = x["w_in"][0]
    u, y, q, k, v, g0, g1 = np.split(w_in, np.cumsum([DM, DM, DM, NKV * HD, NKV * HD, DM]), axis=1)
    q = _tiles(q[:, rows])
    k, v, u, y, g0, g1 = (_tiles(w) for w in (k, v, u, y, g0, g1))
    br_l, br_a = _tiles(x["w_br_lru"][0]), _tiles(x["w_br_attn"][0][rows])
    out = _tiles(x["w_out"][0])
    gate, up = (_tiles(w) for w in np.split(x["w_up"][0], 2, axis=1))
    down = [_tiles(w) for w in np.split(x["w_down"][0], FFN_PARTS, axis=0)]
    slots = []
    for a in range(2):
        slots += [k[a], *q[4 * a:4 * a + 4], v[a]]

    def gated(g, b):
        return [g[0], g[1]] + [w for j in range(KT - 2) for w in (b[j], g[j + 2])] + [b[KT - 2], b[KT - 1]]

    slots += gated(g1, br_a)
    for j in range(KT):
        slots += [u[j], y[j]]
    slots += gated(g0, br_l)
    slots += list(out)
    for f in range(FFN_PARTS):
        for j in range(KT):
            slots += [gate[KT * f + j], up[KT * f + j]]
        slots += list(down[f])
    W = np.stack(slots)
    assert W.shape[0] == NSLOT

    xT = np.zeros((DM, T), f32)
    xT[:, :SEQ], xT[:, SMP:] = x["x_prompt"][0].T, x["x_sample"][0].T
    wab = np.zeros((KT, P, 2, P), f32)
    for m, name in enumerate(("w_lru_a", "w_lru_i")):
        for j in range(KT):
            for e in range(2):
                wab[j, HD * e:HD * e + HD, m, HD * e:HD * e + HD] = x[name][0, 2 * j + e]
    sink = x["attn_sink"][0]
    sink_p = np.stack([np.repeat([sink[4 * (2 * a + e) + 2 * uu + s] for s in range(2)], CHUNK)
                       for a in range(2) for e in range(2) for uu in range(2)], axis=1)
    sink_s = np.stack([np.repeat([sink[4 * (2 * a + e) + s] for s in range(4)], DSEQ)
                       for a in range(2) for e in range(2)], axis=1)
    bg = x["b_gate"][0]
    parts = dict(bg_lru=_cols(bg[:DM]), bg_att=_cols(bg[DM:]),
                 conv_w=x["w_lru_conv"][0].reshape(4, KT, P).transpose(2, 1, 0).reshape(P, -1), conv_b=_cols(x["b_lru_conv"][0]),
                 b_a=_cols(x["b_lru_a"][0]), b_i=_cols(x["b_lru_i"][0]), lam=_cols(x["lru_lambda"][0]),
                 g_mix=_cols(x["g_mix"][0]), g_ffn=_cols(x["g_ffn"][0]),
                 fconv_w=x["w_ffn_conv"][0].reshape(3, FT, P).transpose(2, 1, 0).reshape(P, -1), fconv_b=_cols(x["b_ffn_conv"][0]),
                 h0=_cols(x["state_lru_h"][0, 0]), g_q=np.tile(x["g_q"][0], 2)[:, None], g_k=np.tile(x["g_k"][0], 2)[:, None],
                 sink_p=sink_p, sink_s=sink_s,
                 conv0=x["state_lru_conv"][0, 0].reshape(LRU_HIST, KT, P).transpose(2, 1, 0).reshape(P, -1),
                 fconv0=x["state_ffn_conv"][0, 0].reshape(FFN_HIST, FT, P).transpose(2, 1, 0).reshape(P, -1))
    vecs = cat([parts[name] for name in VEC], axis=1)
    assert vecs.shape[1] == NVEC and all(parts[n].shape[1] == VEC[n][1] for n in VEC)
    two = np.kron(np.eye(2, dtype=f32), np.ones((HD, HD), f32))
    mats = np.stack([np.eye(P, dtype=f32), np.ones((P, P), f32), two], axis=1)
    kc, vc = (x[name][0, 0].transpose(1, 2, 0).reshape(2, P, WIN).transpose(1, 0, 2) for name in ("cache_k", "cache_v"))

    nc = bacc.Bacc("TRN2", target_bir_lowering=False, num_devices=1)
    arrays, args = {}, []
    for name, a in (("xT", xT.reshape(KT, P, T)), ("W", W), ("wab", wab), ("vecs", vecs), ("mats", mats), ("kc", kc), ("vc", vc)):
        arrays[name] = ct(a)
        args.append(nc.dram_tensor(name, list(a.shape), F32, kind="ExternalInput").ap())
    outs = dict(yT=[KT, P, T], lconv=[P, KT, 2, LRU_HIST], h=[P, KT, 2], fconv=[P, FT, 2, FFN_HIST],
                kp=[2, P, WIN], ks=[2, P, DSEQ], vp=[2, P, WIN], vs=[2, P, DSEQ])
    for name, shape in outs.items():
        args.append(nc.dram_tensor("o_" + name, shape, F32, kind="ExternalOutput").ap())
    build(nc, *args)
    r = run_bass_kernel_spmd(nc, [arrays], core_ids=[0]).results[0]
    o = {name: np.asarray(r["o_" + name]) for name in outs}
    yT = o["yT"].reshape(DM, T)

    def state(t, r_):
        return ct(t[:, :, r_, :].transpose(2, 1, 0).reshape(1, 1, t.shape[3], -1))

    def heads(t):
        return ct(t.reshape(2, 2, HD, -1).transpose(3, 0, 1, 2).reshape(1, 1, t.shape[2], NKV, HD))

    def last(r_):
        return ct(o["h"][:, :, r_].T.reshape(1, 1, DM))

    return (ct(yT[:, :SEQ].T)[None], ct(yT[:, SMP:].T)[None],
            state(o["lconv"], 0), last(0), heads(o["kp"]), heads(o["vp"]), state(o["fconv"], 0),
            state(o["lconv"], 1), last(1), heads(o["ks"]), heads(o["vs"]), state(o["fconv"], 1))
```
